# Optimizing a Trainium2 kernel written in Bass

```python
import math
import jax, jax.numpy as jnp
from jax import lax
import numpy as np
import jax
import jax.numpy as jnp

D_MODEL = 1024
BATCH = 1
SEQ = 512
DEPTH = 1

D_FF = 2816
A_WIDTH = 512
A_GROUPS = 8
A_GROUP_DIM = A_WIDTH // A_GROUPS
CHUNK = 128
B_HEADS = 8
B_QK_DIM = 64
B_V_DIM = 2 * B_QK_DIM
B_WIDTH = B_HEADS * B_V_DIM
ROPE_THETA = 500000.0
ROT_DIM = B_QK_DIM // 4
Q_BLOCK = 128
NORM_EPS = 1e-6
LN_EPS = 1e-5
COL_SIZES = (D_MODEL, D_MODEL, 2 * A_WIDTH,
             B_HEADS * 2 * B_QK_DIM, B_HEADS * 2 * B_QK_DIM, B_WIDTH)
IN_COLS = sum(COL_SIZES)
COL_SPLITS = tuple(int(c) for c in np.cumsum(COL_SIZES)[:-1])


def rms_norm(x, gain, eps=NORM_EPS):
    xf = x.astype(jnp.float32)
    y = xf * lax.rsqrt(jnp.mean(xf * xf, axis=-1, keepdims=True) + eps)
    return (y * gain.astype(jnp.float32)).astype(x.dtype)

def layer_norm(x, gain, bias, eps=LN_EPS):
    xf = x.astype(jnp.float32)
    mu = jnp.mean(xf, axis=-1, keepdims=True)
    xc = xf - mu
    y = xc * lax.rsqrt(jnp.mean(xc * xc, axis=-1, keepdims=True) + eps)
    return (y * gain.astype(jnp.float32) + bias.astype(jnp.float32)).astype(x.dtype)

def swiglu(h, w_gate, w_up, w_down):
    return (jax.nn.silu(h @ w_gate) * (h @ w_up)) @ w_down

def rope_tables(positions):
    inv = ROPE_THETA ** (-jnp.arange(0, ROT_DIM, 2, dtype=jnp.float32) / ROT_DIM)
    ang = positions.astype(jnp.float32)[..., None] * inv
    return jnp.cos(ang), jnp.sin(ang)

def apply_partial_rope(t, cos, sin):
    half = ROT_DIM // 2
    r1, r2, rest = t[..., :half], t[..., half:ROT_DIM], t[..., ROT_DIM:]
    return jnp.concatenate([r1 * cos - r2 * sin, r2 * cos + r1 * sin, rest], axis=-1)

def gmlp_chunk_mixer(z_uv, ln_g, ln_b, w_s, b_s):
    bsz, seq, _ = z_uv.shape
    z = jax.nn.gelu(z_uv, approximate=False)
    u, v = jnp.split(z, 2, axis=-1)
    v = layer_norm(v, ln_g, ln_b)
    vc = v.reshape(bsz, seq // CHUNK, CHUNK, A_GROUPS, A_GROUP_DIM)
    causal = jnp.tril(jnp.ones((CHUNK, CHUNK), dtype=bool))
    w = jnp.where(causal[None], w_s, jnp.zeros_like(w_s))
    f = jnp.einsum('gts,bcsge->bctge', w, vc) + b_s.T[:, :, None]
    return u * f.reshape(bsz, seq, A_WIDTH)

def diff_attention(q, k, v, positions, q_gain, k_gain, lq1, lk1, lq2, lk2, subln_g, lam_init):
    bsz, seq = q.shape[0], q.shape[1]
    out_dtype = v.dtype
    cos, sin = rope_tables(positions)
    cos, sin = cos[:, :, None, None, :], sin[:, :, None, None, :]
    qf = apply_partial_rope(rms_norm(q.astype(jnp.float32), q_gain), cos, sin)
    kf = apply_partial_rope(rms_norm(k.astype(jnp.float32), k_gain), cos, sin)
    qf = qf * (B_QK_DIM ** -0.5)
    qf = qf.transpose(0, 2, 3, 1, 4)
    kf = kf.transpose(0, 2, 3, 1, 4)
    vf = v.astype(jnp.float32).transpose(0, 2, 1, 3)
    lam = (jnp.exp(jnp.sum(lq1.astype(jnp.float32) * lk1.astype(jnp.float32)))
           - jnp.exp(jnp.sum(lq2.astype(jnp.float32) * lk2.astype(jnp.float32)))
           + lam_init)
    kpos = jnp.arange(seq)

    def block(i):
        start = i * Q_BLOCK
        qb = lax.dynamic_slice_in_dim(qf, start, Q_BLOCK, axis=3)
        s = jnp.einsum('bhmqd,bhmkd->bhmqk', qb, kf)
        qpos = start + jnp.arange(Q_BLOCK)
        mask = kpos[None, :] <= qpos[:, None]
        p = jax.nn.softmax(jnp.where(mask, s, -jnp.inf), axis=-1)
        a = p[:, :, 0] - lam * p[:, :, 1]
        return jnp.einsum('bhqk,bhkd->bhqd', a, vf)

    o = lax.map(block, jnp.arange(seq // Q_BLOCK))
    o = o.transpose(1, 0, 3, 2, 4).reshape(bsz, seq, B_HEADS, B_V_DIM)
    o = rms_norm(o, subln_g) * (1.0 - lam_init)
    return o.reshape(bsz, seq, B_WIDTH).astype(out_dtype)

def first_inputs(seed: int = 0) -> dict:
    key = jax.random.key(seed)
    ks = jax.random.split(key, 32)
    f32 = jnp.float32
    L = DEPTH

    def nrm(k, shape, scale):
        return jax.random.normal(k, shape, dtype=f32) * scale

    def gain(k, shape):
        return 1.0 + 0.01 * jax.random.normal(k, shape, dtype=f32)

    return {
        'x': jax.random.normal(ks[0], (BATCH, SEQ, D_MODEL), dtype=f32),
        'positions': jnp.broadcast_to(jnp.arange(SEQ, dtype=jnp.int32), (BATCH, SEQ)),
        'ffn1_norm': gain(ks[1], (L, D_MODEL)),
        'ffn1_w_gate': nrm(ks[2], (L, D_MODEL, D_FF), D_MODEL ** -0.5),
        'ffn1_w_up': nrm(ks[3], (L, D_MODEL, D_FF), D_MODEL ** -0.5),
        'ffn1_w_down': nrm(ks[4], (L, D_FF, D_MODEL), D_FF ** -0.5),
        'mix_norm': gain(ks[5], (L, D_MODEL)),
        'w_in': nrm(ks[6], (L, D_MODEL, IN_COLS), D_MODEL ** -0.5),
        'a_ln_gain': gain(ks[7], (L, A_WIDTH)),
        'a_ln_bias': nrm(ks[8], (L, A_WIDTH), 0.01),
        'a_w_s': nrm(ks[9], (L, A_GROUPS, CHUNK, CHUNK), 0.5 * CHUNK ** -0.5),
        'a_b_s': gain(ks[10], (L, A_GROUPS, CHUNK)),
        'a_w_proj': nrm(ks[11], (L, A_WIDTH, D_MODEL), A_WIDTH ** -0.5),
        'b_q_norm': gain(ks[12], (L, B_QK_DIM)),
        'b_k_norm': gain(ks[13], (L, B_QK_DIM)),
        'b_lambda_q1': nrm(ks[14], (L, B_QK_DIM), 0.1),
        'b_lambda_k1': nrm(ks[15], (L, B_QK_DIM), 0.1),
        'b_lambda_q2': nrm(ks[16], (L, B_QK_DIM), 0.1),
        'b_lambda_k2': nrm(ks[17], (L, B_QK_DIM), 0.1),
        'b_subln': gain(ks[18], (L, B_V_DIM)),
        'b_w_proj': nrm(ks[19], (L, B_WIDTH, D_MODEL), B_WIDTH ** -0.5),
        'w_out': nrm(ks[20], (L, D_MODEL, D_MODEL), D_MODEL ** -0.5),
        'ffn2_norm': gain(ks[21], (L, D_MODEL)),
        'ffn2_w_gate': nrm(ks[22], (L, D_MODEL, D_FF), D_MODEL ** -0.5),
        'ffn2_w_up': nrm(ks[23], (L, D_MODEL, D_FF), D_MODEL ** -0.5),
        'ffn2_w_down': nrm(ks[24], (L, D_FF, D_MODEL), D_FF ** -0.5),
    }

def first_block(x, positions, ffn1_norm, ffn1_w_gate, ffn1_w_up, ffn1_w_down, mix_norm, w_in,
              a_ln_gain, a_ln_bias, a_w_s, a_b_s, a_w_proj, b_q_norm, b_k_norm,
              b_lambda_q1, b_lambda_k1, b_lambda_q2, b_lambda_k2, b_subln, b_w_proj, w_out,
              ffn2_norm, ffn2_w_gate, ffn2_w_up, ffn2_w_down):
    bsz, seq, _ = x.shape
    for l in range(DEPTH):
        lam_init = 0.8 - 0.6 * math.exp(-0.3 * l)
        x = x + 0.5 * swiglu(rms_norm(x, ffn1_norm[l]), ffn1_w_gate[l], ffn1_w_up[l], ffn1_w_down[l])
        h = rms_norm(x, mix_norm[l])
        z = h @ w_in[l]
        g_a, g_b, z_uv, z_q, z_k, z_v = jnp.split(z, COL_SPLITS, axis=-1)
        y_a = gmlp_chunk_mixer(z_uv, a_ln_gain[l], a_ln_bias[l], a_w_s[l], a_b_s[l])
        q = z_q.reshape(bsz, seq, B_HEADS, 2, B_QK_DIM)
        k = z_k.reshape(bsz, seq, B_HEADS, 2, B_QK_DIM)
        v = z_v.reshape(bsz, seq, B_HEADS, B_V_DIM)
        y_b = diff_attention(q, k, v, positions, b_q_norm[l], b_k_norm[l],
                             b_lambda_q1[l], b_lambda_k1[l], b_lambda_q2[l], b_lambda_k2[l],
                             b_subln[l], lam_init)
        m = jax.nn.sigmoid(g_a) * (y_a @ a_w_proj[l]) + jax.nn.sigmoid(g_b) * (y_b @ b_w_proj[l])
        x = x + m @ w_out[l]
        x = x + 0.5 * swiglu(rms_norm(x, ffn2_norm[l]), ffn2_w_gate[l], ffn2_w_up[l], ffn2_w_down[l])
    return x


_first_inputs = first_inputs


def first_inputs(seed=0):
    import zlib

    import numpy as np

    out = dict(_first_inputs(seed))
    spreads = {}
    factors = {}
    for name, (base, spread) in spreads.items():
        noise = np.random.default_rng([zlib.crc32(name.encode()), seed]).standard_normal(out[name].shape)
        drawn = base * np.exp(spread * noise) if base else spread * noise
        out[name] = __import__('jax').numpy.asarray(drawn.astype(out[name].dtype))
    for name, factor in factors.items():
        out[name] = (out[name] * factor).astype(out[name].dtype)
    return out


_narrow_inputs = first_inputs


def first_inputs(seed=0):

    out = dict(_narrow_inputs(seed))
    wider = {'ffn1_norm': 12.0,
     'mix_norm': 7.63,
     'a_ln_gain': 12.0,
     'a_ln_bias': 12.0,
     'a_b_s': 12.0,
     'b_q_norm': 12.0,
     'b_k_norm': 12.0,
     'b_lambda_q1': 12.0,
     'b_subln': 12.0,
     'ffn2_norm': 12.0}
    for name, times in wider.items():
        mean = out[name].mean()
        out[name] = (mean + times * (out[name] - mean)).astype(out[name].dtype)
    return out


D_SSM = 512
SSM_GROUP = 16
N_SSM_GROUPS = D_SSM // SSM_GROUP
SSM_STATE = 64
D_ATTN = D_MODEL - D_SSM
HEAD_DIM = 64
N_Q_HEADS = D_ATTN // HEAD_DIM
N_KV_HEADS = 2
Q_PER_KV = N_Q_HEADS // N_KV_HEADS
KV_DIM = N_KV_HEADS * HEAD_DIM
D_IN = D_SSM + D_ATTN + 2 * KV_DIM
WINDOW = 128
BLOCK = 128
N_BUCKETS = 32
MAX_DISTANCE = 128
CONV_WIDTH = 3
N_MOD = 6
EPS = 1e-6
NEG_INF = -1e30


def _rms(x, w):
    xf = x.astype(jnp.float32)
    y = xf * lax.rsqrt(jnp.mean(xf * xf, axis=-1, keepdims=True) + EPS)
    return (y * w.astype(jnp.float32)).astype(x.dtype)

def _t5_bucket(n):
    n = np.maximum(n, 0)
    max_exact = N_BUCKETS // 2
    log_part = np.log(np.maximum(n, 1) / max_exact) / math.log(MAX_DISTANCE / max_exact)
    large = max_exact + (log_part * (N_BUCKETS - max_exact)).astype(np.int32)
    large = np.minimum(large, N_BUCKETS - 1)
    return np.where(n < max_exact, n, large).astype(np.int32)

def _s5(u, lam_re, lam_im, log_dt, b_re, b_im, c_re, c_im, d_skip, w_glu, b_glu):
    bsz, seq = u.shape[0], u.shape[1]
    f32 = jnp.float32
    ug = u.astype(f32).reshape(bsz, seq, N_SSM_GROUPS, SSM_GROUP)
    lr = jnp.minimum(lam_re.astype(f32), -1e-4)
    li = lam_im.astype(f32)
    dt = jnp.exp(log_dt.astype(f32))[:, None]
    mag = jnp.exp(dt * lr)
    a_re = mag * jnp.cos(dt * li)
    a_im = mag * jnp.sin(dt * li)
    den = lr * lr + li * li
    f_re = ((a_re - 1.0) * lr + a_im * li) / den
    f_im = (a_im * lr - (a_re - 1.0) * li) / den
    br = b_re.astype(f32)
    bi = b_im.astype(f32)
    bb_re = f_re[..., None] * br - f_im[..., None] * bi
    bb_im = f_re[..., None] * bi + f_im[..., None] * br
    bu_re = jnp.einsum("blgh,gph->blgp", ug, bb_re)
    bu_im = jnp.einsum("blgh,gph->blgp", ug, bb_im)
    shape_a = (1, seq, N_SSM_GROUPS, SSM_STATE)
    a_re_t = jnp.broadcast_to(a_re, shape_a)
    a_im_t = jnp.broadcast_to(a_im, shape_a)

    def combine(e1, e2):
        a1r, a1i, b1r, b1i = e1
        a2r, a2i, b2r, b2i = e2
        return (a2r * a1r - a2i * a1i,
                a2r * a1i + a2i * a1r,
                a2r * b1r - a2i * b1i + b2r,
                a2r * b1i + a2i * b1r + b2i)

    _, _, s_re, s_im = lax.associative_scan(combine, (a_re_t, a_im_t, bu_re, bu_im), axis=1)
    y = (jnp.einsum("blgp,ghp->blgh", s_re, c_re.astype(f32))
         - jnp.einsum("blgp,ghp->blgh", s_im, c_im.astype(f32))
         + d_skip.astype(f32).reshape(N_SSM_GROUPS, SSM_GROUP) * ug)
    z = jax.nn.gelu(y.reshape(bsz, seq, D_SSM))
    out = z * jax.nn.sigmoid(z @ w_glu.astype(f32) + b_glu.astype(f32))
    return out.astype(u.dtype)

def _swa_sink(q, k, v, rel_bias, sinks):
    bsz, seq = q.shape[0], q.shape[1]
    nb = seq // BLOCK
    f32 = jnp.float32
    qb = q.astype(f32).reshape(bsz, nb, BLOCK, N_KV_HEADS, Q_PER_KV, HEAD_DIM)
    pad = ((0, 0), (BLOCK, 0), (0, 0), (0, 0))
    kb = jnp.pad(k.astype(f32), pad).reshape(bsz, nb + 1, BLOCK, N_KV_HEADS, HEAD_DIM)
    vb = jnp.pad(v.astype(f32), pad).reshape(bsz, nb + 1, BLOCK, N_KV_HEADS, HEAD_DIM)
    k_band = jnp.concatenate([kb[:, :-1], kb[:, 1:]], axis=2)
    v_band = jnp.concatenate([vb[:, :-1], vb[:, 1:]], axis=2)
    logits = jnp.einsum("bnqhgd,bnkhd->bnhgqk", qb, k_band) * (HEAD_DIM ** -0.5)
    q_off = np.arange(BLOCK)[:, None] + BLOCK
    k_off = np.arange(2 * BLOCK)[None, :]
    dist = q_off - k_off
    bias = jnp.take(rel_bias.astype(f32), _t5_bucket(dist), axis=0)
    bias = bias.transpose(2, 0, 1).reshape(N_KV_HEADS, Q_PER_KV, BLOCK, 2 * BLOCK)
    key_pos = np.arange(nb)[:, None, None] * BLOCK + k_off[None] - BLOCK
    mask = (dist[None] >= 0) & (dist[None] < WINDOW) & (key_pos >= 0)
    logits = jnp.where(mask[None, :, None, None], logits + bias, NEG_INF)
    sink = sinks.astype(f32).reshape(N_KV_HEADS, Q_PER_KV)[None, None, :, :, None, None]
    m = jnp.maximum(jnp.max(logits, axis=-1, keepdims=True), sink)
    p = jnp.exp(logits - m)
    probs = p / (jnp.sum(p, axis=-1, keepdims=True) + jnp.exp(sink - m))
    out = jnp.einsum("bnhgqk,bnkhd->bnqhgd", probs, v_band)
    return out.reshape(bsz, seq, D_ATTN).astype(q.dtype)

def _conv_ffn(h, w_up, conv_w, conv_b, w_down):
    up = h @ w_up
    rhs = conv_w.reshape(CONV_WIDTH, 1, 2 * D_FF).astype(up.dtype)
    up = lax.conv_general_dilated(up, rhs, window_strides=(1,),
                                  padding=[(CONV_WIDTH - 1, 0)],
                                  dimension_numbers=("NWC", "WIO", "NWC"),
                                  feature_group_count=2 * D_FF) + conv_b
    val, gate = jnp.split(up, 2, axis=-1)
    return (jax.nn.silu(gate) * val) @ w_down

def second_inputs(seed: int = 0) -> dict:
    key = jax.random.key(seed)
    ks = jax.random.split(key, 28)
    f32 = jnp.float32

    def nrm(k, shape, scale):
        return jax.random.normal(k, shape, f32) * scale

    def gain(k, shape):
        return 1.0 + 0.05 * jax.random.normal(k, shape, f32)

    G, P, H = N_SSM_GROUPS, SSM_STATE, SSM_GROUP
    lam_im0 = math.pi * jnp.arange(P, dtype=f32)
    return {
        "x": nrm(ks[0], (BATCH, SEQ, D_MODEL), 1.0),
        "c": nrm(ks[1], (BATCH, D_MODEL), 1.0),
        "w_mod": nrm(ks[2], (DEPTH, D_MODEL, N_MOD * D_MODEL), 0.5 * D_MODEL ** -0.5),
        "b_mod": nrm(ks[3], (DEPTH, N_MOD * D_MODEL), 0.02),
        "norm1_w": gain(ks[4], (DEPTH, D_MODEL)),
        "w_in": nrm(ks[5], (DEPTH, D_MODEL, D_IN), D_MODEL ** -0.5),
        "lam_re": -0.5 * jnp.exp(0.1 * jax.random.normal(ks[6], (DEPTH, G, P), f32)),
        "lam_im": lam_im0 + 0.05 * jax.random.normal(ks[7], (DEPTH, G, P), f32),
        "log_dt": jax.random.uniform(ks[8], (DEPTH, G), f32, math.log(1e-3), math.log(1e-1)),
        "ssm_b_re": nrm(ks[9], (DEPTH, G, P, H), (2 * H) ** -0.5),
        "ssm_b_im": nrm(ks[10], (DEPTH, G, P, H), (2 * H) ** -0.5),
        "ssm_c_re": nrm(ks[11], (DEPTH, G, H, P), (2 * P) ** -0.5),
        "ssm_c_im": nrm(ks[12], (DEPTH, G, H, P), (2 * P) ** -0.5),
        "ssm_d": nrm(ks[13], (DEPTH, D_SSM), 1.0),
        "w_glu": nrm(ks[14], (DEPTH, D_SSM, D_SSM), D_SSM ** -0.5),
        "b_glu": nrm(ks[15], (DEPTH, D_SSM), 0.02),
        "q_norm_w": gain(ks[16], (DEPTH, HEAD_DIM)),
        "k_norm_w": gain(ks[17], (DEPTH, HEAD_DIM)),
        "rel_bias": nrm(ks[18], (N_BUCKETS, N_Q_HEADS), 0.5),
        "sinks": nrm(ks[19], (DEPTH, N_Q_HEADS), 0.5),
        "out_norm_ssm": gain(ks[20], (DEPTH, D_SSM)),
        "out_norm_attn": gain(ks[21], (DEPTH, D_ATTN)),
        "w_out": nrm(ks[22], (DEPTH, D_MODEL, D_MODEL), D_MODEL ** -0.5),
        "norm2_w": gain(ks[23], (DEPTH, D_MODEL)),
        "w_up": nrm(ks[24], (DEPTH, D_MODEL, 2 * D_FF), D_MODEL ** -0.5),
        "conv_w": nrm(ks[25], (DEPTH, CONV_WIDTH, 2 * D_FF), CONV_WIDTH ** -0.5),
        "conv_b": nrm(ks[26], (DEPTH, 2 * D_FF), 0.02),
        "w_down": nrm(ks[27], (DEPTH, D_FF, D_MODEL), D_FF ** -0.5),
    }

def second_block(x, c, w_mod, b_mod, norm1_w, w_in, lam_re, lam_im, log_dt,
              ssm_b_re, ssm_b_im, ssm_c_re, ssm_c_im, ssm_d, w_glu, b_glu,
              q_norm_w, k_norm_w, rel_bias, sinks, out_norm_ssm, out_norm_attn,
              w_out, norm2_w, w_up, conv_w, conv_b, w_down):
    bsz, seq = x.shape[0], x.shape[1]
    c_act = jax.nn.silu(c)
    for l in range(DEPTH):
        mod = (c_act @ w_mod[l] + b_mod[l])[:, None, :]
        sh1, sc1, g1, sh2, sc2, g2 = jnp.split(mod, N_MOD, axis=-1)

        h = _rms(x, norm1_w[l]) * (1 + sc1) + sh1
        proj = h @ w_in[l]
        u, q, k, v = jnp.split(proj, [D_SSM, D_SSM + D_ATTN, D_SSM + D_ATTN + KV_DIM], axis=-1)
        y_ssm = _s5(u, lam_re[l], lam_im[l], log_dt[l], ssm_b_re[l], ssm_b_im[l],
                    ssm_c_re[l], ssm_c_im[l], ssm_d[l], w_glu[l], b_glu[l])
        q = _rms(q.reshape(bsz, seq, N_Q_HEADS, HEAD_DIM), q_norm_w[l])
        k = _rms(k.reshape(bsz, seq, N_KV_HEADS, HEAD_DIM), k_norm_w[l])
        v = v.reshape(bsz, seq, N_KV_HEADS, HEAD_DIM)
        y_attn = _swa_sink(q, k, v, rel_bias, sinks[l])
        mixed = jnp.concatenate([_rms(y_ssm, out_norm_ssm[l]),
                                 _rms(y_attn, out_norm_attn[l])], axis=-1)
        x = x + g1 * (mixed @ w_out[l])

        h2 = _rms(x, norm2_w[l]) * (1 + sc2) + sh2
        x = x + g2 * _conv_ffn(h2, w_up[l], conv_w[l], conv_b[l], w_down[l])
    return x


def setup_inputs(seed=0):
    out = dict(first_inputs(seed))
    for name, value in second_inputs(seed + 1).items():
        if name != "x":
            out[name + "_2"] = value
    return out


def reference(
    x, positions, ffn1_norm, ffn1_w_gate, ffn1_w_up, ffn1_w_down, mix_norm, w_in, a_ln_gain,
    a_ln_bias, a_w_s, a_b_s, a_w_proj, b_q_norm, b_k_norm, b_lambda_q1, b_lambda_k1,
    b_lambda_q2, b_lambda_k2, b_subln, b_w_proj, w_out, ffn2_norm, ffn2_w_gate, ffn2_w_up,
    ffn2_w_down, c_2, w_mod_2, b_mod_2, norm1_w_2, w_in_2, lam_re_2, lam_im_2, log_dt_2,
    ssm_b_re_2, ssm_b_im_2, ssm_c_re_2, ssm_c_im_2, ssm_d_2, w_glu_2, b_glu_2, q_norm_w_2,
    k_norm_w_2, rel_bias_2, sinks_2, out_norm_ssm_2, out_norm_attn_2, w_out_2, norm2_w_2,
    w_up_2, conv_w_2, conv_b_2, w_down_2,
):
    x = first_block(
        x, positions, ffn1_norm, ffn1_w_gate, ffn1_w_up, ffn1_w_down, mix_norm, w_in, a_ln_gain,
        a_ln_bias, a_w_s, a_b_s, a_w_proj, b_q_norm, b_k_norm, b_lambda_q1, b_lambda_k1,
        b_lambda_q2, b_lambda_k2, b_subln, b_w_proj, w_out, ffn2_norm, ffn2_w_gate, ffn2_w_up,
        ffn2_w_down,
    )
    return second_block(
        x, c_2, w_mod_2, b_mod_2, norm1_w_2, w_in_2, lam_re_2, lam_im_2, log_dt_2, ssm_b_re_2,
        ssm_b_im_2, ssm_c_re_2, ssm_c_im_2, ssm_d_2, w_glu_2, b_glu_2, q_norm_w_2, k_norm_w_2,
        rel_bias_2, sinks_2, out_norm_ssm_2, out_norm_attn_2, w_out_2, norm2_w_2, w_up_2,
        conv_w_2, conv_b_2, w_down_2,
    )


_drawn_inputs = setup_inputs


def setup_inputs(seed=0):
    import zlib

    import numpy as np

    out = dict(_drawn_inputs(seed))
    spreads = {}
    factors = {'a_ln_gain': 4.415,
     'a_ln_bias': 4.485,
     'b_lambda_q1': 53.12,
     'norm1_w_2': 4.799,
     'lam_re_2': 64.0,
     'lam_im_2': 38.496,
     'log_dt_2': 45.56,
     'ssm_b_re_2': 48.976,
     'ssm_b_im_2': 52.64,
     'ssm_c_re_2': 53.52,
     'ssm_c_im_2': 51.296,
     'b_glu_2': 8.0,
     'q_norm_w_2': 8.0,
     'k_norm_w_2': 8.0,
     'sinks_2': 189.535,
     'out_norm_ssm_2': 6.604,
     'out_norm_attn_2': 6.439,
     'norm2_w_2': 4.353,
     'conv_b_2': 8.0}
    for name, (base, spread) in spreads.items():
        noise = np.random.default_rng([zlib.crc32(name.encode()), seed]).standard_normal(out[name].shape)
        drawn = base * np.exp(spread * noise) if base else spread * noise
        out[name] = jnp.asarray(drawn.astype(out[name].dtype))
    for name, factor in factors.items():
        out[name] = (out[name] * factor).astype(out[name].dtype)
    return out
```

```python
import math
from contextlib import ExitStack

import numpy as np

import concourse.bass as bass
from concourse import mybir

F32 = mybir.dt.float32
F32R = mybir.dt.float32r
I32 = mybir.dt.int32
ALU = mybir.AluOpType
ACT = mybir.ActivationFunctionType
AX = mybir.AxisListType

P = 128
T = 512
TB = T // P
D = 1024
KD = D // P
FF = 2816
KF = FF // P
A_W = 512
A_G = 8
HEADS = 8
QK = 64
ROT = 8
LAM_INIT = 0.8 - 0.6 * math.exp(-0.3 * 0)
EPS = 1e-6
LN_EPS = 1e-5
NS = 16
SG = 16
WIN = 128
NQ = 8
NKV = 2
NEG = -1e30
BAND = 2 * P + P - 1
PANEL = 2048
PC = 256
DOWN_K = ((0, 6), (6, 6), (12, 5), (17, 5))
GU_STEPS = FF // PC
BESIDE = KF - 6
BESIDE_STEPS = BESIDE // 2
MOD_GROUPS = 6 * D // T
MOD_SLOTS = 4
ROT_SLOTS = 3
PHASES = {"ffn1": ((0, BESIDE_STEPS, True, True), (BESIDE_STEPS, GU_STEPS, False, False)),
          "ffn2": ((0, MOD_GROUPS - BESIDE_STEPS, True, True), (MOD_GROUPS - BESIDE_STEPS, BESIDE_STEPS, False, True),
                   (BESIDE_STEPS, GU_STEPS, False, False))}
BESIDE_AT = {"ffn1": 0, "ffn2": BESIDE_STEPS}
DOWN_PANELS = 16
FFN_PANELS = 2 * GU_STEPS + DOWN_PANELS
MIX_PANELS = 34
MIX2_PANELS = 10
BASE = {"ffn1": 0}
BASE["mixer"] = BASE["ffn1"] + FFN_PANELS
BASE["ffn2"] = BASE["mixer"] + MIX_PANELS
BASE["mix2"] = BASE["ffn2"] + FFN_PANELS
BASE["ffn3"] = BASE["mix2"] + MIX2_PANELS
END = BASE["ffn3"] + FFN_PANELS
STAGES = ("ffn1", "mixer", "ffn2", "mix2", "ffn3")
ROUND = 12582912.0
TWO_PI = 2.0 * math.pi
PI_1 = 6.28125
PI_2 = float(np.float32(np.round((TWO_PI - PI_1) * 2.0**20) / 2.0**20))
PI_3 = TWO_PI - PI_1 - PI_2
PI_LOW = 3.1415925
ROWS = {}
for _tile, _names in enumerate((
    (("ffn1_norm", 8), ("mix_norm", 8), ("ffn2_norm", 8), ("norm1_w_2", 8), ("norm2_w_2", 8), ("b_mod_2", 48),
     ("ssm_d_2", 4), ("b_glu_2", 4), ("out_norm_ssm_2", 4), ("out_norm_attn_2", 4), ("b_subln", 1), ("c_2", 8)),
    (("lam_re_2", 16), ("lam_im_2", 16), ("conv_b_2", 44), ("conv_w_2:2", 44)),
    (("conv_w_2:0", 44), ("conv_w_2:1", 44)),
)):
    _at = 0
    for _name, _n in _names:
        ROWS[_name] = (_tile, _at, _n)
        _at += _n
ROW_COUNTS = tuple(max(a + n for t, a, n in ROWS.values() if t == tile) for tile in range(3))


class Steps:

    def __init__(self, engine, semaphore):
        self.engine, self.semaphore, self.n = engine, semaphore, 0

    def __call__(self, instruction):
        instruction.then_inc(self.semaphore, 1)
        self.n += 1
        self.engine.wait_ge(self.semaphore, self.n)


def build(nc, inp, rel_onehot, out, last="ffn3"):
    stages = STAGES[:STAGES.index(last) + 1]
    end = BASE[last] + {"mixer": MIX_PANELS, "mix2": MIX2_PANELS}.get(last, FFN_PANELS)

    def col_major(w):
        return w.rearrange("l (k p) n -> p (l k) n", p=P)

    rot_dram = nc.dram_tensor("rotations", (2, NS, P, T), F32).ap()
    band_dram = nc.dram_tensor("band", (NQ, BAND), F32)

    with ExitStack() as ctx:
        def sb(name, shape, dt=F32, scope=ctx):
            return scope.enter_context(nc.sbuf_tensor(name, shape, dt))

        sems = {}

        def S(name):
            if name not in sems:
                sems[name] = ctx.enter_context(nc.semaphore(name))
            return sems[name]

        B = [ctx.enter_context(nc.psum_tensor(f"bank{i}", [P, T], F32)) for i in range(8)]

        x = sb("x", [P, KD, T])
        w_raw = [sb(f"w_raw{i}", [P, PANEL]) for i in range(2)]
        w_hi = [sb(f"w_hi{i}", [P, PANEL], F32R) for i in range(2)]
        w_lo = [sb(f"w_lo{i}", [P, PANEL], F32R) for i in range(2)]
        tmp = sb("tmp", [P, 6, T])
        rstd = sb("rstd", [P, T])
        ident = sb("ident", [P, P])
        ones = sb("ones", [P, P])
        causal = sb("causal", [P, P])
        vec = sb("vec", [P, 3, P])
        small = sb("small", [P, 96])
        stat = sb("stat", [P, 96])
        cos_t = sb("cos_t", [P, TB, ROT])
        sin_t = sb("sin_t", [P, TB, ROT])
        gains = sb("gains", [P, 4, QK])
        lam_in = sb("lam_in", [P, 4, QK])
        sink = sb("sink", [P, NQ])
        mod = sb("mod", [P, 48])
        gain2 = sb("gain2", [P, 2, KD])
        s5 = sb("s5", [P, 24, NS])
        pos_i = sb("pos_i", [P, TB], I32)

        def col(name, i):
            t, a, _ = ROWS[name]
            return vec[:, t, a + i:a + i + 1]

        def cols(name):
            t, a, n = ROWS[name]
            return vec[:, t, a:a + n]

        def col_at(name, i, off=0):
            t, a, _ = ROWS[name]
            return vec[:, t, bass.ds(i + (a + off), 1)]

        def overlay(size, *tiles):
            made = []
            for first, name, shape, dt in tiles:
                with ExitStack() as area:
                    if first:
                        sb(f"under_{name}", [P, first * T], F32, area)
                    made.append(sb(name, shape, dt, area))
            return made

        h_hi, h_lo, o_tok, yb_hi, yb_lo, rot, sc_a, sc_v, sc_p = overlay(
            2 * KD,
            (0, "h_hi", [P, KD, T], F32R), (KD, "h_lo", [P, KD, T], F32R),
            (0, "o_tok", [P, TB, D], F32), (0, "yb_hi", [P, KD, T], F32R), (KD, "yb_lo", [P, KD, T], F32R),
            (0, "rot", [P, ROT_SLOTS, 2, T], F32), (2 * ROT_SLOTS, "sc_a", [P, 4, T], F32),
            (2 * ROT_SLOTS + 4, "sc_v", [P, 4, T], F32), (2 * ROT_SLOTS + 8, "sc_p", [P, 2, T], F32),
        )
        sb("h_area", [P, 2 * KD * T])

        hid_hi, hid_lo, x_in, rows, oh, rel, band, ang, log_dt, rot_t, rot_ti, rot_n, rot_r, rot_abs, rot_cs, mod_acc, mod_raw = overlay(
            2 * KF,
            (0, "hid_hi", [P, KF, T], F32R), (KF, "hid_lo", [P, KF, T], F32R),
            (0, "x_in", [P, TB, D], F32), (8, "rows", [P, 3, P], F32), (9, "oh", [33, BAND], F32),
            (10, "rel", [33, NQ], F32), (11, "band_row", [NQ, BAND], F32), (12, "ang", [P, 3, TB, ROT], F32), (13, "log_dt", [P, 2 * NS], F32),
            (BESIDE, "rot_t", [P, T], F32), (BESIDE + 1, "rot_ti", [P, T], I32), (BESIDE + 1, "rot_n", [P, T], F32),
            (BESIDE + 2, "rot_r", [P, T], F32), (BESIDE + 3, "rot_abs", [P, T], F32), (BESIDE + 4, "rot_cs", [P, 2, T], F32),
            (KF + BESIDE, "mod_acc", [P, T], F32), (KF + BESIDE + 1, "mod_raw", [P, MOD_SLOTS, T], F32),
        )
        vg, u_g, ya_hi, ya_lo, qT, kT, vtok, ga, gb, aT, m_hi, m_lo, ln_g, ln_b, wsT, ws_in, bs, qk_raw0, qk_raw1 = overlay(
            2 * KF,
            (0, "vg", [P, TB, A_W], F32), (4, "u_g", [P, 4, T], F32),
            (8, "ya_hi", [P, 4, T], F32R), (4, "ya_lo", [P, 4, T], F32R),
            (12, "qT", [P, HEADS, T], F32), (20, "kT", [P, HEADS, T], F32), (28, "vtok", [P, TB, D], F32),
            (36, "ga", [P, KD, T], F32),
            (0, "gb", [P, KD, T], F32), (8, "aT", [P, 2, T], F32),
            (12, "m_hi", [P, KD, T], F32R), (20, "m_lo", [P, KD, T], F32R),
            (12, "ln_g", [P, A_W], F32), (13, "ln_b", [P, A_W], F32),
            (28, "wsT", [P, A_G, P], F32), (30, "ws_in", [P, A_G, P], F32), (32, "bs", [P, 4, P], F32),
            (36, "qk_raw0", [P, TB, T], F32), (40, "qk_raw1", [P, TB, T], F32),
        )
        qk_raw = [qk_raw0, qk_raw1]
        (u2, q2T, k2T, v2, bbT, cT, yat, b_in, bb, c_in, bd, bias, hank, k2_dup, q_sq, k_sq, pT, prob,
         z, z_hi, z_lo) = overlay(
            2 * KF,
            (0, "u2", [P, 4, T], F32), (4, "q2T", [P, 4, T], F32), (8, "k2T", [P, NKV, T], F32),
            (10, "v2", [P, TB, NKV, 2, QK], F32),
            (12, "bbT", [P, 2, NS, P], F32), (20, "cT", [P, 2, NS, P], F32), (28, "yat", [P, 4, T], F32),
            (32, "b_in", [P, 2, NS, SG], F32), (33, "bb", [P, 2, NS, SG], F32), (34, "c_in", [P, 2, 4, 2, QK], F32),
            (36, "bd", [P, NS, P], F32), (40, "bias", [P, NQ, 2 * P], F32), (28, "hank", [P, NQ, 2 * P], F32),
            (28, "k2_dup", [P, TB, NKV, 2, QK], F32), (4, "q_sq", [P, TB, T], F32), (8, "k_sq", [P, TB, NKV * QK], F32),
            (32, "pT", [P, 2, 2, T], F32), (36, "prob", [P, 2, 4, 2 * P], F32),
            (32, "z", [P, 4, T], F32), (36, "z_hi", [P, 4, T], F32R), (40, "z_lo", [P, 4, T], F32R),
        )

        SW_UNITS = [(b, n) for b in range(TB) for n in range(NKV)]
        SW_BLOCKS = [(1,) if b == 0 else (0, 1) for b, _ in SW_UNITS]
        SW_BEFORE = [sum(len(k) for k in SW_BLOCKS[:u]) for u in range(len(SW_UNITS) + 1)]

        def scan_product(st, i):
            if st % 2 == 0:
                return tmp[:, i, :]
            return tmp[:, 4 + i, :] if i < 2 else sc_p[:, i - 2, :]

        def sw_cols(first, u):
            return stat[:, first + 4 * (u % 2):first + 4 * (u % 2) + 4]

        sb("shared_area", [P, 2 * KF * T])

        def used(n, quarters=4):
            return 4 * n + quarters

        def panel(buf, n, k, c):
            return buf[n % 2][:, :k * c].rearrange("p (k c) -> p k c", k=k)

        X_OF = {"start": ("x_turned", 1), "ffn1": ("ffn1_x", 5), "mixer": ("mixer_x", 1), "ffn2": ("ffn2_x", 5),
                "mix2": ("mix2_x", 1), "ffn3": ("ffn3_x", 5)}

        NORM = {"n1": 0, "nm": KD, "n2": 2 * KD, "p1": 3 * KD, "pa": 4 * KD, "ps": 4 * KD + 4, "p2": 5 * KD}
        NORMS = list(NORM)
        HID = {"ffn1": 0, "ffn2": KF, "ffn3": 2 * KF}

        def wait_x(eng, stage, k):
            name, first = X_OF[stage]
            eng.wait_ge(S(name), first + k)

        def bank_of(t):
            return B[t % 4]

        MIX = BASE["mixer"]
        MIX2 = BASE["mix2"]
        MIX_PARTS = (("v_gm", 0, 2, 4), ("u_gm", 2, 2, 4), ("qk0", 4, 2, 4), ("qk1", 6, 2, 4), ("qk2", 8, 2, 4),
                     ("qk3", 10, 2, 4), ("v0", 12, 2, 4), ("v1", 14, 2, 4), ("g_a", 16, 4, 8), ("a_proj", 20, 2, 8),
                     ("g_b", 22, 4, 8), ("b_proj", 26, 4, 8), ("w_out", 30, 4, 8))
        MIX2_PARTS = (("u2", 0, 2, 4), ("q2", 2, 2, 4), ("kv2", 4, 1, 4), ("glu", 5, 1, 4), ("w_out2", 6, 4, 8))
        PART = {name: (MIX + first, panels, outs) for name, first, panels, outs in MIX_PARTS}
        PART.update({name: (MIX2 + first, panels, outs) for name, first, panels, outs in MIX2_PARTS})
        BEFORE = {b[0]: a for parts in (MIX_PARTS, MIX2_PARTS) for a, b in zip(parts, parts[1:])}
        BEFORE = {name: (part[0], part[3]) for name, part in BEFORE.items()}
        W_IN_COL = {"v_gm": 2 * D + A_W, "qk0": 2 * D + 2 * A_W, "qk1": 2 * D + 2 * A_W + T, "qk2": 3 * D + 2 * A_W,
                    "qk3": 3 * D + 2 * A_W + T, "v0": 4 * D + 2 * A_W, "v1": 4 * D + 2 * A_W + T}
        UNITS = [(h, i) for h in range(HEADS) for i in range(TB)]

        eps_col, half_pi_col, ln_eps_col = (small[:, i:i + 1] for i in (20, 21, 22))
        q2_raw = tmp[:, 0:4, :]
        k2_raw = tmp[:, 4, :].rearrange("p (b n) -> p b n", b=TB)

        block = ctx.enter_context(nc.Block())

        @block.sync
        def _(sp):
            def load(n, source, k, c):
                if isinstance(n, int):
                    if n >= 2:
                        sp.wait_ge(S("w_split"), n - 1)
                else:
                    sp.wait_ge(S("w_split"), n[0] - 1)
                i = n if isinstance(n, int) else n[1]
                sp.dma_start(panel(w_raw, i, k, c), source).then_inc(S(f"w_landed{i % 2}"), 16)

            def load_ffn(name, gate, up, gate_col, up_col, down):
                base = BASE[name]
                gate_v, up_v, down_v = col_major(gate), col_major(up), col_major(down)
                first = 0
                if base == 0:
                    load(0, gate_v[:, :, gate_col:gate_col + PC], KD, PC)
                    load(1, up_v[:, :, up_col:up_col + PC], KD, PC)
                    first = 1
                with sp.Fori(first, GU_STEPS) as i:
                    load((i * 2 + base, base), gate_v[:, :, bass.ds(i * PC + gate_col, PC)], KD, PC)
                    load((i * 2 + (base + 1), base + 1), up_v[:, :, bass.ds(i * PC + up_col, PC)], KD, PC)
                base += 2 * GU_STEPS
                with sp.Fori(0, 2) as j:
                    for c in range(8):
                        k0, kn = DOWN_K[c % 4]
                        load((j * 8 + (base + c), base + c),
                             down_v[:, k0:k0 + kn, bass.ds(j * 512 + c // 4 * PC, PC)], kn, PC)

            def load_tokens(name, w, at):
                base = PART[name][0]
                for half in range(2):
                    load(base + half, w[:, 4 * half:4 * half + 4, at:at + T], 4, T)

            def load_features(name, w, at, first=0, end=None):
                base, panels, _ = PART[name]
                for i in range(first, end or panels):
                    load(base + i, w[:, :, at + i * PC:at + (i + 1) * PC], KD, PC)

            x_v = inp["x"].rearrange("o (b p) d -> p (o b) d", p=P)
            sp.dma_start(x_in[:, :, 0:T], x_v[:, :, 0:T]).then_inc(S("x_landed0"), 16)
            sp.dma_start(x_in[:, :, T:D], x_v[:, :, T:D]).then_inc(S("x_landed1"), 16)
            load_ffn("ffn1", inp["ffn1_w_gate"], inp["ffn1_w_up"], 0, 0, inp["ffn1_w_down"])
            if "mixer" in stages:
                w_in = col_major(inp["w_in"])

                load_tokens("v_gm", w_in, W_IN_COL["v_gm"])
                load_features("u_gm", w_in, 2 * D)
                for name in ("qk0", "qk1", "qk2", "qk3", "v0", "v1"):
                    load_tokens(name, w_in, W_IN_COL[name])
                load_features("g_a", w_in, 0)
                for i in range(2):
                    load(PART["a_proj"][0] + i, col_major(inp["a_w_proj"])[:, :, i * T:(i + 1) * T], 4, T)
                load_features("g_b", w_in, D)
                load_features("b_proj", col_major(inp["b_w_proj"]), 0)
                load_features("w_out", col_major(inp["w_out"]), 0)
            if "ffn2" in stages:
                load_ffn("ffn2", inp["ffn2_w_gate"], inp["ffn2_w_up"], 0, 0, inp["ffn2_w_down"])
            if "mix2" in stages:
                w_in = col_major(inp["w_in_2"])
                load_features("u2", w_in, 0)
                load_tokens("q2", w_in, T)
                load(PART["kv2"][0], w_in[:, :, 2 * T:2 * T + PC], KD, PC)
                load(PART["glu"][0], col_major(inp["w_glu_2"]), 4, T)
                load_features("w_out2", col_major(inp["w_out_2"]), 0, 0, 3)
                sp.wait_ge(S("rot_stored"), 16 * (NS + 1))
                sp.wait_ge(S("pe_done"), used(PART["kv2"][0]))
                for st in range(NS):
                    if st >= ROT_SLOTS:
                        sp.wait_ge(S("scan_p"), 2 * (st - ROT_SLOTS) + 2)
                        sp.wait_ge(S("scan_q"), 2 * (st - ROT_SLOTS) + 2)
                    sp.dma_start(rot[:, st % ROT_SLOTS], rot_dram[:, st].rearrange("w p t -> p w t")).then_inc(S(f"rot_landed{st % ROT_SLOTS}"), 16)
                load_features("w_out2", col_major(inp["w_out_2"]), 0, 3, 4)
            if "ffn3" in stages:
                load_ffn("ffn3", inp["w_up_2"], inp["w_up_2"], 0, FF, inp["w_down_2"])
            out_v = out.rearrange("o (b p) d -> p (o b) d", p=P)
            for b in range(TB):
                for half in range(2):
                    sp.wait_ge(S(f"out_turned{half}"), b + 1)
                sp.dma_start(out_v[:, b, :], x_in[:, b, :]).then_inc(S("out_stored"), 16)
            sp.wait_ge(S("out_stored"), 16 * TB)

        @block.gpsimd
        def _(pool):
            done = Steps(pool, S("pool_done"))
            done(pool.memset(ones[:], 1.0))
            done(pool.memset(ident[:], 0.0))
            done(pool.memset(causal[:], 0.0))
            done(pool.affine_select(out=ident[:], in_=ident[:], compare_op=ALU.not_equal, fill=1.0, base=0,
                                    pattern=[[-1, P]], channel_multiplier=1))
            done(pool.affine_select(out=causal[:], in_=causal[:], compare_op=ALU.is_ge, fill=NEG, base=0,
                                    pattern=[[-1, P]], channel_multiplier=1))
            pool.memset(rel[32:33, :], 1.0).then_inc(S("consts_made"), 1)
            pool.wait_ge(S("band_made"), 1)
            pool.dma_start(band_dram.ap(), band[:]).then_inc(S("band_stored"), 16)
            wm = col_major(inp["w_mod_2"])

            def beside(name):
                done(pool.iota(rot_ti[:], pattern=[[1, T]], base=0, channel_multiplier=0))
                pool.tensor_copy(rot_t[:], rot_ti[:]).then_inc(S("rot_t_made"), 1)
                first = BESIDE_AT[name]
                groups = sum(end - start for start, end, mods, _ in PHASES[name] if mods)
                with pool.Fori(0, groups) as i:
                    for k in range(KD):
                        pool.wait_ge(S("mod_step"), i * KD + (first * KD + k + 1))
                        pool.dma_start(mod_raw[:, k % MOD_SLOTS, :], wm[:, k, bass.ds(i * T + first * T, T)])\
                            .then_inc(S(f"mod_landed{k % MOD_SLOTS}"), 16)

            beside("ffn1")
            if "mixer" in stages:
                pool.wait_ge(S("ws_landed"), 16)
                pool.affine_select(out=ws_in[:], in_=ws_in[:], compare_op=ALU.is_ge, fill=0.0, base=0,
                                   pattern=[[0, A_G], [-1, P]], channel_multiplier=1).then_inc(S("ws_masked"), 1)
            if "ffn2" in stages:
                wait_x(pool, "mixer", KD - 1)
                beside("ffn2")
            if "mix2" in stages:
                wait_x(pool, "ffn2", 0)
                done(pool.memset(causal[:], 0.0))
                pool.affine_select(out=causal[:], in_=causal[:], compare_op=ALU.not_equal, fill=1.0, base=1 - P,
                                   pattern=[[1, P]], channel_multiplier=1).then_inc(S("flip_made"), 1)
                for st in range(NS + 1):
                    if st < NS:
                        for i, op in enumerate((ALU.add, ALU.subtract)):
                            pool.wait_ge(S("scan_in"), 4 * st + 2 * i + 2)
                            if st:
                                pool.wait_ge(S("scanned"), 2 * (st - 1) + i + 1)
                            pool.tensor_tensor(sc_v[:, i, :], sc_a[:, 2 * i, :], sc_a[:, 2 * i + 1, :], op).then_inc(S("scan_v"), 1)
                    if st:
                        r = rot[:, (st - 1) % ROT_SLOTS]
                        pool.wait_ge(S("scanned"), 2 * st - 1)
                        if st >= 3:
                            pool.wait_ge(S("y_added"), st - 2)
                        for i in range(2):
                            pool.tensor_tensor(scan_product(st - 1, i), sc_v[:, 2, :], r[:, i, :], ALU.mult).then_inc(S("scan_p"), 1)

        @block.scalar
        def _(act):
            done = Steps(act, S("act_done"))

            def split(n, i=None):
                if i is None:
                    if n >= end:
                        return
                    i = n
                    act.wait_ge(S(f"w_landed{i % 2}"), 16 * (n // 2 + 1))
                    if n >= 2:
                        act.wait_ge(S("pe_done"), used(n - 2))
                else:
                    act.wait_ge(S(f"w_landed{i % 2}"), (n - (i % 2)) * 8 + 16)
                    act.wait_ge(S("pe_done"), (n - 2) * 4 + 4)
                act.copy(w_hi[i % 2][:], w_raw[i % 2][:]).then_inc(S("w_hi_done"), 1)

            def norm(name, tiles, ready, count, shift=None, hi=None, width=D):
                hi = h_hi if hi is None else hi
                at = NORM[name]
                for k in range(count):
                    ready(act, k)
                    if k >= 2:
                        act.wait_ge(S("norm_summed"), at + k - 1)
                    act.activation(tmp[:, k % 2, :], tiles[:, k, :], ACT.Square).then_inc(S("norm_sq"), 1)
                act.wait_ge(S("norm_summed"), at + count)
                act.activation(rstd[:], B[7][:], ACT.Sqrt, scale=1.0 / width, bias=eps_col).then_inc(S("norm_root"), 1)
                for k in range(count):
                    act.wait_ge(S("norm_h"), at + k + 1)
                    source = tmp[:, 2 + k % 4, :]
                    if shift is None:
                        act.copy(hi[:, k, :], source).then_inc(S("norm_hi"), 1)
                    else:
                        act.activation(hi[:, k, :], source, ACT.Identity, bias=shift(k)).then_inc(S("norm_hi"), 1)

            def rotations(st):
                act.wait_ge(S("rot_turns"), st + 1)
                act.wait_ge(S("rot_stored"), st * 16 + 16)
                act.activation(rot_cs[:, 1, :], rot_r[:], ACT.Sin, scale=-TWO_PI).then_inc(S("rot_made"), 1)
                act.activation(rot_abs[:], rot_r[:], ACT.Abs).then_inc(S("rot_read"), 1)
                act.wait_ge(S("rot_read"), st + 2)
                act.activation(rot_cs[:, 0, :], rot_abs[:], ACT.Sin, scale=-TWO_PI, bias=half_pi_col).then_inc(S("rot_made"), 1)
                act.wait_ge(S("rot_made"), st * 2 + 2)
                act.dma_start(rot_dram[:, bass.ds(st, 1)].rearrange("w s p t -> p (w s) t"), rot_cs[:]).then_inc(S("rot_stored"), 16)

            def swiglu(name):
                base = BASE[name]
                for start, stop, _, rots in PHASES[name]:
                    if not rots:
                        act.wait_ge(S("rot_stored"), 16 * (BESIDE_AT[name] + BESIDE_STEPS + 1))
                    with act.Fori(start, stop) as i:
                        if rots:
                            rotations(i + BESIDE_AT[name])
                        split(i * 2 + (base + 2), base)
                        for t in range(2):
                            act.wait_ge(S("pe_done"), i * 8 + (4 * base + 2 * t + 2))
                            act.wait_ge(S("hid"), i * 2 + (HID[name] + t + 1))
                            act.activation(tmp[:, t, :], B[t][:], ACT.Silu).then_inc(S("silu"), 1)
                        split(i * 2 + (base + 3), base + 1)
                        for t in range(2):
                            act.wait_ge(S("hid"), i * 2 + (HID[name] + t + 3))
                            act.copy(hid_hi[:, bass.ds(i * 2 + t, 1), :], tmp[:, 2 + t:3 + t, :]).then_inc(S("hid_hi"), 1)

            def down(name):
                base = BASE[name] + 2 * GU_STEPS
                steps = 2
                if base + DOWN_PANELS == end:
                    steps = 1
                with act.Fori(0, steps) as j:
                    for c in range(8):
                        split(j * 8 + (base + c + 2), base + c)
                if steps == 1:
                    for c in range(8):
                        split(base + 8 + c + 2)

            act.sem_inc(S("silu"), 2)
            act.sem_inc(S("rot_read"), 1)
            act.sem_inc(S("rot_stored"), 16)
            for name, (tile, at, n) in ROWS.items():
                param, _, tap = name.partition(":")
                source = inp[param][0, int(tap)] if tap else (inp[param][0] if inp[param].shape[0] == 1 else inp[param])
                if len(source.shape) == 1:
                    source = source.rearrange("(n p) -> n p", p=P)
                elif source.shape[1] != P:
                    source = source.rearrange("(n two) p -> n (two p)", two=P // source.shape[1])
                act.dma_start(rows[at:at + n, tile, :], source).then_inc(S("rows_landed"), 16)
            spread = 0
            for tile, names in ((gains, ("b_q_norm", "b_k_norm", "q_norm_w_2", "k_norm_w_2")),
                                (lam_in, ("b_lambda_q1", "b_lambda_k1", "b_lambda_q2", "b_lambda_k2"))):
                for i, name in enumerate(names):
                    act.dma_start(tile[:, i, :], inp[name][0].partition_broadcast(P)).then_inc(S("spread_landed"), 16)
                    spread += 16
            act.dma_start(sink[:], inp["sinks_2"][0].partition_broadcast(P)).then_inc(S("spread_landed"), 16)
            spread += 48
            act.dma_start(log_dt[:], inp["log_dt_2"][0].partition_broadcast(P)).then_inc(S("spread_landed"), 16)
            act.dma_start(pos_i[:], inp["positions"].rearrange("o (b p) -> p (o b)", p=P),
                          allow_slow_non_contiguous=True).then_inc(S("spread_landed"), 16)
            act.dma_start(rel[0:32, :], inp["rel_bias_2"]).then_inc(S("rel_landed"), 16)
            act.dma_start(oh[:], rel_onehot).then_inc(S("rel_landed"), 16)
            act.wait_ge(S("cols_made"), 1)

            split(0)
            split(1)
            norm("n1", x, lambda eng, k: wait_x(eng, "start", k), KD)
            act.wait_ge(S("vec_made"), 3)
            act.activation(small[:, 0:KD], cols("c_2"), ACT.Silu).then_inc(S("prep_a"), 1)
            act.wait_ge(S("spread_landed"), spread)
            for half in range(2):
                own = slice(64 * half, 64 * half + 64)
                act.activation(s5[own, 2, :], log_dt[own, half::2], ACT.Exp).then_inc(S("prep_a"), 1)
            act.wait_ge(S("prep_v"), 1)
            act.activation(small[:, 10:12], small[:, 8:10], ACT.Exp).then_inc(S("prep_a"), 1)
            act.wait_ge(S("prep_v"), 2)
            act.activation(s5[:, 3, :], s5[:, 15, :], ACT.Exp).then_inc(S("prep_a"), 1)
            act.wait_ge(S("prep_v"), 3)
            for angle, sine, cosine in ((s5[:, 4, :], s5[:, 6, :], s5[:, 7, :]), (ang[:, 0], sin_t[:], cos_t[:])):
                act.activation(sine, angle, ACT.Sin).then_inc(S("prep_a"), 1)
                done(act.activation(cosine, angle, ACT.Abs))
                act.activation(cosine, cosine, ACT.Sin, scale=-1.0, bias=half_pi_col).then_inc(S("prep_a"), 1)

            act.wait_ge(S("band_stored"), 16)
            swiglu("ffn1")
            down("ffn1")

            if "mixer" in stages:
                wait_x(act, "ffn1", KD - 1)
                act.dma_start(ws_in[:], inp["a_w_s"][0].rearrange("g t s -> t g s")).then_inc(S("ws_landed"), 16)
                for name, tile in (("a_ln_gain", ln_g), ("a_ln_bias", ln_b)):
                    act.dma_start(tile[:], inp[name][0].partition_broadcast(P)).then_inc(S("ln_landed"), 16)
                for half in range(2):
                    act.dma_start(bs[64 * half:64 * half + 64], inp["a_b_s"][0].rearrange("(f two) t -> two f t", two=2)[half]
                                  .partition_broadcast(64)).then_inc(S("bs_landed"), 16)
                norm("nm", x, lambda eng, k: wait_x(eng, "ffn1", k), KD)

                def tokens(name, evacuate):
                    n = PART[name][0]
                    split(n + 2)
                    for b in range(TB):
                        if b == TB - 1:
                            split(n + 3)
                        act.wait_ge(S("pe_done"), used(n + 1, b + 1))
                        evacuate(b)

                def features(name, evacuate):
                    n, panels, _ = PART[name]
                    for i in range(panels):
                        for t in range(2):
                            if t == 1:
                                split(n + i + 2)
                            act.wait_ge(S("pe_done"), used(n + i, 2 * t + 2))
                            evacuate(2 * i + t)

                tokens("v_gm", lambda b: act.activation(vg[:, b, :], B[b][:], ACT.Gelu).then_inc(S("v_gm_out"), 1))
                features("u_gm", lambda t: act.activation(u_g[:, t, :], bank_of(t)[:], ACT.Gelu).then_inc(S("u_gm_out"), 1))
                act.wait_ge(S("ln_var"), 1)
                act.activation(stat[:, 40:44], stat[:, 36:40], ACT.Sqrt, bias=ln_eps_col).then_inc(S("ln_root"), 1)

                def turned(j):
                    dst = (qT, kT)[j // 2]
                    for f in range(4):
                        act.wait_ge(S("qk_t"), 4 * j + f + 1)
                        act.copy(dst[:, 4 * (j % 2) + f, :], B[4 + f % 2][:]).then_inc(S("qk_t_out"), 1)

                for j in range(4):
                    raw = qk_raw[j % 2]
                    if j >= 2:
                        act.wait_ge(S("qk_t"), 4 * (j - 1))
                    tokens(f"qk{j}", lambda b: act.copy(raw[:, b, :], B[b][:]).then_inc(S(f"qk{j}_out"), 1))
                    act.wait_ge(S(f"qk{j}_out"), TB)
                    if j:
                        act.wait_ge(S("qk_done"), j)
                    act.activation(tmp[:, 0:4, :], raw[:], ACT.Square).then_inc(S("qk_sq"), 1)
                    act.wait_ge(S("qk_ssq"), j + 1)
                    act.activation(stat[:, 0:32], stat[:, 0:32], ACT.Sqrt, scale=1.0 / QK, bias=eps_col).then_inc(S("qk_root"), 1)
                    if j == 1:
                        for f in range(2):
                            act.wait_ge(S("ws_t"), f + 1)
                            act.copy(wsT[:, 4 * f:4 * f + 4, :], B[6 + f][:].rearrange("p (g t) -> p g t", g=4)).then_inc(S("ws_t_out"), 1)
                        for f in range(4):
                            act.wait_ge(S("ya_h"), 2 * f + 2)
                            act.copy(ya_hi[:, f, :], tmp[:, 4 + f % 2, :]).then_inc(S("ya_hi_out"), 1)
                    if j:
                        turned(j - 1)
                for g in range(2):
                    if g == 0:
                        act.wait_ge(S("ya_h"), 8)
                    tokens(f"v{g}", lambda b: act.copy(vtok[:, b, g * T:(g + 1) * T], B[b][:]).then_inc(S(f"v{g}_out"), 1))
                    if g == 0:
                        turned(3)
                features("g_a", lambda t: act.activation(ga[:, t, :], bank_of(t)[:], ACT.Sigmoid).then_inc(S("g_a_out"), 1))
                for i in range(2):
                    split(PART["a_proj"][0] + i + 2)
                features("g_b", lambda t: act.activation(gb[:, t, :], bank_of(t)[:], ACT.Sigmoid).then_inc(S("g_b_out"), 1))

                def soft(u):
                    h, i = UNITS[u]
                    keys = (i + 1) * P
                    s = u % 2
                    for m in range(2):
                        bank = 2 * (u % 3) + m
                        act.wait_ge(S("at_max"), 2 * u + m + 1)
                        if u >= 2:
                            act.wait_ge(S("at_a"), 2 * (u - 1))
                        act.activation(tmp[:, 2 * s + m, :keys], B[bank][:, :keys], ACT.Exp, bias=stat[:, bank:bank + 1],
                                       accum_out=stat[:, 6 + 2 * s + m:7 + 2 * s + m]).then_inc(S("at_exp"), 1)

                def a_turned(u):
                    keys = (UNITS[u][1] + 1) * P
                    act.wait_ge(S("at_t"), u + 1)
                    if u >= 2:
                        act.wait_ge(S("at_pv"), u - 1)
                    act.copy(aT[:, u % 2, :keys], B[6][:, :keys]).then_inc(S("at_t_out"), 1)

                def o_out(u):
                    h, i = UNITS[u]
                    act.wait_ge(S("at_pv"), u + 1)
                    done(act.copy(o_tok[:, i, h * P:(h + 1) * P], B[7][:, 0:P]))
                    act.activation(rstd[:, 0:P], o_tok[:, i, h * P:(h + 1) * P], ACT.Square,
                                   accum_out=stat[:, 16 + i * HEADS + h:17 + i * HEADS + h]).then_inc(S("at_o"), 1)

                soft(0)
                for u in range(len(UNITS)):
                    if u + 1 < len(UNITS):
                        soft(u + 1)
                    a_turned(u)
                    if u:
                        o_out(u - 1)
                o_out(len(UNITS) - 1)
                act.wait_ge(S("at_o"), len(UNITS))
                act.activation(stat[:, 16:48], stat[:, 16:48], ACT.Sqrt, scale=1.0 / P, bias=eps_col).then_inc(S("at_root"), 1)
                for h in range(HEADS):
                    act.wait_ge(S("yb_h"), h + 1)
                    act.copy(yb_hi[:, h, :], tmp[:, h % 4, :]).then_inc(S("yb_hi_out"), 1)

                def parts(name, evacuate=None):
                    n, panels, outs = PART[name]
                    for i in range(panels):
                        split(n + i + 2)
                        if evacuate:
                            for t in range(outs // panels):
                                evacuate(i * outs // panels + t)

                def m_hi_out(t):
                    act.wait_ge(S("m_h"), t + 1)
                    act.copy(m_hi[:, t, :], tmp[:, t % 4, :]).then_inc(S("m_hi_out"), 1)

                parts("b_proj", m_hi_out)
                parts("w_out")

            if "ffn2" in stages:
                norm("n2", x, lambda eng, k: wait_x(eng, "mixer", k), KD)
                swiglu("ffn2")

                down("ffn2")

            if "mix2" in stages:
                s5_b = [inp[f"ssm_b_{part}_2"].rearrange("o (s two) n h -> (two n) (o s) h", two=2) for part in ("re", "im")]
                wait_x(act, "ffn2", KD - 1)
                for i in range(2):
                    act.dma_start(b_in[:, i], s5_b[i]).then_inc(S("s5_landed"), 16)
                    c_v = inp[f"ssm_c_{('re', 'im')[i]}_2"].rearrange("o (c g) h n -> (g h) (o c) n", c=4)
                    for twice in range(2):
                        act.dma_start(c_in[:, i, :, twice, :], c_v).then_inc(S("s5_landed"), 16)
                act.wait_ge(S("band_stored"), 16)
                act.dma_start(hank[:], bass.AP(band_dram, 0, [[1, P], [BAND, NQ], [1, 2 * P]])).then_inc(S("hank_landed"), 16)
                act.wait_ge(S("mod_made"), 2)
                norm("p1", x, lambda eng, k: wait_x(eng, "ffn2", k), KD, shift=lambda k: mod[:, k:k + 1])
                n = PART["u2"][0]
                for i in range(2):
                    for t in range(2):
                        if t == 1:
                            split(n + i + 2)
                        act.wait_ge(S("pe_done"), used(n + i, 2 * t + 2))
                        act.copy(u2[:, 2 * i + t, :], bank_of(2 * i + t)[:]).then_inc(S("u2_out"), 1)
                for g in range(4):
                    act.wait_ge(S("bias_flipped"), g + 1)
                    act.copy(bias[:, 2 * g:2 * g + 2, :], B[4 + g][:].rearrange("p (h k) -> p h k", h=2)).then_inc(S("bias_out"), 1)
                for g in range(8):
                    act.wait_ge(S("bb_t"), g + 1)
                    act.copy(bbT[:, g // 4, 4 * (g % 4):4 * (g % 4) + 4, :],
                             B[4 + g % 2][:].rearrange("p (s c) -> p s c", s=4)).then_inc(S("bb_t_out"), 1)
                n = PART["q2"][0]
                split(n + 2)
                for b in range(TB):
                    if b == TB - 1:
                        split(n + 3)
                    act.wait_ge(S("pe_done"), used(n + 1, b + 1))
                    act.copy(q2_raw[:, b, :], B[b][:]).then_inc(S("q2_out"), 1)
                act.wait_ge(S("q2_out"), TB)
                act.activation(q_sq[:], q2_raw[:], ACT.Square).then_inc(S("qk2_sq"), 1)
                n = PART["kv2"][0]
                for b in range(TB):
                    act.wait_ge(S("pe_done"), used(n, b + 1))
                    act.copy(k2_raw[:, b, :], B[b][:, 0:NKV * QK]).then_inc(S("k2_out"), 1)
                    for twice in range(2):
                        act.copy(v2[:, b, :, twice, :], B[b][:, NKV * QK:2 * NKV * QK].rearrange("p (n d) -> p n d", n=NKV)).then_inc(S("v2_out"), 1)
                act.wait_ge(S("k2_out"), TB)
                act.activation(k_sq[:], k2_raw[:], ACT.Square).then_inc(S("qk2_sq"), 1)
                split(n + 2)
                act.wait_ge(S("qk2_ssq"), 2)
                act.activation(stat[:, 0:40], stat[:, 0:40], ACT.Sqrt, scale=1.0 / QK, bias=eps_col).then_inc(S("qk2_root"), 1)
                for f in range(6):
                    act.wait_ge(S("qk2_t"), f + 1)
                    dst = q2T[:, f, :] if f < 4 else k2T[:, f - 4, :]
                    act.copy(dst, B[4 + f % 2][:]).then_inc(S("qk2_t_out"), 1)
                def sw_exp(u):
                    b, n = SW_UNITS[u]
                    lo = P if b == 0 else 0
                    act.wait_ge(S("sw_max"), u + 1)
                    for h in range(4):
                        p = prob[:, u % 2, h, lo:]
                        act.activation(p, p, ACT.Exp, bias=sw_cols(48, u)[:, h:h + 1], accum_out=sw_cols(56, u)[:, h:h + 1]).then_inc(S("sw_exp"), 1)
                    act.activation(sw_cols(64, u), sw_cols(64, u), ACT.Exp).then_inc(S("sw_exp"), 1)

                def sw_turned(u):
                    if u >= 2:
                        act.wait_ge(S("sw_pv"), u - 1)
                    for i, kb in enumerate(SW_BLOCKS[u]):
                        act.wait_ge(S("sw_t"), SW_BEFORE[u] + i + 1)
                        act.copy(pT[:, u % 2, kb, :], B[5 + kb][:]).then_inc(S("sw_t_out"), 1)

                def sw_out(u):
                    b, n = SW_UNITS[u]
                    act.wait_ge(S("sw_pv"), u + 1)
                    o = B[7][:].rearrange("p (j two q) -> p j two q", j=2, two=2)
                    for half in range(2):
                        rows_of = slice(64 * half, 64 * half + 64)
                        act.copy(yat[rows_of, 2 * n:2 * n + 2, b * P:(b + 1) * P], o[rows_of, :, half, :]).then_inc(S("sw_out"), 1)

                for u in range(len(SW_UNITS)):
                    sw_exp(u)
                    sw_turned(u)
                    sw_out(u)
                act.wait_ge(S("y_added"), NS)
                norm("pa", yat, lambda eng, k: eng.wait_ge(S("sw_out"), 2 * len(SW_UNITS)), 4, hi=h_hi[:, 4:8], width=T)
                for t in range(4):
                    act.wait_ge(S("s5_y"), t + 1)
                    act.activation(z[:, t, :], u2[:, t, :], ACT.Gelu_apprx_tanh).then_inc(S("z_out"), 1)
                for t in range(4):
                    act.wait_ge(S("z_out"), t + 1)
                    act.copy(z_hi[:, t, :], z[:, t, :]).then_inc(S("z_hi_out"), 1)
                n = PART["glu"][0]
                split(n + 2)
                for t in range(4):
                    act.wait_ge(S("pe_done"), used(n, t + 1))
                    act.activation(tmp[:, 4 + t % 2, :] if t < 2 else tmp[:, t, :], bank_of(t)[:], ACT.Sigmoid, bias=col("b_glu_2", t)).then_inc(S("glu_gate"), 1)
                norm("ps", z, lambda eng, k: eng.wait_ge(S("glu_out"), k + 1), 4, hi=h_hi[:, 0:4], width=T)
                n = PART["w_out2"][0]
                for i in range(4):
                    split(n + i + 2)

            if "ffn3" in stages:
                norm("p2", x, lambda eng, k: wait_x(eng, "mix2", k), KD, shift=lambda k: mod[:, 24 + k:25 + k])
                base = BASE["ffn3"]
                with act.Fori(0, GU_STEPS) as i:
                    for half in range(2):
                        split(i * 2 + (base + 2 + half), base + half)
                        for t in range(2):
                            act.wait_ge(S("pe_done"), i * 8 + (4 * base + 4 * half + 2 * t + 2))
                            act.wait_ge(S("hid"), i * 2 + (HID["ffn3"] + t + 1))
                            act.activation(tmp[:, 2 * half + t, :], B[2 * half + t][:], ACT.Identity,
                                           scale=col_at("conv_w_2:2", i * 2, KF * half + t),
                                           bias=col_at("conv_b_2", i * 2, KF * half + t)).then_inc(S("ffn3_own"), 1)
                    for t in range(2):
                        act.wait_ge(S("ffn3_conv"), i * 8 + (2 * t + 14))
                        act.activation(tmp[:, 2 + t, :], tmp[:, 2 + t, :], ACT.Silu).then_inc(S("silu"), 1)
                    for t in range(2):
                        act.wait_ge(S("hid"), i * 2 + (HID["ffn3"] + t + 3))
                        act.copy(hid_hi[:, bass.ds(i * 2 + t, 1), :], tmp[:, 4 + t:5 + t, :]).then_inc(S("hid_hi"), 1)
                down("ffn3")
            for b in range(TB):
                act.wait_ge(S("out_t"), 2 * b + 2)
                act.copy(x_in[:, b, T:D], B[4 + (2 * b + 1) % 4][:]).then_inc(S("out_turned1"), 1)

        @block.vector
        def _(dve):
            done = Steps(dve, S("dve_done"))

            def split(n, i=None):
                if i is None:
                    if n >= end:
                        return
                    i = n
                dve.wait_ge(S("w_hi_done"), n + 1)
                s = i % 2
                dve.tensor_tensor(w_lo[s][:], w_raw[s][:], w_hi[s][:].bitcast(F32), ALU.subtract).then_inc(S("w_split"), 1)

            def norm(name, tiles, count, gain, shift=None, hi=None, lo=None):
                hi, lo = (h_hi, h_lo) if hi is None else (hi, lo)
                at = NORM[name]
                dve.wait_ge(S("norm_root"), NORMS.index(name) + 1)
                done(dve.reciprocal(rstd[:], rstd[:]))
                for k in range(count + 1):
                    if k < count:
                        if k >= 4:
                            dve.wait_ge(S("norm_split"), at + k - 3)
                        dve.scalar_tensor_tensor(tmp[:, 2 + k % 4, :], tiles[:, k, :], gain(k), rstd[:],
                                                 ALU.mult, ALU.mult).then_inc(S("norm_h"), 1)
                    if k:
                        dve.wait_ge(S("norm_hi"), at + k)
                        h, hi_k = tmp[:, 2 + (k - 1) % 4, :], hi[:, k - 1, :].bitcast(F32)
                        if shift is None:
                            ins = dve.tensor_tensor(lo[:, k - 1, :], h, hi_k, ALU.subtract)
                        else:
                            ins = dve.scalar_tensor_tensor(lo[:, k - 1, :], h, shift(k - 1), hi_k, ALU.add, ALU.subtract)
                        ins.then_inc(S("norm_split"), 1)

            def hid_lo_of(name, i, t, slot):
                dve.wait_ge(S("hid_hi"), i * 2 + (HID[name] + t + 1))
                dve.tensor_tensor(hid_lo[:, bass.ds(i * 2 + t, 1), :], tmp[:, slot:slot + 1, :],
                                  hid_hi[:, bass.ds(i * 2 + t, 1), :].bitcast(F32), ALU.subtract).then_inc(S("hid_split"), 1)

            def turns(st):
                fh_c, fl_c = (s5[:, row, bass.ds(st, 1)] for row in (13, 14))
                r = rot_r[:]
                dve.wait_ge(S("rot_read"), st + 1)
                dve.tensor_scalar(rot_n[:], rot_t[:], fh_c, ROUND, ALU.mult, ALU.add).then_inc(S("rot_step"), 1)
                dve.tensor_scalar(r, rot_t[:], fh_c, None, ALU.mult).then_inc(S("rot_step"), 1)
                dve.wait_ge(S("rot_step"), st * 5 + 2)
                dve.scalar_tensor_tensor(r, rot_n[:], ROUND, r, ALU.subtract, ALU.subtract).then_inc(S("rot_step"), 1)
                dve.wait_ge(S("rot_step"), st * 5 + 3)
                dve.scalar_tensor_tensor(r, rot_t[:], fl_c, r, ALU.mult, ALU.subtract).then_inc(S("rot_step"), 1)
                dve.wait_ge(S("rot_step"), st * 5 + 4)
                dve.tensor_scalar(rot_n[:], r, 1.0, ROUND, ALU.mult, ALU.add).then_inc(S("rot_step"), 1)
                dve.wait_ge(S("rot_step"), st * 5 + 5)
                dve.scalar_tensor_tensor(r, rot_n[:], ROUND, r, ALU.subtract, ALU.subtract).then_inc(S("rot_turns"), 1)

            def modulation(g):
                dve.wait_ge(S("mod_acc_free"), g + 1)
                for k in range(KD):
                    dve.wait_ge(S(f"mod_landed{k % MOD_SLOTS}"), g * 32 + (k // MOD_SLOTS + 1) * 16)
                    if k == 0:
                        ins = dve.tensor_scalar(mod_acc[:], mod_raw[:, k % MOD_SLOTS, :], small[:, k:k + 1], None, ALU.mult)
                    else:
                        dve.wait_ge(S("mod_step"), g * KD + (k + MOD_SLOTS))
                        ins = dve.scalar_tensor_tensor(mod_acc[:], mod_raw[:, k % MOD_SLOTS, :], small[:, k:k + 1], mod_acc[:], ALU.mult, ALU.add)
                    ins.then_inc(S("mod_step"), 1)

            def swiglu(name):
                base = BASE[name]
                dve.wait_ge(S("rot_t_made"), 1 + list(PHASES).index(name))
                for start, stop, mods, rots in PHASES[name]:
                    if not rots:
                        groups = sum(b - a for f in list(PHASES)[:list(PHASES).index(name) + 1] for a, b, m, _ in PHASES[f] if m)
                        dve.wait_ge(S("mod_acc_free"), groups + 1)
                    with dve.Fori(start, stop) as i:
                        if rots:
                            turns(i + BESIDE_AT[name])
                        if mods:
                            modulation(i + BESIDE_AT[name])
                        split(i * 2 + (base + 2), base)
                        for t in range(2):
                            dve.wait_ge(S("pe_done"), i * 8 + (4 * base + 4 + 2 * t + 2))
                            dve.wait_ge(S("silu"), i * 2 + (HID[name] + t + 3))
                            dve.wait_ge(S("hid_split"), i * 2 + (HID[name] + t + 1))
                            dve.tensor_tensor(tmp[:, 2 + t, :], tmp[:, t, :], B[2 + t][:], ALU.mult).then_inc(S("hid"), 1)
                        split(i * 2 + (base + 3), base + 1)
                        for t in range(2):
                            hid_lo_of(name, i, t, 2 + t)
                first = 4 * BESIDE_AT[name]
                last_col = 4 * groups
                dve.tensor_tensor(mod[:, first:last_col], B[6][:, 0:last_col - first], cols("b_mod_2")[:, first:last_col],
                                  ALU.add).then_inc(S("mod_made"), 1)

            def down(name, factor):
                base = BASE[name] + 2 * GU_STEPS
                steps = 1 if base + DOWN_PANELS == end else 2

                def body(j):
                    for c in range(8):
                        if c % 4 == 3:
                            for t in range(2):
                                dve.wait_ge(S("pe_done"), j * 32 + (4 * (base + c) + 2 * t + 2))
                                x_t = x[:, bass.ds(j * 4 + (c // 4 * 2 + t), 1), :]
                                dve.scalar_tensor_tensor(x_t, B[c // 4 * 2 + t][:].unsqueeze(1), factor(j, c // 4 * 2 + t), x_t,
                                                         ALU.mult, ALU.add).then_inc(S(name + "_x"), 1)
                        if isinstance(j, int):
                            split(base + 8 * j + c + 2)
                        else:
                            split(j * 8 + (base + c + 2), base + c)

                with dve.Fori(0, steps) as j:
                    body(j)
                if steps == 1:
                    body(1)

            dve.sem_inc(S("hid"), 2)
            dve.sem_inc(S("hid_split"), 2)
            for name in ("ffn1", "ffn2", "ffn3"):
                dve.sem_inc(S(name + "_x"), 4)
            dve.sem_inc(S("ffn3_conv"), 8)
            dve.sem_inc(S("mod_step"), MOD_SLOTS)
            for i, value in ((20, EPS), (21, math.pi / 2.0)):
                done(dve.memset(small[:, i:i + 1], value))
            dve.memset(small[:, 22:23], LN_EPS).then_inc(S("cols_made"), 1)
            dve.wait_ge(S("rows_t"), 3)
            for tile in range(3):
                dve.tensor_copy(vec[:, tile, :ROW_COUNTS[tile]], B[0][:, tile * P:tile * P + ROW_COUNTS[tile]]).then_inc(S("vec_made"), 1)
            for k in range(KD):
                dve.wait_ge(S("x_t"), k + 1)
                dve.tensor_copy(x[:, k, :], B[4 + k % 4][:]).then_inc(S("x_turned"), 1)
            split(0)
            split(1)
            dve.wait_ge(S("vec_made"), 3)
            norm("n1", x, KD, lambda k: col("ffn1_norm", k))
            dve.wait_ge(S("band_t"), 1)
            dve.tensor_copy(band[:], B[1][0:NQ, 0:BAND]).then_inc(S("band_made"), 1)

            dve.wait_ge(S("spread_landed"), 16 * 11)
            for i in range(2):
                done(dve.tensor_tensor(lam_in[:, 2 * i, :], lam_in[:, 2 * i, :], lam_in[:, 2 * i + 1, :], ALU.mult))
                ins = dve.tensor_reduce(small[:, 8 + i:9 + i], lam_in[:, 2 * i, :], AX.X, ALU.add)
                if i == 0:
                    done(ins)
            ins.then_inc(S("prep_v"), 1)
            for i in (0, 2):
                done(dve.tensor_scalar(gains[:, i, :], gains[:, i, :], QK**-0.5, None, ALU.mult))
            lr, dt, mag, th, n_, sn, cs, fh, fl, tv, t2, a_re, a_im, f_re, f_im = (
                s5[:, i, :] for i in (0, 2, 3, 4, 5, 6, 7, 13, 14, 15, 16, 8, 9, 11, 12))
            li = cols("lam_im_2")
            done(dve.tensor_scalar(lr, cols("lam_re_2"), -1e-4, None, ALU.min))
            dve.wait_ge(S("prep_a"), 3)
            done(dve.tensor_tensor(th, dt, li, ALU.mult))
            dve.tensor_tensor(tv, dt, lr, ALU.mult).then_inc(S("prep_v"), 1)

            def reduce_angle(a, n):
                done(dve.tensor_scalar(n, a, 1.0 / TWO_PI, ROUND, ALU.mult, ALU.add))
                done(dve.tensor_scalar(n, n, ROUND, None, ALU.subtract))
                for part in (PI_1, PI_2, PI_3):
                    done(dve.scalar_tensor_tensor(a, n, -part, a, ALU.mult, ALU.add))

            reduce_angle(th, n_)
            done(dve.tensor_scalar(fh, th, 2.0**15 / TWO_PI, ROUND, ALU.mult, ALU.add))
            done(dve.tensor_scalar(fh, fh, ROUND, 2.0**-15, ALU.subtract, ALU.mult))
            done(dve.tensor_copy(fl, th))
            for part in (PI_1, PI_2, PI_3):
                done(dve.scalar_tensor_tensor(fl, fh, -part, fl, ALU.mult, ALU.add))
            done(dve.tensor_scalar(fl, fl, 1.0 / TWO_PI, None, ALU.mult))
            done(dve.tensor_scalar(th, th, PI_LOW, -PI_LOW, ALU.min, ALU.max))
            posf = stat[:, 0:TB]
            done(dve.tensor_copy(posf, pos_i[:]))
            for r in range(ROT):
                inv = float(np.float32(500000.0) ** np.float32(-np.float32(2 * r) / np.float32(2 * ROT)))
                done(dve.tensor_scalar(ang[:, 0, :, r], posf, inv, None, ALU.mult))
            reduce_angle(ang[:, 0], ang[:, 1])
            dve.tensor_scalar(ang[:, 0], ang[:, 0], PI_LOW, -PI_LOW, ALU.min, ALU.max).then_inc(S("prep_v"), 1)
            neg_lam = small[:, 12:13]
            dve.wait_ge(S("prep_a"), 9)
            done(dve.tensor_tensor(neg_lam, small[:, 11:12], small[:, 10:11], ALU.subtract))
            done(dve.tensor_scalar(neg_lam, neg_lam, -LAM_INIT, None, ALU.add))
            done(dve.tensor_tensor(a_re, mag, cs, ALU.mult))
            done(dve.tensor_tensor(a_im, mag, sn, ALU.mult))
            done(dve.tensor_scalar(a_re, a_re, -1.0, None, ALU.add))
            done(dve.tensor_tensor(tv, lr, lr, ALU.mult))
            done(dve.tensor_tensor(t2, li, li, ALU.mult))
            done(dve.tensor_tensor(tv, tv, t2, ALU.add))
            done(dve.reciprocal(tv, tv))
            done(dve.tensor_tensor(f_re, a_re, lr, ALU.mult))
            done(dve.tensor_tensor(t2, a_im, li, ALU.mult))
            done(dve.tensor_tensor(f_re, f_re, t2, ALU.add))
            done(dve.tensor_tensor(f_re, f_re, tv, ALU.mult))
            done(dve.tensor_tensor(f_im, a_im, lr, ALU.mult))
            done(dve.tensor_tensor(t2, a_re, li, ALU.mult))
            done(dve.tensor_tensor(f_im, f_im, t2, ALU.subtract))
            done(dve.tensor_tensor(f_im, f_im, tv, ALU.mult))

            swiglu("ffn1")

            down("ffn1", lambda j, t: 0.5)

            if "mixer" in stages:
                norm("nm", x, KD, lambda k: col("mix_norm", k))

                def part_splits(name):
                    n, panels, _ = PART[name]
                    for i in range(panels):
                        split(n + i + 2)

                def spread(ap, shape):
                    return ap.unsqueeze(2).to_broadcast(shape)

                part_splits("v_gm")
                dve.wait_ge(S("v_gm_out"), TB)
                for b in range(TB):
                    done(dve.bn_stats(tmp[:, 4, 6 * b:6 * b + 6], vg[:, b, :]))
                    done(dve.bn_aggr(tmp[:, 5, 2 * b:2 * b + 2], tmp[:, 4, 6 * b:6 * b + 6]))
                dve.tensor_copy(stat[:, 36:40], tmp[:, 5, 1:2 * TB:2]).then_inc(S("ln_var"), 1)
                part_splits("u_gm")
                dve.wait_ge(S("ln_root"), 1)
                done(dve.reciprocal(stat[:, 40:44], stat[:, 40:44]))
                dve.wait_ge(S("ln_landed"), 32)
                for b in range(TB):
                    done(dve.tensor_scalar(vg[:, b, :], vg[:, b, :], tmp[:, 5, 2 * b:2 * b + 1], stat[:, 40 + b:41 + b],
                                           ALU.subtract, ALU.mult))
                    done(dve.tensor_tensor(vg[:, b, :], vg[:, b, :], ln_g[:], ALU.mult))
                    dve.tensor_tensor(vg[:, b, :], vg[:, b, :], ln_b[:], ALU.add).then_inc(S("ln_out"), 1)

                def heads(j):
                    raw = qk_raw[j % 2][:].rearrange("p b (h d) -> p (b h) d", d=QK)
                    n = TB * HEADS
                    dve.wait_ge(S("qk_sq"), j + 1)
                    dve.tensor_reduce(stat[:, 0:n], tmp[:, 0:4, :].rearrange("p b (h d) -> p (b h) d", d=QK), AX.X, ALU.add).then_inc(S("qk_ssq"), 1)
                    dve.wait_ge(S("qk_root"), j + 1)
                    done(dve.reciprocal(stat[:, 0:n], stat[:, 0:n]))
                    done(dve.tensor_tensor(raw, raw, spread(stat[:, 0:n], [P, n, QK]), ALU.mult))
                    done(dve.tensor_tensor(raw, raw, gains[:, j // 2:j // 2 + 1, :].to_broadcast([P, n, QK]), ALU.mult))
                    raw4 = qk_raw[j % 2][:].rearrange("p b (h d) -> p b h d", d=QK)
                    r1, r2 = raw4[:, :, :, 0:ROT], raw4[:, :, :, ROT:2 * ROT]
                    shape = [P, TB, HEADS, ROT]
                    cos_b, sin_b = (a[:].unsqueeze(2).to_broadcast(shape) for a in (cos_t, sin_t))
                    t = [tmp[:, 0, 256 * (i % 2):256 * (i % 2) + 256] if i < 2 else tmp[:, 1, 256 * (i % 2):256 * (i % 2) + 256] for i in range(4)]
                    t = [a.rearrange("p (b h d) -> p b h d", b=TB, h=HEADS) for a in t]
                    dve.wait_ge(S("qk_ssq"), j + 1)
                    done(dve.tensor_tensor(t[0], r1, cos_b, ALU.mult))
                    done(dve.tensor_tensor(t[1], r2, sin_b, ALU.mult))
                    done(dve.tensor_tensor(t[2], r2, cos_b, ALU.mult))
                    done(dve.tensor_tensor(t[3], r1, sin_b, ALU.mult))
                    done(dve.tensor_tensor(r1, t[0], t[1], ALU.subtract))
                    dve.tensor_tensor(r2, t[2], t[3], ALU.add).then_inc(S("qk_done"), 1)

                def gmlp():
                    dve.wait_ge(S("bs_landed"), 32)
                    dve.wait_ge(S("u_gm_out"), 4)
                    for f in range(4):
                        y = tmp[:, 4 + f % 2, :]
                        dve.wait_ge(S("f_done"), f + 1)
                        dve.tensor_tensor(y.rearrange("p (c t) -> p c t", c=TB), B[6 + f % 2][:].rearrange("p (c t) -> p c t", c=TB),
                                          bs[:, f:f + 1, :].to_broadcast([P, TB, P]), ALU.add).then_inc(S("ya_h"), 1)
                        dve.wait_ge(S("ya_h"), 2 * f + 1)
                        dve.tensor_tensor(y, y, u_g[:, f, :], ALU.mult).then_inc(S("ya_h"), 1)
                        dve.wait_ge(S("ya_hi_out"), f + 1)
                        dve.tensor_tensor(ya_lo[:, f, :], y, ya_hi[:, f, :].bitcast(F32), ALU.subtract).then_inc(S("ya_split"), 1)

                for j in range(4):
                    part_splits(f"qk{j}")
                    heads(j)
                    if j == 1:
                        gmlp()
                part_splits("v0")
                part_splits("v1")
                part_splits("g_a")
                n = PART["a_proj"][0]
                for i in range(2):
                    for t in range(4):
                        dve.wait_ge(S("pe_done"), used(n + i, t + 1))
                        g = ga[:, 4 * i + t, :]
                        dve.wait_ge(S("g_a_out"), 4 * i + t + 1)
                        dve.tensor_tensor(g, g, bank_of(t)[:], ALU.mult).then_inc(S("a_proj_out"), 1)
                    split(n + i + 2)
                part_splits("g_b")

                def row_max(u):
                    keys = (UNITS[u][1] + 1) * P
                    for m in range(2):
                        bank = 2 * (u % 3) + m
                        dve.wait_ge(S("at_s"), 2 * u + m + 1)
                        dve.tensor_reduce(stat[:, bank:bank + 1], B[bank][:, :keys], AX.X, ALU.max,
                                          negate=True).then_inc(S("at_max"), 1)

                def differ(u):
                    keys = (UNITS[u][1] + 1) * P
                    s = u % 2
                    r = stat[:, 10 + 2 * s:12 + 2 * s]
                    dve.wait_ge(S("at_exp"), 2 * u + 2)
                    done(dve.reciprocal(r, stat[:, 6 + 2 * s:8 + 2 * s]))
                    done(dve.tensor_tensor(r[:, 1:2], r[:, 1:2], neg_lam, ALU.mult))
                    if u >= 2:
                        dve.wait_ge(S("at_t"), u - 1)
                    a = tmp[:, 4 + s, :keys]
                    dve.tensor_scalar(a, tmp[:, 2 * s, :keys], r[:, 0:1], None, ALU.mult).then_inc(S("at_a"), 1)
                    dve.wait_ge(S("at_a"), 2 * u + 1)
                    dve.scalar_tensor_tensor(a, tmp[:, 2 * s + 1, :keys], r[:, 1:2], a, ALU.mult, ALU.add).then_inc(S("at_a"), 1)

                row_max(0)
                row_max(1)
                for u in range(len(UNITS)):
                    differ(u)
                    if u + 2 < len(UNITS):
                        row_max(u + 2)
                dve.wait_ge(S("at_root"), 1)
                done(dve.reciprocal(stat[:, 16:48], stat[:, 16:48]))
                for i in range(TB):
                    o = o_tok[:, i, :].rearrange("p (h d) -> p h d", h=HEADS)
                    dve.tensor_tensor(o, o, spread(stat[:, 16 + i * HEADS:16 + (i + 1) * HEADS], [P, HEADS, P]), ALU.mult).then_inc(S("o_scaled"), 1)
                dve.wait_ge(S("yb_t"), HEADS)
                for h in range(HEADS + 1):
                    if h < HEADS:
                        if h >= 4:
                            dve.wait_ge(S("yb_split"), h - 3)
                        dve.tensor_scalar(tmp[:, h % 4, :], B[h][:], col("b_subln", 0), 1.0 - LAM_INIT, ALU.mult, ALU.mult).then_inc(S("yb_h"), 1)
                    if h:
                        dve.wait_ge(S("yb_hi_out"), h)
                        dve.tensor_tensor(yb_lo[:, h - 1, :], tmp[:, (h - 1) % 4, :], yb_hi[:, h - 1, :].bitcast(F32), ALU.subtract).then_inc(S("yb_split"), 1)
                n, panels, _ = PART["b_proj"]
                for i in range(panels):
                    for t in range(2 * i, 2 * i + 2):
                        y = tmp[:, t % 4, :]
                        dve.wait_ge(S("pe_done"), used(n + i, 2 * (t % 2) + 2))
                        if t >= 4:
                            dve.wait_ge(S("m_split"), t - 3)
                        dve.tensor_tensor(y, gb[:, t, :], bank_of(t)[:], ALU.mult).then_inc(S("b_proj_out"), 1)
                        dve.wait_ge(S("b_proj_out"), t + 1)
                        dve.tensor_tensor(y, y, ga[:, t, :], ALU.add).then_inc(S("m_h"), 1)
                    split(n + i + 2)
                    for t in range(2 * i, 2 * i + 2):
                        dve.wait_ge(S("m_hi_out"), t + 1)
                        dve.tensor_tensor(m_lo[:, t, :], tmp[:, t % 4, :], m_hi[:, t, :].bitcast(F32), ALU.subtract).then_inc(S("m_split"), 1)
                n, panels, _ = PART["w_out"]
                for i in range(panels):
                    for t in range(2 * i, 2 * i + 2):
                        dve.wait_ge(S("pe_done"), used(n + i, 2 * (t % 2) + 2))
                        dve.tensor_tensor(x[:, t, :], x[:, t, :], bank_of(t)[:], ALU.add).then_inc(S("mixer_x"), 1)
                    split(n + i + 2)

            if "ffn2" in stages:
                norm("n2", x, KD, lambda k: col("ffn2_norm", k))
                swiglu("ffn2")

                down("ffn2", lambda j, t: 0.5)

            if "mix2" in stages:
                dve.wait_ge(S("mod_made"), 2)
                for i, name in enumerate(("norm1_w_2", "norm2_w_2")):
                    at = 8 + 24 * i
                    done(dve.scalar_tensor_tensor(gain2[:, i, :], mod[:, at:at + 8], 1.0, cols(name), ALU.add, ALU.mult))
                norm("p1", x, KD, lambda k: gain2[:, 0, k:k + 1], lambda k: mod[:, k:k + 1])
                n, panels, _ = PART["u2"]
                for i in range(panels):
                    split(n + i + 2)
                dve.wait_ge(S("s5_landed"), 96)
                shape = [P, NS, SG]
                f_re_b, f_im_b = (s5[:, row, :].unsqueeze(2).to_broadcast(shape) for row in (11, 12))
                t = [tmp[:, 4, 256 * i:256 * i + 256].rearrange("p (s h) -> p s h", s=NS) for i in range(2)]
                for part, (first, second, op) in enumerate(((0, 1, ALU.subtract), (1, 0, ALU.add))):
                    done(dve.tensor_tensor(t[0], b_in[:, first], f_re_b, ALU.mult))
                    done(dve.tensor_tensor(t[1], b_in[:, second], f_im_b, ALU.mult))
                    done(dve.tensor_tensor(bb[:, part], t[0], t[1], op))
                for part in range(2):
                    if part:
                        dve.wait_ge(S("bb_t"), 4)
                    done(dve.memset(bd[:], 0.0))
                    for s4 in range(4):
                        for half in range(2):
                            own = slice(64 * half, 64 * half + 64)
                            at = s4 * 2 * SG + half * SG
                            dve.tensor_copy(bd[own, s4::4, at:at + SG], bb[own, part, s4::4, :]).then_inc(S("bd_made"), 1)
                done(dve.memset(cT[:], 0.0))
                for part, sign in enumerate((1.0, -1.0)):
                    dve.wait_ge(S("c_t"), part + 1)
                    c_v = B[6 + part][:].rearrange("p (c n) -> p c n", c=4)
                    for s4 in range(4):
                        for half in range(2):
                            own = slice(64 * half, 64 * half + 64)
                            at = s4 * 2 * SG + half * SG
                            dve.tensor_scalar(cT[own, part, s4::4, at:at + SG], c_v[own, :, at:at + SG], sign, None, ALU.mult).then_inc(S("c_out"), 1)
                n = PART["q2"][0]
                split(n + 2)
                split(n + 3)
                dve.wait_ge(S("qk2_sq"), 1)
                dve.tensor_reduce(stat[:, 0:32], q_sq[:].rearrange("p b (h d) -> p (b h) d", d=QK), AX.X, ALU.add).then_inc(S("qk2_ssq"), 1)
                dve.wait_ge(S("qk2_sq"), 2)
                dve.tensor_reduce(stat[:, 32:40], k_sq[:].rearrange("p b (h d) -> p (b h) d", d=QK), AX.X, ALU.add).then_inc(S("qk2_ssq"), 1)
                split(PART["kv2"][0] + 2)
                dve.wait_ge(S("qk2_root"), 1)
                done(dve.reciprocal(stat[:, 0:40], stat[:, 0:40]))
                q_v = q2_raw[:].rearrange("p b (h d) -> p (b h) d", d=QK)
                k_v = k2_raw[:].rearrange("p b (h d) -> p (b h) d", d=QK)
                done(dve.tensor_tensor(q_v, q_v, spread(stat[:, 0:32], [P, 32, QK]), ALU.mult))
                dve.tensor_tensor(q_v, q_v, gains[:, 2:3, :].to_broadcast([P, 32, QK]), ALU.mult).then_inc(S("qk2_made"), 1)
                done(dve.tensor_tensor(k_v, k_v, spread(stat[:, 32:40], [P, 8, QK]), ALU.mult))
                for twice in range(2):
                    dve.tensor_tensor(k2_dup[:, :, :, twice, :].rearrange("p b n d -> p (b n) d"), k_v,
                                      gains[:, 3:4, :].to_broadcast([P, 8, QK]), ALU.mult).then_inc(S("qk2_made"), 1)
                def sw_max(u):
                    b, n = SW_UNITS[u]
                    lo = P if b == 0 else 0
                    p = prob[:, u % 2]
                    if u == 0:
                        dve.wait_ge(S("bias_out"), 4)
                    if u >= 2:
                        dve.wait_ge(S("sw_t"), SW_BEFORE[u - 1])
                    for odd in range(2):
                        first = 4 * n + odd
                        dve.wait_ge(S("sw_s"), 2 * u + odd + 1)
                        dve.tensor_tensor(p[:, odd:odd + 3:2, lo:], B[5 + odd][:].rearrange("p (h k) -> p h k", h=2)[:, :, lo:],
                                          bias[:, first:first + 3:2, lo:], ALU.add).then_inc(S("sw_read"), 1)
                    sinks = sink[:, 4 * n:4 * n + 4]
                    dve.wait_ge(S("sw_read"), 2 * u + 2)
                    done(dve.tensor_reduce(sw_cols(72, u), p[:, :, lo:], AX.X, ALU.max))
                    done(dve.tensor_tensor(sw_cols(72, u), sw_cols(72, u), sinks, ALU.max))
                    done(dve.tensor_tensor(sw_cols(64, u), sinks, sw_cols(72, u), ALU.subtract))
                    dve.tensor_scalar(sw_cols(48, u), sw_cols(72, u), -1.0, None, ALU.mult).then_inc(S("sw_max"), 1)

                def sw_scale(u):
                    lo = P if SW_UNITS[u][0] == 0 else 0
                    p = prob[:, u % 2, :, lo:]
                    dve.wait_ge(S("sw_exp"), 5 * (u + 1))
                    done(dve.tensor_tensor(sw_cols(80, u), sw_cols(56, u), sw_cols(64, u), ALU.add))
                    done(dve.reciprocal(sw_cols(80, u), sw_cols(80, u)))
                    dve.tensor_tensor(p, p, spread(sw_cols(80, u), [P, 4, 2 * P - lo]), ALU.mult).then_inc(S("sw_p"), 1)

                def scan_in(st):
                    re, im = B[2 * (st % 2)], B[2 * (st % 2) + 1]
                    r = rot[:, st % ROT_SLOTS]
                    dve.wait_ge(S("bu"), 2 * st + 2)
                    dve.wait_ge(S(f"rot_landed{st % ROT_SLOTS}"), 16 * (st // ROT_SLOTS + 1))
                    if st:
                        dve.wait_ge(S("scan_v"), 2 * st)
                    for i, (a, w) in enumerate(((re, 0), (im, 1), (im, 0), (re, 1))):
                        dve.tensor_tensor(sc_a[:, i, :], a[:], r[:, w, :], ALU.mult).then_inc(S("scan_in"), 1)

                def scan(st):
                    if st:
                        dve.wait_ge(S("scan_p"), 2 * st)
                        dve.wait_ge(S("scan_q"), 2 * st)
                    for i in range(2):
                        dve.wait_ge(S("scan_v"), 2 * st + i + 1)
                        dve.tensor_tensor_scan(sc_v[:, 2 + i, :], s5[:, 3, st:st + 1].to_broadcast([P, T]), sc_v[:, i, :], 0.0,
                                               ALU.mult, ALU.add).then_inc(S("scanned"), 1)

                def scan_out(st):
                    dve.wait_ge(S("scanned"), 2 * st + 2)
                    if st >= 2:
                        dve.wait_ge(S("y_added"), st - 1)
                    r = rot[:, st % ROT_SLOTS]
                    dve.scalar_tensor_tensor(scan_product(st, 2), sc_v[:, 3, :], -1.0, r[:, 1, :], ALU.mult, ALU.mult).then_inc(S("scan_q"), 1)
                    dve.tensor_tensor(scan_product(st, 3), sc_v[:, 3, :], r[:, 0, :], ALU.mult).then_inc(S("scan_q"), 1)

                def s5_y(c):
                    dve.wait_ge(S("y_added"), 4 * c + 4)
                    dve.scalar_tensor_tensor(u2[:, c, :], u2[:, c, :], col("ssm_d_2", c), B[4][:], ALU.mult, ALU.add).then_inc(S("s5_y"), 1)

                scan_in(0)
                for st in range(NS):
                    if st % 4 == 1 and st > 4:
                        s5_y(st // 4 - 1)
                    if st + 1 < NS:
                        scan_in(st + 1)
                    scan(st)
                    if st % 2:
                        sw_scale(st // 2)
                    scan_out(st)
                    if st % 2 == 0:
                        sw_max(st // 2)
                s5_y(3)
                norm("pa", yat, 4, lambda k: col("out_norm_attn_2", k), hi=h_hi[:, 4:8], lo=h_lo[:, 4:8])
                for t in range(4):
                    dve.wait_ge(S("z_hi_out"), t + 1)
                    dve.tensor_tensor(z_lo[:, t, :], z[:, t, :], z_hi[:, t, :].bitcast(F32), ALU.subtract).then_inc(S("z_split"), 1)
                split(PART["glu"][0] + 2)
                for t in range(4):
                    dve.wait_ge(S("glu_gate"), t + 1)
                    dve.wait_ge(S("z_split"), t + 1)
                    dve.tensor_tensor(z[:, t, :], z[:, t, :], tmp[:, 4 + t % 2, :] if t < 2 else tmp[:, t, :], ALU.mult).then_inc(S("glu_out"), 1)
                norm("ps", z, 4, lambda k: col("out_norm_ssm_2", k), hi=h_hi[:, 0:4], lo=h_lo[:, 0:4])
                n, panels, _ = PART["w_out2"]
                for i in range(panels):
                    for t in range(2 * i, 2 * i + 2):
                        dve.wait_ge(S("pe_done"), used(n + i, 2 * (t % 2) + 2))
                        dve.scalar_tensor_tensor(x[:, t, :], bank_of(t)[:], mod[:, 16 + t:17 + t], x[:, t, :],
                                                 ALU.mult, ALU.add).then_inc(S("mix2_x"), 1)
                    split(n + i + 2)

            if "ffn3" in stages:
                norm("p2", x, KD, lambda k: gain2[:, 1, k:k + 1], lambda k: mod[:, 24 + k:25 + k])
                base = BASE["ffn3"]
                with dve.Fori(0, GU_STEPS) as i:
                    for half in range(2):
                        split(i * 2 + (base + 2 + half), base + half)
                        for t in range(2):
                            up, y = B[2 * half + t], tmp[:, 2 * half + t, :]
                            dve.wait_ge(S("ffn3_own"), i * 4 + (2 * half + t + 1))
                            for back in (1, 2):
                                dve.scalar_tensor_tensor(y[:, back:], up[:, :T - back], col_at(f"conv_w_2:{2 - back}", i * 2, KF * half + t),
                                                         y[:, back:], ALU.mult, ALU.add).then_inc(S("ffn3_conv"), 1)
                                if back == 1:
                                    dve.wait_ge(S("ffn3_conv"), i * 8 + (4 * half + 2 * t + 9))
                    for t in range(2):
                        dve.wait_ge(S("silu"), i * 2 + (HID["ffn3"] + t + 3))
                        dve.wait_ge(S("hid_split"), i * 2 + (HID["ffn3"] + t + 1))
                        dve.tensor_tensor(tmp[:, 4 + t, :], tmp[:, 2 + t, :], tmp[:, t, :], ALU.mult).then_inc(S("hid"), 1)
                    for t in range(2):
                        hid_lo_of("ffn3", i, t, 4 + t)
                down("ffn3", lambda j, t: mod[:, bass.ds(j * 4 + (40 + t), 1)])
            for b in range(TB):
                dve.wait_ge(S("out_t"), 2 * b + 1)
                dve.tensor_copy(x_in[:, b, 0:T], B[4 + 2 * b % 4][:]).then_inc(S("out_turned0"), 1)

        @block.tensor
        def _(pe):
            def products(out_ap, terms, first=True, last=True):
                for i, (stationary, moving) in enumerate(terms):
                    mm = pe.matmul(out_ap, stationary, moving, start=first and i == 0, stop=last and i == len(terms) - 1)
                return mm

            def feature_terms(n, k, c, at, hi, lo, wait=None, k0=0):
                wh, wl = panel(w_hi, n, k, c), panel(w_lo, n, k, c)
                for i in range(k):
                    if wait:
                        wait(i)
                    yield wh[:, i, at:at + P], hi[:, k0 + i, :]
                    yield wh[:, i, at:at + P], lo[:, k0 + i, :]
                    yield wl[:, i, at:at + P], hi[:, k0 + i, :]

            def token_terms(n, k, c, b, hi, lo, wait=None, k0=0):
                wh, wl = panel(w_hi, n, k, c), panel(w_lo, n, k, c)
                own = slice(b * P, (b + 1) * P)
                for i in range(k):
                    if wait:
                        wait(i)
                    yield hi[:, k0 + i, own], wh[:, i, :]
                    yield hi[:, k0 + i, own], wl[:, i, :]
                    yield lo[:, k0 + i, own], wh[:, i, :]

            def stream(out_ap, terms, total, first=True, last=True):
                for i, (stationary, moving) in enumerate(terms):
                    mm = pe.matmul(out_ap, stationary, moving, start=first and i == 0, stop=last and i == total - 1)
                return mm

            def norm(name, count):
                for k in range(count):
                    pe.wait_ge(S("norm_sq"), NORM[name] + k + 1)
                    pe.matmul(B[7][:], ones[:], tmp[:, k % 2, :], start=k == 0, stop=k == count - 1).then_inc(S("norm_summed"), 1)

            def ready(name):
                return lambda k: pe.wait_ge(S("norm_split"), NORM[name] + k + 1)

            def gate_up(name, h_name, free):
                base = BASE[name]
                for start, stop, mods, _ in PHASES.get(name, ((0, GU_STEPS, False, False),)):
                    with pe.Fori(start, stop) as i:
                        for half in range(2):
                            pe.wait_ge(S("w_split"), i * 2 + (base + half + 1))
                            free(i, half)
                            for t in range(2):
                                terms = feature_terms(base + half, KD, PC, t * P, h_hi, h_lo, ready(h_name) if half == 0 and t == 0 else None)
                                stream(B[2 * half + t][:], terms, 3 * KD).then_inc(S("pe_done"), 2)
                        if mods:
                            pe.wait_ge(S("mod_step"), i * KD + (KD * (BESIDE_AT[name] + 1) + MOD_SLOTS))
                            for s4 in range(4):
                                mm = pe.matmul(B[6][:, bass.ds(i * 4 + s4, 1)], mod_acc[:, s4 * P:(s4 + 1) * P], ones[:, 0:1], start=True, stop=True)
                            mm.then_inc(S("mod_acc_free"), 1)

            def down(name):
                base = BASE[name] + 2 * GU_STEPS
                if name == "ffn3":
                    pe.wait_ge(S("ffn3_conv"), 8 * GU_STEPS + 8)
                else:
                    pe.wait_ge(S("silu"), HID[name] + KF + 2)
                with pe.Fori(0, 2) as j:
                    for c in range(8):
                        k0, kn = DOWN_K[c % 4]
                        pe.wait_ge(S("w_split"), j * 8 + (base + c + 1))
                        pe.wait_ge(S("hid_split"), HID[name] + k0 + kn + 2)
                        if c % 4 == 0:
                            pe.wait_ge(S(name + "_x"), j * 4 + (c // 4 * 2 + 2))
                        for t in range(2):
                            terms = feature_terms(base + c, kn, PC, t * P, hid_hi, hid_lo, None, k0)
                            mm = stream(B[c // 4 * 2 + t][:], terms, 3 * kn, c % 4 == 0, c % 4 == 3)
                            if c % 4 == 3:
                                mm.then_inc(S("pe_done"), 2)
                        if c % 4 < 3:
                            mm.then_inc(S("pe_done"), 4)

            pe.sem_inc(S("mod_acc_free"), 1)
            pe.wait_ge(S("pool_done"), 5)
            for k in range(KD):
                if k >= 4:
                    pe.wait_ge(S("x_turned"), k - 3)
                pe.wait_ge(S(f"x_landed{k // 4}"), 16)
                for b in range(TB):
                    mm = pe.transpose(B[4 + k % 4][:, b * P:(b + 1) * P], x_in[:, b, k * P:(k + 1) * P], ident[:])
                mm.then_inc(S("x_t"), 1)
                if k == 3:
                    pe.wait_ge(S("rows_landed"), 16 * len(ROWS))
                    for tile in range(3):
                        n = ROW_COUNTS[tile]
                        pe.transpose(B[0][:, tile * P:tile * P + n], rows[0:n, tile, :], ident[0:n, 0:n]).then_inc(S("rows_t"), 1)
                    pe.wait_ge(S("rel_landed"), 32)
                    pe.wait_ge(S("consts_made"), 1)
                    pe.matmul(B[1][0:NQ, 0:BAND], rel[:], oh[:], start=True, stop=True).then_inc(S("band_t"), 1)
            pe.wait_ge(S("x_turned"), KD)
            norm("n1", KD)
            pe.wait_ge(S("band_made"), 1)

            def silu_free(name):
                def free(i, half):
                    pe.wait_ge(S(("silu", "hid")[half]), i * 2 + (HID[name] + 2))
                return free

            gate_up("ffn1", "n1", silu_free("ffn1"))

            down("ffn1")
            if last == "ffn1":
                pe.wait_ge(S("mod_made"), 1)

            if "mixer" in stages:
                wait_x(pe, "ffn1", KD - 1)
                norm("nm", KD)

                def bank_wait(name, t, outs, before, before_outs):
                    if t >= 4:
                        pe.wait_ge(S(name), t - 3)
                    elif before:
                        pe.wait_ge(S(before), before_outs - 3 + t)

                def tokens(name, before, first=False):
                    n = PART[name][0]
                    for half in range(2):
                        pe.wait_ge(S("w_split"), n + half + 1)
                        for b in range(TB):
                            if half == 0 and before:
                                pe.wait_ge(S(before[0]), before[1] - 3 + b)
                            mm = stream(B[b][:], token_terms(n + half, 4, T, b, h_hi, h_lo,
                                                             (lambda i: pe.wait_ge(S("norm_split"), NORM["nm"] + 4 * half + i + 1)) if first and b == 0 else None, 4 * half),
                                        12, half == 0, half == 1)
                            if half:
                                mm.then_inc(S("pe_done"), 1)
                        if half == 0:
                            mm.then_inc(S("pe_done"), 4)

                def features(name, evac, before, hi, lo, wait=None):
                    n, panels, outs = PART[name]
                    for t in range(outs):
                        i, per = divmod(t, outs // panels)
                        if per == 0:
                            pe.wait_ge(S("w_split"), n + i + 1)
                        if t >= 4:
                            pe.wait_ge(S(evac), t - 3)
                        elif before:
                            pe.wait_ge(S(before[0]), before[1] - 3 + t)
                        k, c = (4, T) if outs // panels == 4 else (KD, PC)
                        stream(bank_of(t)[:], feature_terms(n + i, k, c, per * P, hi, lo, wait if t == 0 else None), 3 * k)\
                            .then_inc(S("pe_done"), 4 // (outs // panels))

                def turn(j):
                    pe.wait_ge(S("qk_done"), j + 1)
                    for f in range(4):
                        if 4 * j + f >= 2:
                            pe.wait_ge(S("qk_t_out"), 4 * j + f - 1)
                        for b in range(TB):
                            mm = pe.transpose(B[4 + f % 2][:, b * P:(b + 1) * P], qk_raw[j % 2][:, b, f * P:(f + 1) * P], ident[:])
                        mm.then_inc(S("qk_t"), 1)

                tokens("v_gm", None, True)
                features("u_gm", "u_gm_out", ("v_gm_out", 4), h_hi, h_lo)
                tokens("qk0", ("u_gm_out", 4))
                tokens("qk1", ("qk0_out", 4))
                pe.wait_ge(S("mod_made"), 1)
                pe.wait_ge(S("ws_masked"), 1)
                for f in range(2):
                    for g in range(4):
                        mm = pe.transpose(B[6 + f][:, g * P:(g + 1) * P], ws_in[:, 4 * f + g, :], ident[:])
                    mm.then_inc(S("ws_t"), 1)
                pe.wait_ge(S("ws_t_out"), 2)
                pe.wait_ge(S("ln_out"), TB)
                for f in range(4):
                    if f >= 2:
                        pe.wait_ge(S("ya_h"), 2 * (f - 1))
                    for half in range(2):
                        g = 2 * f + half
                        for c in range(TB):
                            mm = pe.matmul(B[6 + f % 2][64 * half:64 * half + 64, c * P:(c + 1) * P],
                                           vg[:, c, g * 64:(g + 1) * 64], wsT[:, g, :], start=True, stop=True)
                    mm.then_inc(S("f_done"), 1)
                turn(0)
                tokens("qk2", ("qk1_out", 4))
                turn(1)
                tokens("qk3", ("qk2_out", 4))
                turn(2)
                tokens("v0", ("qk3_out", 4))
                turn(3)
                tokens("v1", ("v0_out", 4))
                features("g_a", "g_a_out", ("v1_out", 4), h_hi, h_lo)
                features("a_proj", "a_proj_out", ("g_a_out", 8), ya_hi, ya_lo, lambda k: pe.wait_ge(S("ya_split"), k + 1))
                features("g_b", "g_b_out", ("a_proj_out", 8), h_hi, h_lo)

                def scores(u):
                    h, i = UNITS[u]
                    keys = (i + 1) * P
                    if u == 0:
                        pe.wait_ge(S("g_b_out"), 8)
                        pe.wait_ge(S("qk_t_out"), 16)
                    if u >= 3:
                        pe.wait_ge(S("at_exp"), 2 * (u - 2))
                    for m in range(2):
                        half = slice(64 * m, 64 * m + 64)
                        bank = B[2 * (u % 3) + m]
                        pe.matmul(bank[:, :keys], qT[half, h, i * P:(i + 1) * P], kT[half, h, :keys], start=True, stop=False)
                        pe.matmul(bank[:, i * P:keys], ident[:], causal[:], start=False, stop=True).then_inc(S("at_s"), 1)

                def weigh(u):
                    h, i = UNITS[u]
                    s = u % 2
                    pe.wait_ge(S("at_a"), 2 * u + 2)
                    if u:
                        pe.wait_ge(S("at_t_out"), u)
                    for j in range(i + 1):
                        mm = pe.transpose(B[6][:, j * P:(j + 1) * P], tmp[:, 4 + s, j * P:(j + 1) * P], ident[:])
                    mm.then_inc(S("at_t"), 1)

                def values(u):
                    h, i = UNITS[u]
                    s = u % 2
                    pe.wait_ge(S("at_t_out"), u + 1)
                    if u:
                        pe.wait_ge(S("at_o"), u)
                    products(B[7][:, 0:P], [(aT[:, s, j * P:(j + 1) * P], vtok[:, j, h * P:(h + 1) * P])
                                                for j in range(i + 1)]).then_inc(S("at_pv"), 1)

                scores(0)
                scores(1)
                for u in range(len(UNITS)):
                    if u + 2 < len(UNITS):
                        scores(u + 2)
                    weigh(u)
                    if u:
                        values(u - 1)
                values(len(UNITS) - 1)
                pe.wait_ge(S("at_o"), len(UNITS))
                pe.wait_ge(S("o_scaled"), TB)
                for h in range(HEADS):
                    for b in range(TB):
                        mm = pe.transpose(B[h][:, b * P:(b + 1) * P], o_tok[:, b, h * P:(h + 1) * P], ident[:])
                    mm.then_inc(S("yb_t"), 1)
                pe.wait_ge(S("yb_h"), HEADS)
                features("b_proj", "b_proj_out", None, yb_hi, yb_lo, lambda k: pe.wait_ge(S("yb_split"), k + 1))
                features("w_out", "mixer_x", ("b_proj_out", 8), m_hi, m_lo, lambda k: pe.wait_ge(S("m_split"), k + 1))

            if "ffn2" in stages:
                wait_x(pe, "mixer", KD - 1)
                norm("n2", KD)
                gate_up("ffn2", "n2", silu_free("ffn2"))
                down("ffn2")

            if "mix2" in stages:
                wait_x(pe, "ffn2", KD - 1)
                pe.wait_ge(S("mod_made"), 2)
                norm("p1", KD)
                features("u2", "u2_out", None, h_hi, h_lo, ready("p1"))
                pe.wait_ge(S("hank_landed"), 16)
                pe.wait_ge(S("flip_made"), 1)
                for g in range(4):
                    pe.matmul(B[4 + g][:], causal[:], hank[:, 2 * g:2 * g + 2, :], start=True, stop=True).then_inc(S("bias_flipped"), 1)
                pe.wait_ge(S("bias_out"), 4)
                pe.wait_ge(S("s5_landed"), 96)
                for part in range(2):
                    for c in range(4):
                        mm = pe.transpose(B[6 + part][:, c * P:(c + 1) * P], c_in[:, part, c].rearrange("p w n -> p (w n)"), ident[:])
                    mm.then_inc(S("c_t"), 1)
                for g in range(8):
                    if g % 4 == 0:
                        pe.wait_ge(S("bd_made"), 8 * (g // 4 + 1))
                    if g >= 2:
                        pe.wait_ge(S("bb_t_out"), g - 1)
                    for i in range(4):
                        mm = pe.transpose(B[4 + g % 2][:, i * P:(i + 1) * P], bd[:, 4 * (g % 4) + i, :], ident[:])
                    mm.then_inc(S("bb_t"), 1)
                tokens("q2", ("u2_out", 4))
                n = PART["kv2"][0]
                pe.wait_ge(S("w_split"), n + 1)
                for b in range(TB):
                    pe.wait_ge(S("q2_out"), b + 1)
                    stream(B[b][:, 0:PC], token_terms(n, KD, PC, b, h_hi, h_lo), 3 * KD).then_inc(S("pe_done"), 1)
                for f in range(6):
                    if f == 0:
                        pe.wait_ge(S("qk2_made"), 1)
                        pe.wait_ge(S("bb_t_out"), 8)
                    if f == 4:
                        pe.wait_ge(S("qk2_made"), 3)
                    if f >= 2:
                        pe.wait_ge(S("qk2_t_out"), f - 1)
                    for b in range(TB):
                        source = q2_raw[:, b, f * P:(f + 1) * P] if f < 4 else k2_dup[:, b, f - 4].rearrange("p w d -> p (w d)")
                        mm = pe.transpose(B[4 + f % 2][:, b * P:(b + 1) * P], source, ident[:])
                    mm.then_inc(S("qk2_t"), 1)
                pe.wait_ge(S("v2_out"), 8)
                pe.wait_ge(S("k2_out"), TB)
                pe.wait_ge(S("c_out"), 16)
                pe.wait_ge(S("qk2_t_out"), 6)

                def sw_scores(u):
                    b, n = SW_UNITS[u]
                    lo = P if b == 0 else 0
                    if u:
                        pe.wait_ge(S("sw_t_out"), SW_BEFORE[u])
                    for slot in range(2):
                        for odd in range(2):
                            half = slice(64 * odd, 64 * odd + 64)
                            mm = pe.matmul(B[5 + odd][:, slot * 2 * P + lo:(slot + 1) * 2 * P], q2T[half, 2 * n + slot, b * P:(b + 1) * P],
                                           k2T[half, n, (b - 1) * P + lo:(b + 1) * P], start=True, stop=True)
                            if slot:
                                mm.then_inc(S("sw_s"), 1)

                def sw_turn(u):
                    pe.wait_ge(S("sw_p"), u + 1)
                    for kb in SW_BLOCKS[u]:
                        for h in range(4):
                            mm = pe.transpose(B[5 + kb][:, h * P:(h + 1) * P], prob[:, u % 2, h, kb * P:(kb + 1) * P], ident[:])
                        mm.then_inc(S("sw_t"), 1)

                def sw_values(u):
                    b, n = SW_UNITS[u]
                    pe.wait_ge(S("sw_t_out"), SW_BEFORE[u + 1])
                    if u:
                        pe.wait_ge(S("sw_out"), 2 * u)
                    products(B[7][:], [(v2[:, b - 1 + kb, n].rearrange("p w d -> p (w d)"), pT[:, u % 2, kb, :]) for kb in SW_BLOCKS[u]])\
                        .then_inc(S("sw_pv"), 1)

                def inputs(st):
                    if st >= 2:
                        pe.wait_ge(S("scan_in"), 4 * (st - 1))
                    for part in range(2):
                        pe.matmul(B[2 * (st % 2) + part][:], bbT[:, part, st, :], u2[:, st // 4, :], start=True, stop=True).then_inc(S("bu"), 1)

                SCAN_TERMS = (0, 2, 1, 3)

                def outputs(st):
                    if st >= 4 and st % 4 == 0:
                        pe.wait_ge(S("s5_y"), st // 4)
                    pe.wait_ge(S("scan_p"), 2 * st + 2)
                    pe.wait_ge(S("scan_q"), 2 * st + 2)
                    products(B[4][:], [(cT[:, i % 2, st, :], scan_product(st, i)) for i in SCAN_TERMS],
                             st % 4 == 0, st % 4 == 3).then_inc(S("y_added"), 1)

                inputs(0)
                for st in range(NS):
                    u = st // 2
                    if st + 1 < NS:
                        inputs(st + 1)
                    if st % 2 == 0:
                        if u:
                            sw_values(u - 1)
                        sw_scores(u)
                    if st:
                        outputs(st - 1)
                    if st % 2:
                        sw_turn(u)
                sw_values(len(SW_UNITS) - 1)
                outputs(NS - 1)
                norm("pa", 4)
                features("glu", "glu_gate", None, z_hi, z_lo, lambda k: pe.wait_ge(S("z_split"), k + 1))
                norm("ps", 4)
                features("w_out2", "mix2_x", ("glu_gate", 4), h_hi, h_lo, lambda k: pe.wait_ge(S("norm_split"), NORM["pa"] + 4 + (k + 1 if k < 4 else 4)))

            if "ffn3" in stages:
                wait_x(pe, "mix2", KD - 1)
                norm("p2", KD)
                gate_up("ffn3", "p2", lambda i, half: pe.wait_ge(S("ffn3_conv"), i * 8 + (4 * half + 4)))
                down("ffn3")
            for b in range(TB):
                for half in range(2):
                    wait_x(pe, stages[-1], 4 * half + 3)
                    if b >= 2:
                        pe.wait_ge(S(f"out_turned{half}"), b - 1)
                    for k in range(4):
                        mm = pe.transpose(B[4 + (2 * b + half) % 4][:, k * P:(k + 1) * P], x[:, 4 * half + k, b * P:(b + 1) * P], ident[:])
                    mm.then_inc(S("out_t"), 1)


NAMES = (
    "x", "positions", "ffn1_norm", "ffn1_w_gate", "ffn1_w_up", "ffn1_w_down", "mix_norm", "w_in", "a_ln_gain", "a_ln_bias",
    "a_w_s", "a_b_s", "a_w_proj", "b_q_norm", "b_k_norm", "b_lambda_q1", "b_lambda_k1", "b_lambda_q2", "b_lambda_k2", "b_subln",
    "b_w_proj", "w_out", "ffn2_norm", "ffn2_w_gate", "ffn2_w_up", "ffn2_w_down", "c_2", "w_mod_2", "b_mod_2", "norm1_w_2",
    "w_in_2", "lam_re_2", "lam_im_2", "log_dt_2", "ssm_b_re_2", "ssm_b_im_2", "ssm_c_re_2", "ssm_c_im_2", "ssm_d_2", "w_glu_2",
    "b_glu_2", "q_norm_w_2", "k_norm_w_2", "rel_bias_2", "sinks_2", "out_norm_ssm_2", "out_norm_attn_2", "w_out_2", "norm2_w_2",
    "w_up_2", "conv_w_2", "conv_b_2", "w_down_2",
)


def distance_buckets():
    dist = 2 * P - 1 - np.arange(BAND)
    n = np.maximum(dist, 0)
    log_part = np.log(np.maximum(n, 1) / 16) / math.log(128 / 16)
    bucket = np.where(n < 16, n, np.minimum(16 + (log_part * 16).astype(np.int32), 31))
    seen = (dist >= 0) & (dist < WIN)
    table = np.zeros((33, BAND), np.float32)
    table[bucket[seen], np.flatnonzero(seen)] = 1.0
    table[32, ~seen] = NEG
    return table


def kernel(**inputs):
    from concourse import bacc
    from concourse.bass_utils import run_bass_kernel_spmd

    nc = bacc.Bacc("TRN2", target_bir_lowering=False, num_devices=1)
    arrays, aps = {}, {}
    for name in NAMES:
        a = np.ascontiguousarray(inputs[name])
        arrays[f"in_{name}"] = a
        aps[name] = nc.dram_tensor(f"in_{name}", a.shape, mybir.dt.from_np(a.dtype), kind="ExternalInput").ap()
    table = distance_buckets()
    arrays["rel_onehot"] = table
    onehot = nc.dram_tensor("rel_onehot", table.shape, F32, kind="ExternalInput").ap()
    out = nc.dram_tensor("out_x", (1, T, D), F32, kind="ExternalOutput").ap()
    build(nc, aps, onehot, out)
    r = run_bass_kernel_spmd(nc, [arrays], core_ids=[0])
    return r.results[0]["out_x"]
```

```python
import math
from contextlib import ExitStack

import numpy as np

import concourse.bass as bass
from concourse import mybir

F32 = mybir.dt.float32
F32R = mybir.dt.float32r
I32 = mybir.dt.int32
ALU = mybir.AluOpType
ACT = mybir.ActivationFunctionType
AX = mybir.AxisListType

P = 128
T = 512
TB = T // P
D = 1024
KD = D // P
FF = 2816
KF = FF // P
A_W = 512
A_G = 8
HEADS = 8
QK = 64
ROT = 8
LAM_INIT = 0.8 - 0.6 * math.exp(-0.3 * 0)
EPS = 1e-6
LN_EPS = 1e-5
NS = 16
SG = 16
WIN = 128
NQ = 8
NKV = 2
NEG = -1e30
BAND = 2 * P + P - 1
PANEL = 2048
PC = 256
DOWN_K = ((0, 6), (6, 6), (12, 5), (17, 5))
GU_STEPS = FF // PC
BESIDE = KF - 6
BESIDE_STEPS = BESIDE // 2
MOD_GROUPS = 6 * D // T
MOD_SLOTS = 4
ROT_SLOTS = 3
PHASES = {"ffn1": ((0, BESIDE_STEPS, True, True), (BESIDE_STEPS, GU_STEPS, False, False)),
          "ffn2": ((0, MOD_GROUPS - BESIDE_STEPS, True, True), (MOD_GROUPS - BESIDE_STEPS, BESIDE_STEPS, False, True),
                   (BESIDE_STEPS, GU_STEPS, False, False))}
BESIDE_AT = {"ffn1": 0, "ffn2": BESIDE_STEPS}
DOWN_PANELS = 16
FFN_PANELS = 2 * GU_STEPS + DOWN_PANELS
MIX_PANELS = 34
MIX2_PANELS = 10
BASE = {"ffn1": 0}
BASE["mixer"] = BASE["ffn1"] + FFN_PANELS
BASE["ffn2"] = BASE["mixer"] + MIX_PANELS
BASE["mix2"] = BASE["ffn2"] + FFN_PANELS
BASE["ffn3"] = BASE["mix2"] + MIX2_PANELS
END = BASE["ffn3"] + FFN_PANELS
STAGES = ("ffn1", "mixer", "ffn2", "mix2", "ffn3")
ROUND = 12582912.0
TWO_PI = 2.0 * math.pi
PI_1 = 6.28125
PI_2 = float(np.float32(np.round((TWO_PI - PI_1) * 2.0**20) / 2.0**20))
PI_3 = TWO_PI - PI_1 - PI_2
PI_LOW = 3.1415925
ROWS = {}
for _tile, _names in enumerate((
    (("ffn1_norm", 8), ("mix_norm", 8), ("ffn2_norm", 8), ("norm1_w_2", 8), ("norm2_w_2", 8), ("b_mod_2", 48),
     ("ssm_d_2", 4), ("b_glu_2", 4), ("out_norm_ssm_2", 4), ("out_norm_attn_2", 4), ("b_subln", 1), ("c_2", 8)),
    (("lam_re_2", 16), ("lam_im_2", 16), ("conv_b_2", 44), ("conv_w_2:2", 44)),
    (("conv_w_2:0", 44), ("conv_w_2:1", 44)),
)):
    _at = 0
    for _name, _n in _names:
        ROWS[_name] = (_tile, _at, _n)
        _at += _n
ROW_COUNTS = tuple(max(a + n for t, a, n in ROWS.values() if t == tile) for tile in range(3))


class Steps:

    def __init__(self, engine, semaphore):
        self.engine, self.semaphore, self.n = engine, semaphore, 0

    def __call__(self, instruction):
        instruction.then_inc(self.semaphore, 1)
        self.n += 1
        self.engine.wait_ge(self.semaphore, self.n)


def build(nc, inp, rel_onehot, out, last="ffn3"):
    stages = STAGES[:STAGES.index(last) + 1]
    end = BASE[last] + {"mixer": MIX_PANELS, "mix2": MIX2_PANELS}.get(last, FFN_PANELS)

    def col_major(w):
        return w.rearrange("l (k p) n -> p (l k) n", p=P)

    rot_dram = nc.dram_tensor("rotations", (2, NS, P, T), F32).ap()
    band_dram = nc.dram_tensor("band", (NQ, BAND), F32)

    with ExitStack() as ctx:
        def sb(name, shape, dt=F32, scope=ctx):
            return scope.enter_context(nc.sbuf_tensor(name, shape, dt))

        sems = {}

        def S(name):
            if name not in sems:
                sems[name] = ctx.enter_context(nc.semaphore(name))
            return sems[name]

        B = [ctx.enter_context(nc.psum_tensor(f"bank{i}", [P, T], F32)) for i in range(8)]

        x = sb("x", [P, KD, T])
        w_raw = [sb(f"w_raw{i}", [P, PANEL]) for i in range(2)]
        w_hi = [sb(f"w_hi{i}", [P, PANEL], F32R) for i in range(2)]
        w_lo = [sb(f"w_lo{i}", [P, PANEL], F32R) for i in range(2)]
        tmp = sb("tmp", [P, 6, T])
        rstd = sb("rstd", [P, T])
        ident = sb("ident", [P, P])
        ones = sb("ones", [P, P])
        causal = sb("causal", [P, P])
        vec = sb("vec", [P, 3, P])
        small = sb("small", [P, 96])
        stat = sb("stat", [P, 96])
        cos_t = sb("cos_t", [P, TB, ROT])
        sin_t = sb("sin_t", [P, TB, ROT])
        gains = sb("gains", [P, 4, QK])
        lam_in = sb("lam_in", [P, 4, QK])
        sink = sb("sink", [P, NQ])
        mod = sb("mod", [P, 48])
        gain2 = sb("gain2", [P, 2, KD])
        s5 = sb("s5", [P, 24, NS])
        pos_i = sb("pos_i", [P, TB], I32)

        def col(name, i):
            t, a, _ = ROWS[name]
            return vec[:, t, a + i:a + i + 1]

        def cols(name):
            t, a, n = ROWS[name]
            return vec[:, t, a:a + n]

        def col_at(name, i, off=0):
            t, a, _ = ROWS[name]
            return vec[:, t, bass.ds(i + (a + off), 1)]

        def overlay(size, *tiles):
            made = []
            for first, name, shape, dt in tiles:
                with ExitStack() as area:
                    if first:
                        sb(f"under_{name}", [P, first * T], F32, area)
                    made.append(sb(name, shape, dt, area))
            return made

        h_hi, h_lo, o_tok, yb_hi, rot, sc_a, sc_v, sc_p = overlay(
            2 * KD,
            (0, "h_hi", [P, KD, T], F32R), (KD, "h_lo", [P, KD, T], F32R),
            (KD, "o_tok", [P, TB, D], F32), (0, "yb_hi", [P, KD, T], F32R),
            (0, "rot", [P, ROT_SLOTS, 2, T], F32), (2 * ROT_SLOTS, "sc_a", [P, 4, T], F32),
            (2 * ROT_SLOTS + 4, "sc_v", [P, 4, T], F32), (2 * ROT_SLOTS + 8, "sc_p", [P, 2, T], F32),
        )
        sb("h_area", [P, 2 * KD * T])

        hid_hi, hid_lo, x_in, rows, oh, rel, band, ang, log_dt, rot_t, rot_ti, rot_n, rot_r, rot_abs, rot_cs, mod_acc, mod_raw = overlay(
            2 * KF,
            (0, "hid_hi", [P, KF, T], F32R), (KF, "hid_lo", [P, KF, T], F32R),
            (0, "x_in", [P, TB, D], F32), (8, "rows", [P, 3, P], F32), (9, "oh", [33, BAND], F32),
            (10, "rel", [33, NQ], F32), (11, "band_row", [NQ, BAND], F32), (12, "ang", [P, 3, TB, ROT], F32), (13, "log_dt", [P, 2 * NS], F32),
            (BESIDE, "rot_t", [P, T], F32), (BESIDE + 1, "rot_ti", [P, T], I32), (BESIDE + 1, "rot_n", [P, T], F32),
            (BESIDE + 2, "rot_r", [P, T], F32), (BESIDE + 3, "rot_abs", [P, T], F32), (BESIDE + 4, "rot_cs", [P, 2, T], F32),
            (KF + BESIDE, "mod_acc", [P, T], F32), (KF + BESIDE + 1, "mod_raw", [P, MOD_SLOTS, T], F32),
        )
        vg, u_g, ya_hi, ya_lo, qT, kT, vtok, ga, gb, aT, m_hi, m_lo, yb_lo, ln_g, ln_b, wsT, ws_in, bs, qk_raw0, qk_raw1 = overlay(
            2 * KF,
            (0, "vg", [P, TB, A_W], F32), (4, "u_g", [P, 4, T], F32),
            (8, "ya_hi", [P, 4, T], F32R), (4, "ya_lo", [P, 4, T], F32R),
            (12, "qT", [P, HEADS, T], F32), (20, "kT", [P, HEADS, T], F32), (28, "vtok", [P, TB, D], F32),
            (36, "ga", [P, KD, T], F32),
            (0, "gb", [P, KD, T], F32), (8, "aT", [P, 2, T], F32),
            (12, "m_hi", [P, KD, T], F32R), (20, "m_lo", [P, KD, T], F32R), (28, "yb_lo", [P, KD, T], F32R),
            (12, "ln_g", [P, A_W], F32), (13, "ln_b", [P, A_W], F32),
            (28, "wsT", [P, A_G, P], F32), (30, "ws_in", [P, A_G, P], F32), (32, "bs", [P, 4, P], F32),
            (36, "qk_raw0", [P, TB, T], F32), (40, "qk_raw1", [P, TB, T], F32),
        )
        qk_raw = [qk_raw0, qk_raw1]
        (u2, q2T, k2T, v2, bbT, cT, yat, b_in, bb, c_in, bd, bias, hank, q_sq, k_sq, pT, prob,
         z_hi, z_lo, yat_sq, gate) = overlay(
            2 * KF,
            (0, "u2", [P, 4, T], F32), (4, "q2T", [P, 4, T], F32), (8, "k2T", [P, NKV, T], F32),
            (10, "v2", [P, TB, NKV, 2, QK], F32),
            (12, "bbT", [P, 2, NS, P], F32), (20, "cT", [P, 2, NS, P], F32), (28, "yat", [P, 4, T], F32),
            (32, "b_in", [P, 2, NS, SG], F32), (33, "bb", [P, 2, NS, SG], F32), (34, "c_in", [P, 2, 4, 2, QK], F32),
            (36, "bd", [P, NS, P], F32), (40, "bias", [P, NQ, 2 * P], F32), (28, "hank", [P, NQ, 2 * P], F32),
            (4, "q_sq", [P, TB, T], F32), (8, "k_sq", [P, TB, NKV * QK], F32),
            (32, "pT", [P, 2, 2, T], F32), (36, "prob", [P, 2, 4, 2 * P], F32),
            (12, "z_hi", [P, 4, T], F32R), (16, "z_lo", [P, 4, T], F32R), (4, "yat_sq", [P, 4, T], F32), (8, "gate", [P, 4, T], F32),
        )

        SW_UNITS = [(b, n) for b in range(TB) for n in range(NKV)]
        SW_BLOCKS = [(1,) if b == 0 else (0, 1) for b, _ in SW_UNITS]
        SW_BEFORE = [sum(len(k) for k in SW_BLOCKS[:u]) for u in range(len(SW_UNITS) + 1)]

        def scan_product(st, i):
            if st % 2 == 0:
                return tmp[:, i, :]
            return tmp[:, 4 + i, :] if i < 2 else sc_p[:, i - 2, :]

        def glu_bank(t):
            return B[(2, 3, 5, 6)[t]]

        def sw_cols(first, u):
            return stat[:, first + 4 * (u % 2):first + 4 * (u % 2) + 4]

        sb("shared_area", [P, 2 * KF * T])

        def used(n, quarters=4):
            return 4 * n + quarters

        def panel(buf, n, k, c):
            return buf[n % 2][:, :k * c].rearrange("p (k c) -> p k c", k=k)

        X_OF = {"start": ("x_turned", 1), "ffn1": ("ffn1_x", 5), "mixer": ("mixer_x", 1), "ffn2": ("ffn2_x", 5),
                "mix2": ("mix2_x", 1), "ffn3": ("ffn3_x", 5)}

        NORM_PARTS = {"n1": (KD, KD), "nm": (KD, 2), "n2": (KD, 2), "p1": (KD, 2), "pa": (4, 4), "ps": (4, 4), "p2": (KD, 2)}
        NORMS = list(NORM_PARTS)
        NORM, NORM_SQ, NORM_SUM = {}, {}, {}
        for name in NORMS:
            before = [NORM_PARTS[b] for b in NORMS[:len(NORM)]]
            NORM[name] = sum(tiles for tiles, _ in before)
            NORM_SQ[name] = sum(direct for _, direct in before)
            NORM_SUM[name] = NORM_SQ[name] + sum(direct < tiles for tiles, direct in before)
        ADDED = [name for name in NORMS if NORM_PARTS[name][1] < NORM_PARTS[name][0]]

        def sums_of(name):
            tiles, direct = NORM_PARTS[name]
            return NORM_SUM[name] + direct + (direct < tiles)

        HID = {"ffn1": 0, "ffn2": KF, "ffn3": 2 * KF}

        def wait_x(eng, stage, k):
            name, first = X_OF[stage]
            eng.wait_ge(S(name), first + k)

        def bank_of(t):
            return B[t % 4]

        MIX = BASE["mixer"]
        MIX2 = BASE["mix2"]
        MIX_PARTS = (("v_gm", 0, 2, 4), ("u_gm", 2, 2, 4), ("qk0", 4, 2, 4), ("qk1", 6, 2, 4), ("qk2", 8, 2, 4),
                     ("v0", 10, 2, 4), ("qk3", 12, 2, 4), ("v1", 14, 2, 4), ("g_a", 16, 4, 8), ("a_proj", 20, 2, 8),
                     ("g_b", 22, 4, 8), ("b_proj", 26, 4, 8), ("w_out", 30, 4, 8))
        MIX2_PARTS = (("u2", 0, 2, 4), ("q2", 2, 2, 4), ("kv2", 4, 1, 4), ("glu", 5, 1, 4), ("w_out2", 6, 4, 8))
        PART = {name: (MIX + first, panels, outs) for name, first, panels, outs in MIX_PARTS}
        PART.update({name: (MIX2 + first, panels, outs) for name, first, panels, outs in MIX2_PARTS})
        BEFORE = {b[0]: a for parts in (MIX_PARTS, MIX2_PARTS) for a, b in zip(parts, parts[1:])}
        BEFORE = {name: (part[0], part[3]) for name, part in BEFORE.items()}
        W_IN_COL = {"v_gm": 2 * D + A_W, "qk0": 2 * D + 2 * A_W, "qk1": 2 * D + 2 * A_W + T, "qk2": 3 * D + 2 * A_W,
                    "qk3": 3 * D + 2 * A_W + T, "v0": 4 * D + 2 * A_W, "v1": 4 * D + 2 * A_W + T}
        UNITS = [(h, i) for h in range(HEADS) for i in range(TB)]

        eps_col, half_pi_col, ln_eps_col = (small[:, i:i + 1] for i in (20, 21, 22))
        eps_width_col = {T: EPS * T, D: EPS * D}
        q2_raw = tmp[:, 0:4, :]
        k2_raw = tmp[:, 4, :].rearrange("p (b n) -> p b n", b=TB)

        block = ctx.enter_context(nc.Block())

        @block.sync
        def _(sp):
            def load(n, source, k, c):
                if isinstance(n, int):
                    if n >= 2:
                        sp.wait_ge(S("w_split"), n - 1)
                else:
                    sp.wait_ge(S("w_split"), n[0] - 1)
                i = n if isinstance(n, int) else n[1]
                sp.dma_start(panel(w_raw, i, k, c), source).then_inc(S(f"w_landed{i % 2}"), 16)

            def load_ffn(name, gate, up, gate_col, up_col, down):
                base = BASE[name]
                gate_v, up_v, down_v = col_major(gate), col_major(up), col_major(down)
                first = 0
                if base == 0:
                    load(0, gate_v[:, :, gate_col:gate_col + PC], KD, PC)
                    load(1, up_v[:, :, up_col:up_col + PC], KD, PC)
                    first = 1
                with sp.Fori(first, GU_STEPS) as i:
                    load((i * 2 + base, base), gate_v[:, :, bass.ds(i * PC + gate_col, PC)], KD, PC)
                    load((i * 2 + (base + 1), base + 1), up_v[:, :, bass.ds(i * PC + up_col, PC)], KD, PC)
                base += 2 * GU_STEPS
                with sp.Fori(0, 2) as j:
                    for c in range(8):
                        k0, kn = DOWN_K[c % 4]
                        load((j * 8 + (base + c), base + c),
                             down_v[:, k0:k0 + kn, bass.ds(j * 512 + c // 4 * PC, PC)], kn, PC)

            def load_tokens(name, w, at):
                base = PART[name][0]
                for half in range(2):
                    load(base + half, w[:, 4 * half:4 * half + 4, at:at + T], 4, T)

            def load_features(name, w, at, first=0, end=None):
                base, panels, _ = PART[name]
                for i in range(first, end or panels):
                    load(base + i, w[:, :, at + i * PC:at + (i + 1) * PC], KD, PC)

            x_v = inp["x"].rearrange("o (b p) d -> p (o b) d", p=P)
            sp.dma_start(x_in[:, :, 0:T], x_v[:, :, 0:T]).then_inc(S("x_landed0"), 16)
            sp.dma_start(x_in[:, :, T:D], x_v[:, :, T:D]).then_inc(S("x_landed1"), 16)
            load_ffn("ffn1", inp["ffn1_w_gate"], inp["ffn1_w_up"], 0, 0, inp["ffn1_w_down"])
            if "mixer" in stages:
                w_in = col_major(inp["w_in"])

                load_tokens("v_gm", w_in, W_IN_COL["v_gm"])
                load_features("u_gm", w_in, 2 * D)
                for name in ("qk0", "qk1", "qk2", "v0", "qk3", "v1"):
                    load_tokens(name, w_in, W_IN_COL[name])
                load_features("g_a", w_in, 0)
                for i in range(2):
                    load(PART["a_proj"][0] + i, col_major(inp["a_w_proj"])[:, :, i * T:(i + 1) * T], 4, T)
                load_features("g_b", w_in, D)
                load_features("b_proj", col_major(inp["b_w_proj"]), 0)
                load_features("w_out", col_major(inp["w_out"]), 0)
            if "ffn2" in stages:
                load_ffn("ffn2", inp["ffn2_w_gate"], inp["ffn2_w_up"], 0, 0, inp["ffn2_w_down"])
            if "mix2" in stages:
                w_in = col_major(inp["w_in_2"])
                load_features("u2", w_in, 0)
                load_tokens("q2", w_in, T)
                load(PART["kv2"][0], w_in[:, :, 2 * T:2 * T + PC], KD, PC)
                load(PART["glu"][0], col_major(inp["w_glu_2"]), 4, T)
                load_features("w_out2", col_major(inp["w_out_2"]), 0, 0, 3)
                sp.wait_ge(S("rot_stored"), 16 * (NS + 1))
                sp.wait_ge(S("pe_done"), used(PART["kv2"][0]))
                for st in range(NS):
                    if st >= ROT_SLOTS:
                        sp.wait_ge(S("scan_p"), 2 * (st - ROT_SLOTS) + 2)
                        sp.wait_ge(S("scan_q"), 2 * (st - ROT_SLOTS) + 2)
                    sp.dma_start(rot[:, st % ROT_SLOTS], rot_dram[:, st].rearrange("w p t -> p w t")).then_inc(S(f"rot_landed{st % ROT_SLOTS}"), 16)
                load_features("w_out2", col_major(inp["w_out_2"]), 0, 3, 4)
            if "ffn3" in stages:
                load_ffn("ffn3", inp["w_up_2"], inp["w_up_2"], 0, FF, inp["w_down_2"])
            out_v = out.rearrange("o (b p) d -> p (o b) d", p=P)
            for b in range(TB):
                for half in range(2):
                    sp.wait_ge(S(f"out_turned{half}"), b + 1)
                sp.dma_start(out_v[:, b, :], x_in[:, b, :]).then_inc(S("out_stored"), 16)
            sp.wait_ge(S("out_stored"), 16 * TB)

        @block.gpsimd
        def _(pool):
            done = Steps(pool, S("pool_done"))
            done(pool.memset(ones[:], 1.0))
            done(pool.memset(ident[:], 0.0))
            done(pool.memset(causal[:], 0.0))
            done(pool.affine_select(out=ident[:], in_=ident[:], compare_op=ALU.not_equal, fill=1.0, base=0,
                                    pattern=[[-1, P]], channel_multiplier=1))
            done(pool.affine_select(out=causal[:], in_=causal[:], compare_op=ALU.is_ge, fill=NEG, base=0,
                                    pattern=[[-1, P]], channel_multiplier=1))
            pool.memset(rel[32:33, :], 1.0).then_inc(S("consts_made"), 1)
            pool.wait_ge(S("band_made"), 1)
            pool.dma_start(band_dram.ap(), band[:]).then_inc(S("band_stored"), 16)
            wm = col_major(inp["w_mod_2"])

            def beside(name):
                done(pool.iota(rot_ti[:], pattern=[[1, T]], base=0, channel_multiplier=0))
                pool.tensor_copy(rot_t[:], rot_ti[:]).then_inc(S("rot_t_made"), 1)
                first = BESIDE_AT[name]
                groups = sum(end - start for start, end, mods, _ in PHASES[name] if mods)
                with pool.Fori(0, groups) as i:
                    for k in range(KD):
                        pool.wait_ge(S("mod_step"), i * KD + (first * KD + k + 1))
                        pool.dma_start(mod_raw[:, k % MOD_SLOTS, :], wm[:, k, bass.ds(i * T + first * T, T)])\
                            .then_inc(S(f"mod_landed{k % MOD_SLOTS}"), 16)

            beside("ffn1")

            def split(n):
                pool.wait_ge(S("w_hi_done"), n + 1)
                s = n % 2
                pool.tensor_tensor(w_lo[s][:], w_raw[s][:], w_hi[s][:].bitcast(F32), ALU.subtract).then_inc(S("w_split"), 1)

            def norm(name, before):
                tiles, direct = NORM_PARTS[name]
                for k in range(tiles - direct):
                    wait_x(pool, before, k)
                    done(pool.tensor_tensor(tmp[:, min(k, 1), :], x[:, k, :], x[:, k, :], ALU.mult))
                    if k:
                        ins = pool.tensor_tensor(tmp[:, 0, :], tmp[:, 0, :], tmp[:, 1, :], ALU.add)
                        if k < tiles - direct - 1:
                            done(ins)
                ins.then_inc(S("norm_added"), 1)

            if "mixer" in stages:
                norm("nm", "ffn1")
                split(BASE["mixer"] + 1)
                pool.wait_ge(S("ws_landed"), 16)
                pool.affine_select(out=ws_in[:], in_=ws_in[:], compare_op=ALU.is_ge, fill=0.0, base=0,
                                   pattern=[[0, A_G], [-1, P]], channel_multiplier=1).then_inc(S("ws_masked"), 1)
            if "ffn2" in stages:
                norm("n2", "mixer")
                split(BASE["ffn2"] + 1)
                wait_x(pool, "mixer", KD - 1)
                beside("ffn2")
            if "mix2" in stages:
                norm("p1", "ffn2")
                split(BASE["mix2"] + 1)
                wait_x(pool, "ffn2", 0)
                done(pool.memset(causal[:], 0.0))
                pool.affine_select(out=causal[:], in_=causal[:], compare_op=ALU.not_equal, fill=1.0, base=1 - P,
                                   pattern=[[1, P]], channel_multiplier=1).then_inc(S("flip_made"), 1)
                pool.memset(bd[:], 0.0).then_inc(S("zeroed"), 1)
                pool.memset(cT[:], 0.0).then_inc(S("zeroed"), 1)
                for st in range(NS + 1):
                    if st < NS:
                        for i, op in enumerate((ALU.add, ALU.subtract)):
                            pool.wait_ge(S("scan_in"), 4 * st + 2 * i + 2)
                            if st:
                                pool.wait_ge(S("scanned"), 2 * (st - 1) + i + 1)
                            pool.tensor_tensor(sc_v[:, i, :], sc_a[:, 2 * i, :], sc_a[:, 2 * i + 1, :], op).then_inc(S("scan_v"), 1)
                    if st:
                        r = rot[:, (st - 1) % ROT_SLOTS]
                        pool.wait_ge(S("scanned"), 2 * st - 1)
                        if st >= 3:
                            pool.wait_ge(S("y_added"), st - 2)
                        for i in range(2):
                            pool.tensor_tensor(scan_product(st - 1, i), sc_v[:, 2, :], r[:, i, :], ALU.mult).then_inc(S("scan_p"), 1)
                for k in range(4):
                    pool.wait_ge(S("sw_out"), 2 * len(SW_UNITS) - (2 if k < 2 else 0))
                    pool.tensor_tensor(yat_sq[:, k, :], yat[:, k, :], yat[:, k, :], ALU.mult).then_inc(S("norm_sq"), 1)
            if "ffn3" in stages:
                norm("p2", "mix2")
                split(BASE["ffn3"] + 1)

        @block.scalar
        def _(act):
            done = Steps(act, S("act_done"))

            def split(n, i=None):
                if i is None:
                    if n >= end:
                        return
                    i = n
                    act.wait_ge(S(f"w_landed{i % 2}"), 16 * (n // 2 + 1))
                    if n >= 2:
                        act.wait_ge(S("pe_done"), used(n - 2))
                else:
                    act.wait_ge(S(f"w_landed{i % 2}"), (n - (i % 2)) * 8 + 16)
                    act.wait_ge(S("pe_done"), (n - 2) * 4 + 4)
                act.copy(w_hi[i % 2][:], w_raw[i % 2][:]).then_inc(S("w_hi_done"), 1)

            def norm(name, tiles, ready, shift=None, hi=None, width=D, panel=None):
                hi = h_hi if hi is None else hi
                count, direct = NORM_PARTS[name]
                for d in range(direct if ready else 0):
                    ready(act, count - direct + d)
                    if d >= 2:
                        act.wait_ge(S("norm_summed"), NORM_SUM[name] + d - 1)
                    act.activation(tmp[:, 2 + d % 2, :], tiles[:, count - direct + d, :], ACT.Square).then_inc(S("norm_sq"), 1)
                act.wait_ge(S("norm_summed"), sums_of(name))
                act.activation(rstd[:], B[7][:], ACT.Abs_reciprocal_sqrt, scale=1.0 / width, bias=eps_col).then_inc(S("norm_root"), 1)
                if panel is not None:
                    split(panel)
                for k in range(count):
                    act.wait_ge(S("norm_h"), NORM[name] + k + 1)
                    source = tmp[:, 2 + k % 4, :]
                    if shift is None:
                        act.copy(hi[:, k, :], source).then_inc(S("norm_hi"), 1)
                    else:
                        act.activation(hi[:, k, :], source, ACT.Identity, bias=shift(k)).then_inc(S("norm_hi"), 1)

            def rotations(st):
                act.wait_ge(S("rot_turns"), st + 1)
                act.wait_ge(S("rot_stored"), st * 16 + 16)
                act.activation(rot_cs[:, 1, :], rot_r[:], ACT.Sin, scale=-TWO_PI).then_inc(S("rot_made"), 1)
                act.activation(rot_abs[:], rot_r[:], ACT.Abs).then_inc(S("rot_read"), 1)
                act.wait_ge(S("rot_read"), st + 2)
                act.activation(rot_cs[:, 0, :], rot_abs[:], ACT.Sin, scale=-TWO_PI, bias=half_pi_col).then_inc(S("rot_made"), 1)
                act.wait_ge(S("rot_made"), st * 2 + 2)
                act.dma_start(rot_dram[:, bass.ds(st, 1)].rearrange("w s p t -> p (w s) t"), rot_cs[:]).then_inc(S("rot_stored"), 16)

            def swiglu(name):
                base = BASE[name]
                for start, stop, _, rots in PHASES[name]:
                    if not rots:
                        act.wait_ge(S("rot_stored"), 16 * (BESIDE_AT[name] + BESIDE_STEPS + 1))
                    with act.Fori(start, stop) as i:
                        if rots:
                            rotations(i + BESIDE_AT[name])
                        split(i * 2 + (base + 2), base)
                        for t in range(2):
                            act.wait_ge(S("pe_done"), i * 8 + (4 * base + 2 * t + 2))
                            act.wait_ge(S("hid"), i * 2 + (HID[name] + t + 1))
                            act.activation(tmp[:, t, :], B[t][:], ACT.Silu).then_inc(S("silu"), 1)
                        split(i * 2 + (base + 3), base + 1)
                        for t in range(2):
                            act.wait_ge(S("hid"), i * 2 + (HID[name] + t + 3))
                            act.copy(hid_hi[:, bass.ds(i * 2 + t, 1), :], tmp[:, 2 + t:3 + t, :]).then_inc(S("hid_hi"), 1)

            def down(name):
                for n in range(BASE[name] + 2 * GU_STEPS, BASE[name] + FFN_PANELS - 1):
                    split(n + 2)

            act.sem_inc(S("silu"), 2)
            act.sem_inc(S("rot_read"), 1)
            act.sem_inc(S("rot_stored"), 16)
            for name, (tile, at, n) in ROWS.items():
                param, _, tap = name.partition(":")
                source = inp[param][0, int(tap)] if tap else (inp[param][0] if inp[param].shape[0] == 1 else inp[param])
                if len(source.shape) == 1:
                    source = source.rearrange("(n p) -> n p", p=P)
                elif source.shape[1] != P:
                    source = source.rearrange("(n two) p -> n (two p)", two=P // source.shape[1])
                act.dma_start(rows[at:at + n, tile, :], source).then_inc(S("rows_landed"), 16)
            spread = 0
            for tile, names in ((gains, ("b_q_norm", "b_k_norm", "q_norm_w_2", "k_norm_w_2")),
                                (lam_in, ("b_lambda_q1", "b_lambda_k1", "b_lambda_q2", "b_lambda_k2"))):
                for i, name in enumerate(names):
                    act.dma_start(tile[:, i, :], inp[name][0].partition_broadcast(P)).then_inc(S("spread_landed"), 16)
                    spread += 16
            act.dma_start(sink[:], inp["sinks_2"][0].partition_broadcast(P)).then_inc(S("spread_landed"), 16)
            spread += 48
            act.dma_start(log_dt[:], inp["log_dt_2"][0].partition_broadcast(P)).then_inc(S("spread_landed"), 16)
            act.dma_start(pos_i[:], inp["positions"].rearrange("o (b p) -> p (o b)", p=P),
                          allow_slow_non_contiguous=True).then_inc(S("spread_landed"), 16)
            act.dma_start(rel[0:32, :], inp["rel_bias_2"]).then_inc(S("rel_landed"), 16)
            act.dma_start(oh[:], rel_onehot).then_inc(S("rel_landed"), 16)
            act.wait_ge(S("cols_made"), 1)

            split(0)
            split(1)
            norm("n1", x, lambda eng, k: wait_x(eng, "start", k))
            act.wait_ge(S("vec_made"), 3)
            act.activation(small[:, 0:KD], cols("c_2"), ACT.Silu).then_inc(S("prep_a"), 1)
            act.wait_ge(S("spread_landed"), spread)
            for half in range(2):
                own = slice(64 * half, 64 * half + 64)
                act.activation(s5[own, 2, :], log_dt[own, half::2], ACT.Exp).then_inc(S("prep_a"), 1)
            act.wait_ge(S("prep_v"), 1)
            act.activation(small[:, 10:12], small[:, 8:10], ACT.Exp).then_inc(S("prep_a"), 1)
            act.wait_ge(S("prep_v"), 2)
            act.activation(s5[:, 3, :], s5[:, 15, :], ACT.Exp).then_inc(S("prep_a"), 1)
            act.wait_ge(S("prep_v"), 3)
            for angle, sine, cosine in ((s5[:, 4, :], s5[:, 6, :], s5[:, 7, :]), (ang[:, 0], sin_t[:], cos_t[:])):
                act.activation(sine, angle, ACT.Sin).then_inc(S("prep_a"), 1)
                done(act.activation(cosine, angle, ACT.Abs))
                act.activation(cosine, cosine, ACT.Sin, scale=-1.0, bias=half_pi_col).then_inc(S("prep_a"), 1)

            act.wait_ge(S("band_stored"), 16)
            swiglu("ffn1")
            down("ffn1")

            if "mixer" in stages:
                wait_x(act, "ffn1", KD - 1)
                act.dma_start(ws_in[:], inp["a_w_s"][0].rearrange("g t s -> t g s")).then_inc(S("ws_landed"), 16)
                for name, tile in (("a_ln_gain", ln_g), ("a_ln_bias", ln_b)):
                    act.dma_start(tile[:], inp[name][0].partition_broadcast(P)).then_inc(S("ln_landed"), 16)
                for half in range(2):
                    act.dma_start(bs[64 * half:64 * half + 64], inp["a_b_s"][0].rearrange("(f two) t -> two f t", two=2)[half]
                                  .partition_broadcast(64)).then_inc(S("bs_landed"), 16)
                norm("nm", x, lambda eng, k: wait_x(eng, "ffn1", k), panel=BASE["mixer"] + 1)

                def tokens(name, evacuate):
                    n = PART[name][0]
                    split(n + 2)
                    for b in range(TB):
                        if b == TB - 1:
                            split(n + 3)
                        act.wait_ge(S("pe_done"), used(n + 1, b + 1))
                        evacuate(b)

                def features(name, evacuate):
                    n, panels, _ = PART[name]
                    for i in range(panels):
                        for t in range(2):
                            if t == 1:
                                split(n + i + 2)
                            act.wait_ge(S("pe_done"), used(n + i, 2 * t + 2))
                            evacuate(2 * i + t)

                tokens("v_gm", lambda b: act.activation(vg[:, b, :], B[b][:], ACT.Gelu).then_inc(S("v_gm_out"), 1))
                features("u_gm", lambda t: act.activation(u_g[:, t, :], bank_of(t)[:], ACT.Gelu).then_inc(S("u_gm_out"), 1))
                act.wait_ge(S("ln_var"), 1)
                act.activation(stat[:, 40:44], stat[:, 36:40], ACT.Sqrt, bias=ln_eps_col).then_inc(S("ln_root"), 1)

                def turned(j):
                    dst = (qT, kT)[j // 2]
                    for f in range(4):
                        act.wait_ge(S("qk_t"), 4 * j + f + 1)
                        act.copy(dst[:, 4 * (j % 2) + f, :], B[4 + f][:]).then_inc(S("qk_t_out"), 1)

                def queries_keys(j):
                    raw = qk_raw[j % 2]
                    if j >= 2:
                        act.wait_ge(S("qk_t"), 4 * (j - 1))
                    tokens(f"qk{j}", lambda b: act.copy(raw[:, b, :], B[b][:]).then_inc(S(f"qk{j}_out"), 1))
                    if j == 2:
                        for f in range(4):
                            act.wait_ge(S("ya_h"), 2 * f + 2)
                            act.copy(ya_hi[:, f, :], tmp[:, 4 + f % 2, :]).then_inc(S("ya_hi_out"), 1)
                    act.wait_ge(S(f"qk{j}_out"), TB)
                    if j:
                        act.wait_ge(S("qk_done"), j)
                    act.activation(tmp[:, 0:4, :], raw[:], ACT.Square).then_inc(S("qk_sq"), 1)
                    act.wait_ge(S("qk_ssq"), j + 1)
                    act.activation(stat[:, 0:32], stat[:, 0:32], ACT.Sqrt, scale=1.0 / QK, bias=eps_col).then_inc(S("qk_root"), 1)

                def values(g):
                    tokens(f"v{g}", lambda b: act.copy(vtok[:, b, g * T:(g + 1) * T], B[b][:]).then_inc(S(f"v{g}_out"), 1))

                queries_keys(0)
                for f in range(2):
                    act.wait_ge(S("ws_t"), f + 1)
                    act.copy(wsT[:, 4 * f:4 * f + 4, :], B[6 + f][:].rearrange("p (g t) -> p g t", g=4)).then_inc(S("ws_t_out"), 1)
                queries_keys(1)
                turned(0)
                queries_keys(2)
                act.wait_ge(S("ya_h"), 8)
                values(0)
                turned(1)
                queries_keys(3)
                turned(2)
                values(1)
                turned(3)
                features("g_a", lambda t: act.activation(ga[:, t, :], bank_of(t)[:], ACT.Sigmoid).then_inc(S("g_a_out"), 1))
                for i in range(2):
                    split(PART["a_proj"][0] + i + 2)
                features("g_b", lambda t: act.activation(gb[:, t, :], bank_of(t)[:], ACT.Sigmoid).then_inc(S("g_b_out"), 1))

                def soft(u):
                    h, i = UNITS[u]
                    keys = (i + 1) * P
                    s = u % 2
                    for m in range(2):
                        bank = 2 * (u % 3) + m
                        act.wait_ge(S("at_max"), 2 * u + m + 1)
                        if u >= 2:
                            act.wait_ge(S("at_a"), 2 * (u - 1))
                        act.activation(tmp[:, 2 * s + m, :keys], B[bank][:, :keys], ACT.Exp, bias=stat[:, bank:bank + 1],
                                       accum_out=stat[:, 6 + 2 * s + m:7 + 2 * s + m]).then_inc(S("at_exp"), 1)

                def a_turned(u):
                    keys = (UNITS[u][1] + 1) * P
                    act.wait_ge(S("at_t"), u + 1)
                    if u >= 2:
                        act.wait_ge(S("at_pv"), u - 1)
                    act.copy(aT[:, u % 2, :keys], B[6][:, :keys]).then_inc(S("at_t_out"), 1)

                def o_out(u):
                    h, i = UNITS[u]
                    act.wait_ge(S("at_pv"), u + 1)
                    done(act.copy(o_tok[:, i, h * P:(h + 1) * P], B[7][:, 0:P]))
                    act.activation(rstd[:, 0:P], o_tok[:, i, h * P:(h + 1) * P], ACT.Square,
                                   accum_out=stat[:, 16 + i * HEADS + h:17 + i * HEADS + h]).then_inc(S("at_o"), 1)

                soft(0)
                for u in range(len(UNITS)):
                    if u + 1 < len(UNITS):
                        soft(u + 1)
                    a_turned(u)
                    if u:
                        o_out(u - 1)
                o_out(len(UNITS) - 1)
                act.wait_ge(S("at_o"), len(UNITS))
                act.activation(stat[:, 16:48], stat[:, 16:48], ACT.Sqrt, scale=1.0 / P, bias=eps_col).then_inc(S("at_root"), 1)
                for h in range(HEADS):
                    act.wait_ge(S("yb_h"), h + 1)
                    act.copy(yb_hi[:, h, :], tmp[:, h % 4, :]).then_inc(S("yb_hi_out"), 1)

                def parts(name, evacuate=None):
                    n, panels, outs = PART[name]
                    for i in range(panels):
                        if n + i + 2 != BASE["ffn2"] + 1:
                            split(n + i + 2)
                        if evacuate:
                            for t in range(outs // panels):
                                evacuate(i * outs // panels + t)

                def m_hi_out(t):
                    act.wait_ge(S("m_h"), t + 1)
                    act.copy(m_hi[:, t, :], tmp[:, t % 4, :]).then_inc(S("m_hi_out"), 1)

                parts("b_proj", m_hi_out)
                parts("w_out")

            if "ffn2" in stages:
                norm("n2", x, lambda eng, k: wait_x(eng, "mixer", k), panel=BASE["ffn2"] + 1)
                swiglu("ffn2")

                down("ffn2")

            if "mix2" in stages:
                s5_b = [inp[f"ssm_b_{part}_2"].rearrange("o (s two) n h -> (two n) (o s) h", two=2) for part in ("re", "im")]
                wait_x(act, "ffn2", KD - 1)
                for i in range(2):
                    act.dma_start(b_in[:, i], s5_b[i]).then_inc(S("s5_landed"), 16)
                    c_v = inp[f"ssm_c_{('re', 'im')[i]}_2"].rearrange("o (c g) h n -> (g h) (o c) n", c=4)
                    for twice in range(2):
                        act.dma_start(c_in[:, i, :, twice, :], c_v).then_inc(S("s5_landed"), 16)
                act.wait_ge(S("band_stored"), 16)
                act.dma_start(hank[:], bass.AP(band_dram, 0, [[1, P], [BAND, NQ], [1, 2 * P]])).then_inc(S("hank_landed"), 16)
                act.wait_ge(S("mod_made"), 2)
                norm("p1", x, lambda eng, k: wait_x(eng, "ffn2", k), panel=BASE["mix2"] + 1, shift=lambda k: mod[:, k:k + 1])
                n = PART["u2"][0]
                for i in range(2):
                    for t in range(2):
                        if t == 1:
                            split(n + i + 2)
                        act.wait_ge(S("pe_done"), used(n + i, 2 * t + 2))
                        act.copy(u2[:, 2 * i + t, :], bank_of(2 * i + t)[:]).then_inc(S("u2_out"), 1)
                def flipped():
                    for g in range(4):
                        act.wait_ge(S("bias_flipped"), g + 1)
                        act.copy(bias[:, 2 * g:2 * g + 2, :], B[4 + g][:].rearrange("p (h k) -> p h k", h=2)).then_inc(S("bias_out"), 1)

                def s5_inputs(part):
                    for g in range(4 * part, 4 * part + 4):
                        act.wait_ge(S("bb_t"), g + 1)
                        act.copy(bbT[:, part, 4 * (g % 4):4 * (g % 4) + 4, :],
                                 B[4 + g % 4][:].rearrange("p (s c) -> p s c", s=4)).then_inc(S("bb_t_out"), 1)

                n = PART["q2"][0]
                split(n + 2)
                for b in range(TB):
                    if b == TB - 1:
                        split(n + 3)
                    act.wait_ge(S("pe_done"), used(n + 1, b + 1))
                    act.copy(q2_raw[:, b, :], B[b][:]).then_inc(S("q2_out"), 1)
                act.wait_ge(S("q2_out"), TB)
                act.activation(q_sq[:], q2_raw[:], ACT.Square).then_inc(S("qk2_sq"), 1)
                s5_inputs(0)
                n = PART["kv2"][0]
                for b in range(TB):
                    act.wait_ge(S("pe_done"), used(n, b + 1))
                    act.copy(k2_raw[:, b, :], B[b][:, 0:NKV * QK]).then_inc(S("k2_out"), 1)
                    for twice in range(2):
                        act.copy(v2[:, b, :, twice, :], B[b][:, NKV * QK:2 * NKV * QK].rearrange("p (n d) -> p n d", n=NKV)).then_inc(S("v2_out"), 1)
                act.wait_ge(S("k2_out"), TB)
                act.activation(k_sq[:], k2_raw[:], ACT.Square).then_inc(S("qk2_sq"), 1)
                split(n + 2)
                flipped()
                act.wait_ge(S("qk2_ssq"), 2)
                act.activation(stat[:, 0:40], stat[:, 0:40], ACT.Sqrt, scale=1.0 / QK, bias=eps_col).then_inc(S("qk2_root"), 1)
                s5_inputs(1)
                for f in range(6):
                    act.wait_ge(S("qk2_t"), f + 1)
                    dst = q2T[:, f, :] if f < 4 else k2T[:, f - 4, :]
                    act.copy(dst, B[5 + f % 2][:]).then_inc(S("qk2_t_out"), 1)
                def sw_exp(u):
                    b, n = SW_UNITS[u]
                    lo = P if b == 0 else 0
                    act.wait_ge(S("sw_max"), u + 1)
                    for h in range(4):
                        p = prob[:, u % 2, h, lo:]
                        act.activation(p, p, ACT.Exp, bias=sw_cols(48, u)[:, h:h + 1], accum_out=sw_cols(56, u)[:, h:h + 1]).then_inc(S("sw_exp"), 1)
                    act.activation(sw_cols(64, u), sw_cols(64, u), ACT.Exp).then_inc(S("sw_exp"), 1)

                def sw_turned(u):
                    if u >= 2:
                        act.wait_ge(S("sw_pv"), u - 1)
                    for i, kb in enumerate(SW_BLOCKS[u]):
                        act.wait_ge(S("sw_t"), SW_BEFORE[u] + i + 1)
                        act.copy(pT[:, u % 2, kb, :], B[5 + kb][:]).then_inc(S("sw_t_out"), 1)

                def sw_out(u):
                    b, n = SW_UNITS[u]
                    act.wait_ge(S("sw_pv"), u + 1)
                    o = B[7][:].rearrange("p (j two q) -> p j two q", j=2, two=2)
                    for half in range(2):
                        rows_of = slice(64 * half, 64 * half + 64)
                        act.copy(yat[rows_of, 2 * n:2 * n + 2, b * P:(b + 1) * P], o[rows_of, :, half, :]).then_inc(S("sw_out"), 1)

                def s5_gelu(tiles):
                    for t in tiles:
                        act.wait_ge(S("s5_y"), t + 1)
                        act.activation(u2[:, t, :], u2[:, t, :], ACT.Gelu_apprx_tanh).then_inc(S("z_out"), 1)
                    for t in tiles:
                        act.wait_ge(S("z_out"), t + 1)
                        act.copy(z_hi[:, t, :], u2[:, t, :]).then_inc(S("z_hi_out"), 1)

                for u in range(len(SW_UNITS)):
                    sw_exp(u)
                    if u == len(SW_UNITS) - 1:
                        act.wait_ge(S("bu"), 2 * NS)
                        s5_gelu(range(3))
                    sw_turned(u)
                    sw_out(u)
                s5_gelu((3,))
                norm("pa", yat, None, hi=h_hi[:, 4:8], width=T)
                n = PART["glu"][0]
                split(n + 2)
                for t in range(4):
                    act.wait_ge(S("pe_done"), used(n, t + 1))
                    act.activation(gate[:, t, :], glu_bank(t)[:], ACT.Sigmoid, bias=col("b_glu_2", t)).then_inc(S("glu_gate"), 1)
                norm("ps", u2, lambda eng, k: eng.wait_ge(S("glu_out"), k + 1), hi=h_hi[:, 0:4], width=T)
                n = PART["w_out2"][0]
                for i in range(3):
                    split(n + i + 2)

            if "ffn3" in stages:
                norm("p2", x, lambda eng, k: wait_x(eng, "mix2", k), panel=BASE["ffn3"] + 1, shift=lambda k: mod[:, 24 + k:25 + k])
                base = BASE["ffn3"]
                with act.Fori(0, GU_STEPS) as i:
                    for half in range(2):
                        split(i * 2 + (base + 2 + half), base + half)
                        for t in range(2):
                            act.wait_ge(S("pe_done"), i * 8 + (4 * base + 4 * half + 2 * t + 2))
                            act.wait_ge(S("hid"), i * 2 + (HID["ffn3"] + t + 1))
                            act.activation(tmp[:, 2 * half + t, :], B[2 * half + t][:], ACT.Identity,
                                           scale=col_at("conv_w_2:2", i * 2, KF * half + t),
                                           bias=col_at("conv_b_2", i * 2, KF * half + t)).then_inc(S("ffn3_own"), 1)
                    for t in range(2):
                        act.wait_ge(S("ffn3_conv"), i * 8 + (2 * t + 14))
                        act.activation(tmp[:, 2 + t, :], tmp[:, 2 + t, :], ACT.Silu).then_inc(S("silu"), 1)
                    for t in range(2):
                        act.wait_ge(S("hid"), i * 2 + (HID["ffn3"] + t + 3))
                        act.copy(hid_hi[:, bass.ds(i * 2 + t, 1), :], tmp[:, 4 + t:5 + t, :]).then_inc(S("hid_hi"), 1)
                down("ffn3")
            for b in range(TB):
                act.wait_ge(S("out_t"), 2 * b + 2)
                act.copy(x_in[:, b, T:D], B[4 + (2 * b + 1) % 4][:]).then_inc(S("out_turned1"), 1)

        @block.vector
        def _(dve):
            done = Steps(dve, S("dve_done"))

            def split(n, i=None):
                if i is None:
                    if n >= end:
                        return
                    i = n
                dve.wait_ge(S("w_hi_done"), n + 1)
                if not isinstance(n, int) or n:
                    dve.wait_ge(S("w_split"), n)
                s = i % 2
                dve.tensor_tensor(w_lo[s][:], w_raw[s][:], w_hi[s][:].bitcast(F32), ALU.subtract).then_inc(S("w_split"), 1)

            def norm(name, tiles, gain, shift=None, hi=None, lo=None, width=D):
                hi, lo = (h_hi, h_lo) if hi is None else (hi, lo)
                count, at = NORM_PARTS[name][0], NORM[name]
                v, vr = tmp[:, 0, :], tmp[:, 1, :]
                eps = eps_width_col[width]
                dve.wait_ge(S("norm_root"), NORMS.index(name) + 1)
                done(dve.scalar_tensor_tensor(v, B[7][:], eps, rstd[:], ALU.add, ALU.mult))
                done(dve.scalar_tensor_tensor(vr, v, -0.5 / width, rstd[:], ALU.mult, ALU.mult))
                done(dve.scalar_tensor_tensor(rstd[:], vr, 1.5, rstd[:], ALU.add, ALU.mult))
                for k in range(count + 1):
                    if k < count:
                        if k >= 4:
                            dve.wait_ge(S("norm_split"), at + k - 3)
                        dve.scalar_tensor_tensor(tmp[:, 2 + k % 4, :], tiles[:, k, :], gain(k), rstd[:],
                                                 ALU.mult, ALU.mult).then_inc(S("norm_h"), 1)
                    if k:
                        dve.wait_ge(S("norm_hi"), at + k)
                        h, hi_k = tmp[:, 2 + (k - 1) % 4, :], hi[:, k - 1, :].bitcast(F32)
                        if shift is None:
                            ins = dve.tensor_tensor(lo[:, k - 1, :], h, hi_k, ALU.subtract)
                        else:
                            ins = dve.scalar_tensor_tensor(lo[:, k - 1, :], h, shift(k - 1), hi_k, ALU.add, ALU.subtract)
                        ins.then_inc(S("norm_split"), 1)

            def hid_lo_of(name, i, t, slot):
                dve.wait_ge(S("hid_hi"), i * 2 + (HID[name] + t + 1))
                dve.tensor_tensor(hid_lo[:, bass.ds(i * 2 + t, 1), :], tmp[:, slot:slot + 1, :],
                                  hid_hi[:, bass.ds(i * 2 + t, 1), :].bitcast(F32), ALU.subtract).then_inc(S("hid_split"), 1)

            def turns(st):
                fh_c, fl_c = (s5[:, row, bass.ds(st, 1)] for row in (13, 14))
                r = rot_r[:]
                dve.wait_ge(S("rot_read"), st + 1)
                dve.tensor_scalar(rot_n[:], rot_t[:], fh_c, ROUND, ALU.mult, ALU.add).then_inc(S("rot_step"), 1)
                dve.tensor_scalar(r, rot_t[:], fh_c, None, ALU.mult).then_inc(S("rot_step"), 1)
                dve.wait_ge(S("rot_step"), st * 5 + 2)
                dve.scalar_tensor_tensor(r, rot_n[:], ROUND, r, ALU.subtract, ALU.subtract).then_inc(S("rot_step"), 1)
                dve.wait_ge(S("rot_step"), st * 5 + 3)
                dve.scalar_tensor_tensor(r, rot_t[:], fl_c, r, ALU.mult, ALU.subtract).then_inc(S("rot_step"), 1)
                dve.wait_ge(S("rot_step"), st * 5 + 4)
                dve.tensor_scalar(rot_n[:], r, 1.0, ROUND, ALU.mult, ALU.add).then_inc(S("rot_step"), 1)
                dve.wait_ge(S("rot_step"), st * 5 + 5)
                dve.scalar_tensor_tensor(r, rot_n[:], ROUND, r, ALU.subtract, ALU.subtract).then_inc(S("rot_turns"), 1)

            def modulation(g):
                dve.wait_ge(S("mod_acc_free"), g + 1)
                for k in range(KD):
                    dve.wait_ge(S(f"mod_landed{k % MOD_SLOTS}"), g * 32 + (k // MOD_SLOTS + 1) * 16)
                    if k == 0:
                        ins = dve.tensor_scalar(mod_acc[:], mod_raw[:, k % MOD_SLOTS, :], small[:, k:k + 1], None, ALU.mult)
                    else:
                        dve.wait_ge(S("mod_step"), g * KD + (k + MOD_SLOTS))
                        ins = dve.scalar_tensor_tensor(mod_acc[:], mod_raw[:, k % MOD_SLOTS, :], small[:, k:k + 1], mod_acc[:], ALU.mult, ALU.add)
                    ins.then_inc(S("mod_step"), 1)

            def swiglu(name):
                base = BASE[name]
                dve.wait_ge(S("rot_t_made"), 1 + list(PHASES).index(name))
                for start, stop, mods, rots in PHASES[name]:
                    if not rots:
                        groups = sum(b - a for f in list(PHASES)[:list(PHASES).index(name) + 1] for a, b, m, _ in PHASES[f] if m)
                        dve.wait_ge(S("mod_acc_free"), groups + 1)
                    with dve.Fori(start, stop) as i:
                        if rots:
                            turns(i + BESIDE_AT[name])
                        if mods:
                            modulation(i + BESIDE_AT[name])
                        split(i * 2 + (base + 2), base)
                        for t in range(2):
                            dve.wait_ge(S("pe_done"), i * 8 + (4 * base + 4 + 2 * t + 2))
                            dve.wait_ge(S("silu"), i * 2 + (HID[name] + t + 3))
                            dve.wait_ge(S("hid_split"), i * 2 + (HID[name] + t + 1))
                            dve.tensor_tensor(tmp[:, 2 + t, :], tmp[:, t, :], B[2 + t][:], ALU.mult).then_inc(S("hid"), 1)
                        split(i * 2 + (base + 3), base + 1)
                        for t in range(2):
                            hid_lo_of(name, i, t, 2 + t)
                first = 4 * BESIDE_AT[name]
                last_col = 4 * groups
                dve.tensor_tensor(mod[:, first:last_col], B[6][:, 0:last_col - first], cols("b_mod_2")[:, first:last_col],
                                  ALU.add).then_inc(S("mod_made"), 1)

            def down(name, factor):
                base = BASE[name] + 2 * GU_STEPS
                for c in range(DOWN_PANELS):
                    if c % 4 == 3:
                        for k in (c // 4 * 2, c // 4 * 2 + 1):
                            dve.wait_ge(S("pe_done"), used(base + c, 2 * (k % 2) + 2))
                            dve.scalar_tensor_tensor(x[:, k, :], bank_of(k)[:], factor(k), x[:, k, :], ALU.mult, ALU.add).then_inc(S(name + "_x"), 1)
                    if c < DOWN_PANELS - 1:
                        split(base + c + 2)

            dve.sem_inc(S("hid"), 2)
            dve.sem_inc(S("hid_split"), 2)
            for name in ("ffn1", "ffn2", "ffn3"):
                dve.sem_inc(S(name + "_x"), 4)
            dve.sem_inc(S("ffn3_conv"), 8)
            dve.sem_inc(S("mod_step"), MOD_SLOTS)
            for i, value in ((20, EPS), (21, math.pi / 2.0)):
                done(dve.memset(small[:, i:i + 1], value))
            dve.memset(small[:, 22:23], LN_EPS).then_inc(S("cols_made"), 1)
            dve.wait_ge(S("rows_t"), 3)
            for tile in range(3):
                dve.tensor_copy(vec[:, tile, :ROW_COUNTS[tile]], B[0][:, tile * P:tile * P + ROW_COUNTS[tile]]).then_inc(S("vec_made"), 1)
            for k in range(KD):
                dve.wait_ge(S("x_t"), k + 1)
                dve.tensor_copy(x[:, k, :], B[4 + k % 4][:]).then_inc(S("x_turned"), 1)
            split(0)
            split(1)
            dve.wait_ge(S("vec_made"), 3)
            norm("n1", x, lambda k: col("ffn1_norm", k))
            dve.wait_ge(S("band_t"), 1)
            dve.tensor_copy(band[:], B[1][0:NQ, 0:BAND]).then_inc(S("band_made"), 1)

            dve.wait_ge(S("spread_landed"), 16 * 11)
            for i in range(2):
                done(dve.tensor_tensor(lam_in[:, 2 * i, :], lam_in[:, 2 * i, :], lam_in[:, 2 * i + 1, :], ALU.mult))
                ins = dve.tensor_reduce(small[:, 8 + i:9 + i], lam_in[:, 2 * i, :], AX.X, ALU.add)
                if i == 0:
                    done(ins)
            ins.then_inc(S("prep_v"), 1)
            for i in (0, 2):
                done(dve.tensor_scalar(gains[:, i, :], gains[:, i, :], QK**-0.5, None, ALU.mult))
            lr, dt, mag, th, n_, sn, cs, fh, fl, tv, t2, a_re, a_im, f_re, f_im = (
                s5[:, i, :] for i in (0, 2, 3, 4, 5, 6, 7, 13, 14, 15, 16, 8, 9, 11, 12))
            li = cols("lam_im_2")
            done(dve.tensor_scalar(lr, cols("lam_re_2"), -1e-4, None, ALU.min))
            dve.wait_ge(S("prep_a"), 3)
            done(dve.tensor_tensor(th, dt, li, ALU.mult))
            dve.tensor_tensor(tv, dt, lr, ALU.mult).then_inc(S("prep_v"), 1)

            def reduce_angle(a, n):
                done(dve.tensor_scalar(n, a, 1.0 / TWO_PI, ROUND, ALU.mult, ALU.add))
                done(dve.tensor_scalar(n, n, ROUND, None, ALU.subtract))
                for part in (PI_1, PI_2, PI_3):
                    done(dve.scalar_tensor_tensor(a, n, -part, a, ALU.mult, ALU.add))

            reduce_angle(th, n_)
            done(dve.tensor_scalar(fh, th, 2.0**15 / TWO_PI, ROUND, ALU.mult, ALU.add))
            done(dve.tensor_scalar(fh, fh, ROUND, 2.0**-15, ALU.subtract, ALU.mult))
            done(dve.tensor_copy(fl, th))
            for part in (PI_1, PI_2, PI_3):
                done(dve.scalar_tensor_tensor(fl, fh, -part, fl, ALU.mult, ALU.add))
            done(dve.tensor_scalar(fl, fl, 1.0 / TWO_PI, None, ALU.mult))
            done(dve.tensor_scalar(th, th, PI_LOW, -PI_LOW, ALU.min, ALU.max))
            posf = stat[:, 0:TB]
            done(dve.tensor_copy(posf, pos_i[:]))
            for r in range(ROT):
                inv = float(np.float32(500000.0) ** np.float32(-np.float32(2 * r) / np.float32(2 * ROT)))
                done(dve.tensor_scalar(ang[:, 0, :, r], posf, inv, None, ALU.mult))
            reduce_angle(ang[:, 0], ang[:, 1])
            dve.tensor_scalar(ang[:, 0], ang[:, 0], PI_LOW, -PI_LOW, ALU.min, ALU.max).then_inc(S("prep_v"), 1)
            neg_lam = small[:, 12:13]
            dve.wait_ge(S("prep_a"), 9)
            done(dve.tensor_tensor(neg_lam, small[:, 11:12], small[:, 10:11], ALU.subtract))
            done(dve.tensor_scalar(neg_lam, neg_lam, -LAM_INIT, None, ALU.add))
            done(dve.tensor_tensor(a_re, mag, cs, ALU.mult))
            done(dve.tensor_tensor(a_im, mag, sn, ALU.mult))
            done(dve.tensor_scalar(a_re, a_re, -1.0, None, ALU.add))
            done(dve.tensor_tensor(tv, lr, lr, ALU.mult))
            done(dve.tensor_tensor(t2, li, li, ALU.mult))
            done(dve.tensor_tensor(tv, tv, t2, ALU.add))
            done(dve.reciprocal(tv, tv))
            done(dve.tensor_tensor(f_re, a_re, lr, ALU.mult))
            done(dve.tensor_tensor(t2, a_im, li, ALU.mult))
            done(dve.tensor_tensor(f_re, f_re, t2, ALU.add))
            done(dve.tensor_tensor(f_re, f_re, tv, ALU.mult))
            done(dve.tensor_tensor(f_im, a_im, lr, ALU.mult))
            done(dve.tensor_tensor(t2, a_re, li, ALU.mult))
            done(dve.tensor_tensor(f_im, f_im, t2, ALU.subtract))
            done(dve.tensor_tensor(f_im, f_im, tv, ALU.mult))

            swiglu("ffn1")

            down("ffn1", lambda k: 0.5)

            if "mixer" in stages:
                norm("nm", x, lambda k: col("mix_norm", k))

                def part_splits(name):
                    n, panels, _ = PART[name]
                    for i in range(panels):
                        split(n + i + 2)

                def spread(ap, shape):
                    return ap.unsqueeze(2).to_broadcast(shape)

                part_splits("v_gm")
                dve.wait_ge(S("v_gm_out"), TB)
                for b in range(TB):
                    done(dve.bn_stats(tmp[:, 4, 6 * b:6 * b + 6], vg[:, b, :]))
                    done(dve.bn_aggr(tmp[:, 5, 2 * b:2 * b + 2], tmp[:, 4, 6 * b:6 * b + 6]))
                dve.tensor_copy(stat[:, 36:40], tmp[:, 5, 1:2 * TB:2]).then_inc(S("ln_var"), 1)
                part_splits("u_gm")
                dve.wait_ge(S("ln_root"), 1)
                done(dve.reciprocal(stat[:, 40:44], stat[:, 40:44]))
                dve.wait_ge(S("ln_landed"), 32)
                for b in range(TB):
                    done(dve.tensor_scalar(vg[:, b, :], vg[:, b, :], tmp[:, 5, 2 * b:2 * b + 1], stat[:, 40 + b:41 + b],
                                           ALU.subtract, ALU.mult))
                    done(dve.tensor_tensor(vg[:, b, :], vg[:, b, :], ln_g[:], ALU.mult))
                    dve.tensor_tensor(vg[:, b, :], vg[:, b, :], ln_b[:], ALU.add).then_inc(S("ln_out"), 1)

                def heads(j):
                    raw = qk_raw[j % 2][:].rearrange("p b (h d) -> p (b h) d", d=QK)
                    n = TB * HEADS
                    dve.wait_ge(S("qk_sq"), j + 1)
                    dve.tensor_reduce(stat[:, 0:n], tmp[:, 0:4, :].rearrange("p b (h d) -> p (b h) d", d=QK), AX.X, ALU.add).then_inc(S("qk_ssq"), 1)
                    dve.wait_ge(S("qk_root"), j + 1)
                    done(dve.reciprocal(stat[:, 0:n], stat[:, 0:n]))
                    done(dve.tensor_tensor(raw, raw, spread(stat[:, 0:n], [P, n, QK]), ALU.mult))
                    done(dve.tensor_tensor(raw, raw, gains[:, j // 2:j // 2 + 1, :].to_broadcast([P, n, QK]), ALU.mult))
                    raw4 = qk_raw[j % 2][:].rearrange("p b (h d) -> p b h d", d=QK)
                    r1, r2 = raw4[:, :, :, 0:ROT], raw4[:, :, :, ROT:2 * ROT]
                    shape = [P, TB, HEADS, ROT]
                    cos_b, sin_b = (a[:].unsqueeze(2).to_broadcast(shape) for a in (cos_t, sin_t))
                    t = [tmp[:, 0, 256 * (i % 2):256 * (i % 2) + 256] if i < 2 else tmp[:, 1, 256 * (i % 2):256 * (i % 2) + 256] for i in range(4)]
                    t = [a.rearrange("p (b h d) -> p b h d", b=TB, h=HEADS) for a in t]
                    dve.wait_ge(S("qk_ssq"), j + 1)
                    done(dve.tensor_tensor(t[0], r1, cos_b, ALU.mult))
                    done(dve.tensor_tensor(t[1], r2, sin_b, ALU.mult))
                    done(dve.tensor_tensor(t[2], r2, cos_b, ALU.mult))
                    done(dve.tensor_tensor(t[3], r1, sin_b, ALU.mult))
                    done(dve.tensor_tensor(r1, t[0], t[1], ALU.subtract))
                    dve.tensor_tensor(r2, t[2], t[3], ALU.add).then_inc(S("qk_done"), 1)

                def gmlp():
                    dve.wait_ge(S("bs_landed"), 32)
                    dve.wait_ge(S("u_gm_out"), 4)
                    for f in range(4):
                        y = tmp[:, 4 + f % 2, :]
                        dve.wait_ge(S("f_done"), f + 1)
                        dve.tensor_tensor(y.rearrange("p (c t) -> p c t", c=TB), B[4 + f][:].rearrange("p (c t) -> p c t", c=TB),
                                          bs[:, f:f + 1, :].to_broadcast([P, TB, P]), ALU.add).then_inc(S("ya_h"), 1)
                        dve.wait_ge(S("ya_h"), 2 * f + 1)
                        dve.tensor_tensor(y, y, u_g[:, f, :], ALU.mult).then_inc(S("ya_h"), 1)
                        dve.wait_ge(S("ya_hi_out"), f + 1)
                        dve.tensor_tensor(ya_lo[:, f, :], y, ya_hi[:, f, :].bitcast(F32), ALU.subtract).then_inc(S("ya_split"), 1)

                for j in range(3):
                    part_splits(f"qk{j}")
                    if j == 2:
                        gmlp()
                    heads(j)
                part_splits("v0")
                part_splits("qk3")
                heads(3)
                part_splits("v1")
                part_splits("g_a")
                n = PART["a_proj"][0]
                for i in range(2):
                    for t in range(4):
                        dve.wait_ge(S("pe_done"), used(n + i, t + 1))
                        g = ga[:, 4 * i + t, :]
                        dve.wait_ge(S("g_a_out"), 4 * i + t + 1)
                        dve.tensor_tensor(g, g, bank_of(t)[:], ALU.mult).then_inc(S("a_proj_out"), 1)
                    split(n + i + 2)
                part_splits("g_b")

                def row_max(u):
                    keys = (UNITS[u][1] + 1) * P
                    for m in range(2):
                        bank = 2 * (u % 3) + m
                        dve.wait_ge(S("at_s"), 2 * u + m + 1)
                        dve.tensor_reduce(stat[:, bank:bank + 1], B[bank][:, :keys], AX.X, ALU.max,
                                          negate=True).then_inc(S("at_max"), 1)

                def differ(u):
                    keys = (UNITS[u][1] + 1) * P
                    s = u % 2
                    r = stat[:, 10 + 2 * s:12 + 2 * s]
                    dve.wait_ge(S("at_exp"), 2 * u + 2)
                    done(dve.reciprocal(r, stat[:, 6 + 2 * s:8 + 2 * s]))
                    done(dve.tensor_tensor(r[:, 1:2], r[:, 1:2], neg_lam, ALU.mult))
                    if u >= 2:
                        dve.wait_ge(S("at_t"), u - 1)
                    a = tmp[:, 4 + s, :keys]
                    dve.tensor_scalar(a, tmp[:, 2 * s, :keys], r[:, 0:1], None, ALU.mult).then_inc(S("at_a"), 1)
                    dve.wait_ge(S("at_a"), 2 * u + 1)
                    dve.scalar_tensor_tensor(a, tmp[:, 2 * s + 1, :keys], r[:, 1:2], a, ALU.mult, ALU.add).then_inc(S("at_a"), 1)

                row_max(0)
                row_max(1)
                for u in range(len(UNITS)):
                    differ(u)
                    if u + 2 < len(UNITS):
                        row_max(u + 2)
                dve.wait_ge(S("at_root"), 1)
                done(dve.reciprocal(stat[:, 16:48], stat[:, 16:48]))
                root = stat[:, 16:48].rearrange("p (i h) -> p i h", i=TB)

                def scale(h):
                    o = o_tok[:, :, h * P:(h + 1) * P]
                    dve.tensor_tensor(o, o, root[:, :, h:h + 1].to_broadcast([P, TB, P]), ALU.mult).then_inc(S("o_scaled"), 1)

                scale(0)
                scale(1)
                for h in range(HEADS + 1):
                    if h < HEADS:
                        if h >= 4:
                            dve.wait_ge(S("yb_split"), h - 3)
                        dve.wait_ge(S("yb_t"), h + 1)
                        dve.tensor_scalar(tmp[:, h % 4, :], B[4 + h % 4][:], col("b_subln", 0), 1.0 - LAM_INIT, ALU.mult, ALU.mult).then_inc(S("yb_h"), 1)
                    if h + 2 < HEADS:
                        scale(h + 2)
                    if h:
                        dve.wait_ge(S("yb_hi_out"), h)
                        dve.tensor_tensor(yb_lo[:, h - 1, :], tmp[:, (h - 1) % 4, :], yb_hi[:, h - 1, :].bitcast(F32), ALU.subtract).then_inc(S("yb_split"), 1)
                n, panels, _ = PART["b_proj"]
                for i in range(panels):
                    for t in range(2 * i, 2 * i + 2):
                        y = tmp[:, t % 4, :]
                        dve.wait_ge(S("pe_done"), used(n + i, 2 * (t % 2) + 2))
                        if t >= 4:
                            dve.wait_ge(S("m_split"), t - 3)
                        dve.tensor_tensor(y, gb[:, t, :], bank_of(t)[:], ALU.mult).then_inc(S("b_proj_out"), 1)
                        dve.wait_ge(S("b_proj_out"), t + 1)
                        dve.tensor_tensor(y, y, ga[:, t, :], ALU.add).then_inc(S("m_h"), 1)
                    split(n + i + 2)
                    for t in range(2 * i, 2 * i + 2):
                        dve.wait_ge(S("m_hi_out"), t + 1)
                        dve.tensor_tensor(m_lo[:, t, :], tmp[:, t % 4, :], m_hi[:, t, :].bitcast(F32), ALU.subtract).then_inc(S("m_split"), 1)
                n, panels, _ = PART["w_out"]
                for i in range(panels):
                    for t in range(2 * i, 2 * i + 2):
                        dve.wait_ge(S("pe_done"), used(n + i, 2 * (t % 2) + 2))
                        dve.tensor_tensor(x[:, t, :], x[:, t, :], bank_of(t)[:], ALU.add).then_inc(S("mixer_x"), 1)
                    if i < panels - 1:
                        split(n + i + 2)

            if "ffn2" in stages:
                norm("n2", x, lambda k: col("ffn2_norm", k))
                swiglu("ffn2")

                down("ffn2", lambda k: 0.5)

            if "mix2" in stages:
                dve.wait_ge(S("mod_made"), 2)
                for i, name in enumerate(("norm1_w_2", "norm2_w_2")):
                    at = 8 + 24 * i
                    done(dve.scalar_tensor_tensor(gain2[:, i, :], mod[:, at:at + 8], 1.0, cols(name), ALU.add, ALU.mult))
                norm("p1", x, lambda k: gain2[:, 0, k:k + 1], lambda k: mod[:, k:k + 1])
                n, panels, _ = PART["u2"]
                for i in range(panels):
                    split(n + i + 2)
                dve.wait_ge(S("s5_landed"), 96)
                shape = [P, NS, SG]
                f_re_b, f_im_b = (s5[:, row, :].unsqueeze(2).to_broadcast(shape) for row in (11, 12))
                t = [tmp[:, 4, 256 * i:256 * i + 256].rearrange("p (s h) -> p s h", s=NS) for i in range(2)]
                for part, (first, second, op) in enumerate(((0, 1, ALU.subtract), (1, 0, ALU.add))):
                    done(dve.tensor_tensor(t[0], b_in[:, first], f_re_b, ALU.mult))
                    done(dve.tensor_tensor(t[1], b_in[:, second], f_im_b, ALU.mult))
                    done(dve.tensor_tensor(bb[:, part], t[0], t[1], op))
                def blocks(part):
                    for s4 in range(4):
                        for half in range(2):
                            own = slice(64 * half, 64 * half + 64)
                            at = s4 * 2 * SG + half * SG
                            dve.tensor_copy(bd[own, s4::4, at:at + SG], bb[own, part, s4::4, :]).then_inc(S("bd_made"), 1)

                dve.wait_ge(S("zeroed"), 1)
                blocks(0)
                n = PART["q2"][0]
                split(n + 2)
                split(n + 3)
                dve.wait_ge(S("bb_t"), 4)
                blocks(1)
                dve.wait_ge(S("qk2_sq"), 1)
                dve.tensor_reduce(stat[:, 0:32], q_sq[:].rearrange("p b (h d) -> p (b h) d", d=QK), AX.X, ALU.add).then_inc(S("qk2_ssq"), 1)
                dve.wait_ge(S("qk2_sq"), 2)
                dve.tensor_reduce(stat[:, 32:40], k_sq[:].rearrange("p b (h d) -> p (b h) d", d=QK), AX.X, ALU.add).then_inc(S("qk2_ssq"), 1)
                split(PART["kv2"][0] + 2)
                dve.wait_ge(S("qk2_root"), 1)
                done(dve.reciprocal(stat[:, 0:40], stat[:, 0:40]))
                q_v = q2_raw[:].rearrange("p b (h d) -> p (b h) d", d=QK)
                k_v = k2_raw[:].rearrange("p b (h d) -> p (b h) d", d=QK)
                done(dve.tensor_tensor(q_v, q_v, spread(stat[:, 0:32], [P, 32, QK]), ALU.mult))
                dve.tensor_tensor(q_v, q_v, gains[:, 2:3, :].to_broadcast([P, 32, QK]), ALU.mult).then_inc(S("qk2_made"), 1)
                done(dve.tensor_tensor(k_v, k_v, spread(stat[:, 32:40], [P, 8, QK]), ALU.mult))
                dve.tensor_tensor(k_v, k_v, gains[:, 3:4, :].to_broadcast([P, 8, QK]), ALU.mult).then_inc(S("qk2_made"), 1)

                def s5_outputs():
                    dve.wait_ge(S("zeroed"), 2)
                    for part, sign in enumerate((1.0, -1.0)):
                        dve.wait_ge(S("c_t"), part + 1)
                        c_v = B[4 + 3 * part][:].rearrange("p (c n) -> p c n", c=4)
                        for s4 in range(4):
                            for half in range(2):
                                own = slice(64 * half, 64 * half + 64)
                                at = s4 * 2 * SG + half * SG
                                dve.tensor_scalar(cT[own, part, s4::4, at:at + SG], c_v[own, :, at:at + SG], sign, None, ALU.mult).then_inc(S("c_out"), 1)

                s5_outputs()
                def sw_max(u):
                    b, n = SW_UNITS[u]
                    lo = P if b == 0 else 0
                    p = prob[:, u % 2]
                    if u == 0:
                        dve.wait_ge(S("bias_out"), 4)
                    if u >= 2:
                        dve.wait_ge(S("sw_t"), SW_BEFORE[u - 1])
                    for odd in range(2):
                        first = 4 * n + odd
                        dve.wait_ge(S("sw_s"), 2 * u + odd + 1)
                        dve.tensor_tensor(p[:, odd:odd + 3:2, lo:], B[5 + odd][:].rearrange("p (h k) -> p h k", h=2)[:, :, lo:],
                                          bias[:, first:first + 3:2, lo:], ALU.add).then_inc(S("sw_read"), 1)
                    sinks = sink[:, 4 * n:4 * n + 4]
                    dve.wait_ge(S("sw_read"), 2 * u + 2)
                    done(dve.tensor_reduce(sw_cols(72, u), p[:, :, lo:], AX.X, ALU.max))
                    done(dve.tensor_tensor(sw_cols(72, u), sw_cols(72, u), sinks, ALU.max))
                    done(dve.tensor_tensor(sw_cols(64, u), sinks, sw_cols(72, u), ALU.subtract))
                    dve.tensor_scalar(sw_cols(48, u), sw_cols(72, u), -1.0, None, ALU.mult).then_inc(S("sw_max"), 1)

                def sw_scale(u):
                    lo = P if SW_UNITS[u][0] == 0 else 0
                    p = prob[:, u % 2, :, lo:]
                    dve.wait_ge(S("sw_exp"), 5 * (u + 1))
                    done(dve.tensor_tensor(sw_cols(80, u), sw_cols(56, u), sw_cols(64, u), ALU.add))
                    done(dve.reciprocal(sw_cols(80, u), sw_cols(80, u)))
                    dve.tensor_tensor(p, p, spread(sw_cols(80, u), [P, 4, 2 * P - lo]), ALU.mult).then_inc(S("sw_p"), 1)

                def scan_in(st):
                    re, im = B[2 * (st % 2)], B[2 * (st % 2) + 1]
                    r = rot[:, st % ROT_SLOTS]
                    dve.wait_ge(S("bu"), 2 * st + 2)
                    dve.wait_ge(S(f"rot_landed{st % ROT_SLOTS}"), 16 * (st // ROT_SLOTS + 1))
                    if st:
                        dve.wait_ge(S("scan_v"), 2 * st)
                    for i, (a, w) in enumerate(((re, 0), (im, 1), (im, 0), (re, 1))):
                        dve.tensor_tensor(sc_a[:, i, :], a[:], r[:, w, :], ALU.mult).then_inc(S("scan_in"), 1)

                def scan(st):
                    if st:
                        dve.wait_ge(S("scan_p"), 2 * st)
                        dve.wait_ge(S("scan_q"), 2 * st)
                    for i in range(2):
                        dve.wait_ge(S("scan_v"), 2 * st + i + 1)
                        dve.tensor_tensor_scan(sc_v[:, 2 + i, :], s5[:, 3, st:st + 1].to_broadcast([P, T]), sc_v[:, i, :], 0.0,
                                               ALU.mult, ALU.add).then_inc(S("scanned"), 1)

                def scan_out(st):
                    dve.wait_ge(S("scanned"), 2 * st + 2)
                    if st >= 2:
                        dve.wait_ge(S("y_added"), st - 1)
                    r = rot[:, st % ROT_SLOTS]
                    dve.scalar_tensor_tensor(scan_product(st, 2), sc_v[:, 3, :], -1.0, r[:, 1, :], ALU.mult, ALU.mult).then_inc(S("scan_q"), 1)
                    dve.tensor_tensor(scan_product(st, 3), sc_v[:, 3, :], r[:, 0, :], ALU.mult).then_inc(S("scan_q"), 1)

                def s5_y(c):
                    dve.wait_ge(S("y_added"), 4 * c + 4)
                    dve.scalar_tensor_tensor(u2[:, c, :], u2[:, c, :], col("ssm_d_2", c), B[4][:], ALU.mult, ALU.add).then_inc(S("s5_y"), 1)

                scan_in(0)
                for st in range(NS):
                    if st % 4 == 1 and st > 4:
                        s5_y(st // 4 - 1)
                    if st + 1 < NS:
                        scan_in(st + 1)
                    scan(st)
                    if st % 2:
                        sw_scale(st // 2)
                    scan_out(st)
                    if st % 2 == 0:
                        sw_max(st // 2)
                def z_split(tiles):
                    for t in tiles:
                        dve.wait_ge(S("z_hi_out"), t + 1)
                        dve.tensor_tensor(z_lo[:, t, :], u2[:, t, :], z_hi[:, t, :].bitcast(F32), ALU.subtract).then_inc(S("z_split"), 1)

                s5_y(3)
                z_split(range(4))
                norm("pa", yat, lambda k: col("out_norm_attn_2", k), hi=h_hi[:, 4:8], lo=h_lo[:, 4:8], width=T)
                split(PART["glu"][0] + 2)
                for t in range(4):
                    dve.wait_ge(S("glu_gate"), t + 1)
                    dve.tensor_tensor(u2[:, t, :], u2[:, t, :], gate[:, t, :], ALU.mult).then_inc(S("glu_out"), 1)
                norm("ps", u2, lambda k: col("out_norm_ssm_2", k), hi=h_hi[:, 0:4], lo=h_lo[:, 0:4], width=T)
                n, panels, _ = PART["w_out2"]
                for i in range(panels):
                    for t in range(2 * i, 2 * i + 2):
                        dve.wait_ge(S("pe_done"), used(n + i, 2 * (t % 2) + 2))
                        dve.scalar_tensor_tensor(x[:, t, :], bank_of(t)[:], mod[:, 16 + t:17 + t], x[:, t, :],
                                                 ALU.mult, ALU.add).then_inc(S("mix2_x"), 1)
                    if i < panels - 1:
                        split(n + i + 2)

            if "ffn3" in stages:
                norm("p2", x, lambda k: gain2[:, 1, k:k + 1], lambda k: mod[:, 24 + k:25 + k])
                base = BASE["ffn3"]
                with dve.Fori(0, GU_STEPS) as i:
                    for half in range(2):
                        split(i * 2 + (base + 2 + half), base + half)
                        for t in range(2):
                            up, y = B[2 * half + t], tmp[:, 2 * half + t, :]
                            dve.wait_ge(S("ffn3_own"), i * 4 + (2 * half + t + 1))
                            for back in (1, 2):
                                dve.scalar_tensor_tensor(y[:, back:], up[:, :T - back], col_at(f"conv_w_2:{2 - back}", i * 2, KF * half + t),
                                                         y[:, back:], ALU.mult, ALU.add).then_inc(S("ffn3_conv"), 1)
                                if back == 1:
                                    dve.wait_ge(S("ffn3_conv"), i * 8 + (4 * half + 2 * t + 9))
                    for t in range(2):
                        dve.wait_ge(S("silu"), i * 2 + (HID["ffn3"] + t + 3))
                        dve.wait_ge(S("hid_split"), i * 2 + (HID["ffn3"] + t + 1))
                        dve.tensor_tensor(tmp[:, 4 + t, :], tmp[:, 2 + t, :], tmp[:, t, :], ALU.mult).then_inc(S("hid"), 1)
                    for t in range(2):
                        hid_lo_of("ffn3", i, t, 4 + t)
                down("ffn3", lambda k: mod[:, 40 + k:41 + k])
            for b in range(TB):
                dve.wait_ge(S("out_t"), 2 * b + 1)
                dve.tensor_copy(x_in[:, b, 0:T], B[4 + 2 * b % 4][:]).then_inc(S("out_turned0"), 1)

        @block.tensor
        def _(pe):
            def products(out_ap, terms, first=True, last=True):
                for i, (stationary, moving) in enumerate(terms):
                    mm = pe.matmul(out_ap, stationary, moving, start=first and i == 0, stop=last and i == len(terms) - 1)
                return mm

            def feature_terms(n, k, c, at, hi, lo, wait=None, k0=0):
                wh, wl = panel(w_hi, n, k, c), panel(w_lo, n, k, c)
                for i in range(k):
                    if wait:
                        wait(i)
                    yield wh[:, i, at:at + P], hi[:, k0 + i, :]
                    yield wh[:, i, at:at + P], lo[:, k0 + i, :]
                    yield wl[:, i, at:at + P], hi[:, k0 + i, :]

            def token_terms(n, k, c, b, hi, lo, wait=None, k0=0):
                wh, wl = panel(w_hi, n, k, c), panel(w_lo, n, k, c)
                own = slice(b * P, (b + 1) * P)
                for i in range(k):
                    if wait:
                        wait(i)
                    yield hi[:, k0 + i, own], wh[:, i, :]
                    yield hi[:, k0 + i, own], wl[:, i, :]
                    yield lo[:, k0 + i, own], wh[:, i, :]

            def stream(out_ap, terms, total, first=True, last=True):
                for i, (stationary, moving) in enumerate(terms):
                    mm = pe.matmul(out_ap, stationary, moving, start=first and i == 0, stop=last and i == total - 1)
                return mm

            def norm(name):
                tiles, direct = NORM_PARTS[name]
                if direct < tiles:
                    pe.wait_ge(S("norm_added"), ADDED.index(name) + 1)
                    pe.matmul(B[7][:], ones[:], tmp[:, 0, :], start=True, stop=False).then_inc(S("norm_summed"), 1)
                for d in range(direct):
                    pe.wait_ge(S("norm_sq"), NORM_SQ[name] + d + 1)
                    square = yat_sq[:, d, :] if name == "pa" else tmp[:, 2 + d % 2, :]
                    pe.matmul(B[7][:], ones[:], square, start=direct == tiles and d == 0,
                              stop=d == direct - 1).then_inc(S("norm_summed"), 1)

            def ready(name):
                return lambda k: pe.wait_ge(S("norm_split"), NORM[name] + k + 1)

            def by_k(n, banks, hi, lo, wait=None, ks=range(KD), first=0, last=KD - 1):
                wh, wl = panel(w_hi, n, KD, PC), panel(w_lo, n, KD, PC)
                for k in ks:
                    if wait:
                        wait(k)
                    for t, bank in enumerate(banks):
                        at = slice(t * P, (t + 1) * P)
                        for i, (w, h) in enumerate(((wh, hi), (wh, lo), (wl, hi))):
                            mm = pe.matmul(bank[:], w[:, k, at], h[:, k, :], start=k == first and i == 0, stop=k == last and i == 2)
                        if k == last:
                            mm.then_inc(S("pe_done"), 2)

            def gate_up(name, h_name, free):
                base = BASE[name]
                for start, stop, mods, _ in PHASES.get(name, ((0, GU_STEPS, False, False),)):
                    with pe.Fori(start, stop) as i:
                        for half in range(2):
                            pe.wait_ge(S("w_split"), i * 2 + (base + half + 1))
                            free(i, half)
                            by_k(base + half, [B[2 * half], B[2 * half + 1]], h_hi, h_lo, ready(h_name) if half == 0 else None)
                        if mods:
                            pe.wait_ge(S("mod_step"), i * KD + (KD * (BESIDE_AT[name] + 1) + MOD_SLOTS))
                            for s4 in range(4):
                                mm = pe.matmul(B[6][:, bass.ds(i * 4 + s4, 1)], mod_acc[:, s4 * P:(s4 + 1) * P], ones[:, 0:1], start=True, stop=True)
                            mm.then_inc(S("mod_acc_free"), 1)

            def down(name):
                base = BASE[name] + 2 * GU_STEPS
                if name == "ffn3":
                    pe.wait_ge(S("ffn3_conv"), 8 * GU_STEPS + 8)
                else:
                    pe.wait_ge(S("silu"), HID[name] + KF + 2)
                with pe.Fori(0, 2) as j:
                    for c in range(8):
                        k0, kn = DOWN_K[c % 4]
                        pe.wait_ge(S("w_split"), j * 8 + (base + c + 1))
                        pe.wait_ge(S("hid_split"), HID[name] + k0 + kn + 2)
                        if c % 4 == 0:
                            pe.wait_ge(S(name + "_x"), j * 4 + (c // 4 * 2 + 2))
                        for t in range(2):
                            terms = feature_terms(base + c, kn, PC, t * P, hid_hi, hid_lo, None, k0)
                            mm = stream(B[c // 4 * 2 + t][:], terms, 3 * kn, c % 4 == 0, c % 4 == 3)
                            if c % 4 == 3:
                                mm.then_inc(S("pe_done"), 2)
                        if c % 4 < 3:
                            mm.then_inc(S("pe_done"), 4)

            pe.sem_inc(S("mod_acc_free"), 1)
            pe.wait_ge(S("pool_done"), 5)
            for k in range(KD):
                if k >= 4:
                    pe.wait_ge(S("x_turned"), k - 3)
                pe.wait_ge(S(f"x_landed{k // 4}"), 16)
                for b in range(TB):
                    mm = pe.transpose(B[4 + k % 4][:, b * P:(b + 1) * P], x_in[:, b, k * P:(k + 1) * P], ident[:])
                mm.then_inc(S("x_t"), 1)
                if k == 3:
                    pe.wait_ge(S("rows_landed"), 16 * len(ROWS))
                    for tile in range(3):
                        n = ROW_COUNTS[tile]
                        pe.transpose(B[0][:, tile * P:tile * P + n], rows[0:n, tile, :], ident[0:n, 0:n]).then_inc(S("rows_t"), 1)
                    pe.wait_ge(S("rel_landed"), 32)
                    pe.wait_ge(S("consts_made"), 1)
                    pe.matmul(B[1][0:NQ, 0:BAND], rel[:], oh[:], start=True, stop=True).then_inc(S("band_t"), 1)
            pe.wait_ge(S("x_turned"), KD)
            norm("n1")
            pe.wait_ge(S("band_made"), 1)

            def silu_free(name):
                def free(i, half):
                    pe.wait_ge(S(("silu", "hid")[half]), i * 2 + (HID[name] + 2))
                return free

            gate_up("ffn1", "n1", silu_free("ffn1"))

            down("ffn1")
            if last == "ffn1":
                pe.wait_ge(S("mod_made"), 1)

            if "mixer" in stages:
                norm("nm")

                def bank_wait(name, t, outs, before, before_outs):
                    if t >= 4:
                        pe.wait_ge(S(name), t - 3)
                    elif before:
                        pe.wait_ge(S(before), before_outs - 3 + t)

                def tokens(name, before, first=False):
                    n = PART[name][0]
                    for half in range(2):
                        pe.wait_ge(S("w_split"), n + half + 1)
                        wh, wl = panel(w_hi, n + half, 4, T), panel(w_lo, n + half, 4, T)
                        if first and half == 0:
                            for k in range(4):
                                pe.wait_ge(S("norm_split"), NORM["nm"] + k + 1)
                                for b in range(TB):
                                    own = slice(b * P, (b + 1) * P)
                                    for i, (h, w) in enumerate(((h_hi, wh), (h_hi, wl), (h_lo, wh))):
                                        mm = pe.matmul(B[b][:], h[:, k, own], w[:, k, :], start=k == 0 and i == 0, stop=False)
                            mm.then_inc(S("pe_done"), 4)
                            continue
                        for b in range(TB):
                            if half == 0 and before:
                                pe.wait_ge(S(before[0]), before[1] - 3 + b)
                            if first and b == 0:
                                pe.wait_ge(S("norm_split"), NORM["nm"] + KD)
                            mm = stream(B[b][:], token_terms(n + half, 4, T, b, h_hi, h_lo, None, 4 * half), 12, half == 0, half == 1)
                            if half:
                                mm.then_inc(S("pe_done"), 1)
                        if half == 0:
                            mm.then_inc(S("pe_done"), 4)

                def features(name, evac, before, hi, lo, wait=None, start=0):
                    n, panels, outs = PART[name]
                    for t in range(start, outs):
                        i, per = divmod(t, outs // panels)
                        if per == 0:
                            pe.wait_ge(S("w_split"), n + i + 1)
                        if t >= 4:
                            pe.wait_ge(S(evac), t - 3)
                        elif before:
                            pe.wait_ge(S(before[0]), before[1] - 3 + t)
                        k, c = (4, T) if outs // panels == 4 else (KD, PC)
                        stream(bank_of(t)[:], feature_terms(n + i, k, c, per * P, hi, lo, wait if t == start else None), 3 * k)\
                            .then_inc(S("pe_done"), 4 // (outs // panels))

                def turn(j):
                    pe.wait_ge(S("qk_done"), j + 1)
                    for f in range(4):
                        if j:
                            pe.wait_ge(S("qk_t_out"), 4 * (j - 1) + f + 1)
                        elif f >= 2:
                            pe.wait_ge(S("ws_t_out"), f - 1)
                        if j == 1:
                            pe.wait_ge(S("ya_h"), 2 * f + 1)
                        for b in range(TB):
                            mm = pe.transpose(B[4 + f][:, b * P:(b + 1) * P], qk_raw[j % 2][:, b, f * P:(f + 1) * P], ident[:])
                        mm.then_inc(S("qk_t"), 1)

                tokens("v_gm", None, True)
                features("u_gm", "u_gm_out", ("v_gm_out", 4), h_hi, h_lo)
                tokens("qk0", ("u_gm_out", 4))
                pe.wait_ge(S("mod_made"), 1)
                pe.wait_ge(S("ws_masked"), 1)
                for f in range(2):
                    for g in range(4):
                        mm = pe.transpose(B[6 + f][:, g * P:(g + 1) * P], ws_in[:, 4 * f + g, :], ident[:])
                    mm.then_inc(S("ws_t"), 1)
                tokens("qk1", ("qk0_out", 4))
                turn(0)
                tokens("qk2", ("qk1_out", 4))
                pe.wait_ge(S("ws_t_out"), 2)
                pe.wait_ge(S("ln_out"), TB)
                pe.wait_ge(S("qk_t_out"), 4)
                for f in range(4):
                    for half in range(2):
                        g = 2 * f + half
                        for c in range(TB):
                            mm = pe.matmul(B[4 + f][64 * half:64 * half + 64, c * P:(c + 1) * P],
                                           vg[:, c, g * 64:(g + 1) * 64], wsT[:, g, :], start=True, stop=True)
                    mm.then_inc(S("f_done"), 1)
                tokens("v0", ("qk2_out", 4))
                turn(1)
                tokens("qk3", ("v0_out", 4))
                turn(2)
                tokens("v1", ("qk3_out", 4))
                turn(3)
                features("g_a", "g_a_out", ("v1_out", 4), h_hi, h_lo)
                features("a_proj", "a_proj_out", ("g_a_out", 8), ya_hi, ya_lo, lambda k: pe.wait_ge(S("ya_split"), k + 1))
                features("g_b", "g_b_out", ("a_proj_out", 8), h_hi, h_lo)

                def scores(u):
                    h, i = UNITS[u]
                    keys = (i + 1) * P
                    if u == 0:
                        pe.wait_ge(S("g_b_out"), 8)
                        pe.wait_ge(S("qk_t_out"), 16)
                    if u >= 3:
                        pe.wait_ge(S("at_exp"), 2 * (u - 2))
                    for m in range(2):
                        half = slice(64 * m, 64 * m + 64)
                        bank = B[2 * (u % 3) + m]
                        pe.matmul(bank[:, :keys], qT[half, h, i * P:(i + 1) * P], kT[half, h, :keys], start=True, stop=False)
                        pe.matmul(bank[:, i * P:keys], ident[:], causal[:], start=False, stop=True).then_inc(S("at_s"), 1)

                def weigh(u):
                    h, i = UNITS[u]
                    s = u % 2
                    pe.wait_ge(S("at_a"), 2 * u + 2)
                    if u:
                        pe.wait_ge(S("at_t_out"), u)
                    for j in range(i + 1):
                        mm = pe.transpose(B[6][:, j * P:(j + 1) * P], tmp[:, 4 + s, j * P:(j + 1) * P], ident[:])
                    mm.then_inc(S("at_t"), 1)

                def values(u):
                    h, i = UNITS[u]
                    s = u % 2
                    pe.wait_ge(S("at_t_out"), u + 1)
                    if u:
                        pe.wait_ge(S("at_o"), u)
                    products(B[7][:, 0:P], [(aT[:, s, j * P:(j + 1) * P], vtok[:, j, h * P:(h + 1) * P])
                                                for j in range(i + 1)]).then_inc(S("at_pv"), 1)

                scores(0)
                scores(1)
                for u in range(len(UNITS)):
                    if u + 2 < len(UNITS):
                        scores(u + 2)
                    weigh(u)
                    if u:
                        values(u - 1)
                values(len(UNITS) - 1)
                n = PART["b_proj"][0]
                for h in range(HEADS + 2):
                    if h < HEADS:
                        pe.wait_ge(S("o_scaled"), h + 1)
                        if h >= 4:
                            pe.wait_ge(S("yb_h"), h - 3)
                        for b in range(TB):
                            mm = pe.transpose(B[4 + h % 4][:, b * P:(b + 1) * P], o_tok[:, b, h * P:(h + 1) * P], ident[:])
                        mm.then_inc(S("yb_t"), 1)
                    if h >= 2:
                        for i in range(2):
                            pe.wait_ge(S("w_split"), n + i + 1)
                            by_k(n + i, [B[2 * i], B[2 * i + 1]], yb_hi, yb_lo, lambda k: pe.wait_ge(S("yb_split"), k + 1), (h - 2,))
                features("b_proj", "b_proj_out", None, yb_hi, yb_lo, start=4)
                features("w_out", "mixer_x", ("b_proj_out", 8), m_hi, m_lo, lambda k: pe.wait_ge(S("m_split"), k + 1))

            if "ffn2" in stages:
                norm("n2")
                gate_up("ffn2", "n2", silu_free("ffn2"))
                down("ffn2")

            if "mix2" in stages:
                pe.wait_ge(S("mod_made"), 2)
                norm("p1")
                for i in range(2):
                    pe.wait_ge(S("w_split"), PART["u2"][0] + i + 1)
                    by_k(PART["u2"][0] + i, [B[2 * i], B[2 * i + 1]], h_hi, h_lo, ready("p1"))
                def s5_inputs(part):
                    pe.wait_ge(S("bd_made"), 8 * (part + 1))
                    for g in range(4 * part, 4 * part + 4):
                        for i in range(4):
                            mm = pe.transpose(B[4 + g % 4][:, i * P:(i + 1) * P], bd[:, 4 * (g % 4) + i, :], ident[:])
                        mm.then_inc(S("bb_t"), 1)

                tokens("q2", ("u2_out", 4))
                s5_inputs(0)
                n = PART["kv2"][0]
                pe.wait_ge(S("w_split"), n + 1)
                for b in range(TB):
                    pe.wait_ge(S("q2_out"), b + 1)
                    stream(B[b][:, 0:PC], token_terms(n, KD, PC, b, h_hi, h_lo), 3 * KD).then_inc(S("pe_done"), 1)
                pe.wait_ge(S("hank_landed"), 16)
                pe.wait_ge(S("flip_made"), 1)
                pe.wait_ge(S("bb_t_out"), 4)
                for g in range(4):
                    pe.matmul(B[4 + g][:], causal[:], hank[:, 2 * g:2 * g + 2, :], start=True, stop=True).then_inc(S("bias_flipped"), 1)
                pe.wait_ge(S("bias_out"), 4)
                s5_inputs(1)
                pe.wait_ge(S("s5_landed"), 96)
                pe.wait_ge(S("bb_t_out"), 8)
                for part in range(2):
                    for c in range(4):
                        mm = pe.transpose(B[4 + 3 * part][:, c * P:(c + 1) * P], c_in[:, part, c].rearrange("p w n -> p (w n)"), ident[:])
                    mm.then_inc(S("c_t"), 1)
                for f in range(6):
                    if f == 0:
                        pe.wait_ge(S("qk2_made"), 1)
                    if f == 4:
                        pe.wait_ge(S("qk2_made"), 2)
                    if f >= 2:
                        pe.wait_ge(S("qk2_t_out"), f - 1)
                    for b in range(TB):
                        if f < 4:
                            mm = pe.transpose(B[5 + f % 2][:, b * P:(b + 1) * P], q2_raw[:, b, f * P:(f + 1) * P], ident[:])
                        else:
                            head = k2_raw[:, b, (f - 4) * QK:(f - 3) * QK]
                            for twice in range(2):
                                mm = pe.matmul(B[5 + f % 2][twice * QK:(twice + 1) * QK, b * P:(b + 1) * P], head, ident[:], start=True, stop=True)
                    mm.then_inc(S("qk2_t"), 1)
                pe.wait_ge(S("v2_out"), 8)
                pe.wait_ge(S("k2_out"), TB)
                pe.wait_ge(S("bb_t_out"), 8)
                pe.wait_ge(S("qk2_t_out"), 6)

                def sw_scores(u):
                    b, n = SW_UNITS[u]
                    lo = P if b == 0 else 0
                    if u:
                        pe.wait_ge(S("sw_t_out"), SW_BEFORE[u])
                    for slot in range(2):
                        for odd in range(2):
                            half = slice(64 * odd, 64 * odd + 64)
                            mm = pe.matmul(B[5 + odd][:, slot * 2 * P + lo:(slot + 1) * 2 * P], q2T[half, 2 * n + slot, b * P:(b + 1) * P],
                                           k2T[half, n, (b - 1) * P + lo:(b + 1) * P], start=True, stop=True)
                            if slot:
                                mm.then_inc(S("sw_s"), 1)

                def sw_turn(u):
                    pe.wait_ge(S("sw_p"), u + 1)
                    for kb in SW_BLOCKS[u]:
                        for h in range(4):
                            mm = pe.transpose(B[5 + kb][:, h * P:(h + 1) * P], prob[:, u % 2, h, kb * P:(kb + 1) * P], ident[:])
                        mm.then_inc(S("sw_t"), 1)

                def sw_values(u):
                    b, n = SW_UNITS[u]
                    pe.wait_ge(S("sw_t_out"), SW_BEFORE[u + 1])
                    if u:
                        pe.wait_ge(S("sw_out"), 2 * u)
                    products(B[7][:], [(v2[:, b - 1 + kb, n].rearrange("p w d -> p (w d)"), pT[:, u % 2, kb, :]) for kb in SW_BLOCKS[u]])\
                        .then_inc(S("sw_pv"), 1)

                def inputs(st):
                    if st >= 2:
                        pe.wait_ge(S("scan_in"), 4 * (st - 1))
                    for part in range(2):
                        pe.matmul(B[2 * (st % 2) + part][:], bbT[:, part, st, :], u2[:, st // 4, :], start=True, stop=True).then_inc(S("bu"), 1)

                SCAN_TERMS = (0, 2, 1, 3)

                def outputs(st):
                    if st >= 4 and st % 4 == 0:
                        pe.wait_ge(S("s5_y"), st // 4)
                    if st == 0:
                        pe.wait_ge(S("c_out"), 16)
                    pe.wait_ge(S("scan_p"), 2 * st + 2)
                    pe.wait_ge(S("scan_q"), 2 * st + 2)
                    products(B[4][:], [(cT[:, i % 2, st, :], scan_product(st, i)) for i in SCAN_TERMS],
                             st % 4 == 0, st % 4 == 3).then_inc(S("y_added"), 1)

                inputs(0)
                for st in range(NS):
                    u = st // 2
                    if st + 1 < NS:
                        inputs(st + 1)
                    if st % 2 == 0:
                        if u:
                            sw_values(u - 1)
                        sw_scores(u)
                    if st:
                        outputs(st - 1)
                    if st % 2:
                        sw_turn(u)
                sw_values(len(SW_UNITS) - 1)
                outputs(NS - 1)
                pe.wait_ge(S("sw_out"), 2 * len(SW_UNITS))
                norm("pa")
                n = PART["glu"][0]
                pe.wait_ge(S("w_split"), n + 1)
                wh, wl = panel(w_hi, n, 4, T), panel(w_lo, n, 4, T)
                for k in range(4):
                    pe.wait_ge(S("z_split"), k + 1)
                    for t in range(4):
                        own = slice(t * P, (t + 1) * P)
                        for i, (w, h) in enumerate(((wh, z_hi), (wh, z_lo), (wl, z_hi))):
                            mm = pe.matmul(glu_bank(t)[:], w[:, k, own], h[:, k, :], start=k == 0 and i == 0, stop=k == 3 and i == 2)
                        if k == 3:
                            mm.then_inc(S("pe_done"), 1)
                n = PART["w_out2"][0]
                halves = ((4, 5, 6, 7), (0, 1, 2, 3))
                for part, ks in enumerate(halves):
                    for i in range(2):
                        pe.wait_ge(S("w_split"), n + i + 1)
                        if part == 0 and i == 1:
                            pe.wait_ge(S("glu_gate"), 2)
                        by_k(n + i, [B[2 * i], B[2 * i + 1]], h_hi, h_lo,
                             lambda k: pe.wait_ge(S("norm_split"), NORM["pa"] + k - 3 if k >= 4 else NORM["ps"] + k + 1), ks, 4, 3)
                        if part == 0 and i == 0:
                            norm("ps")
                features("w_out2", "mix2_x", None, h_hi, h_lo, start=4)

            if "ffn3" in stages:
                norm("p2")
                gate_up("ffn3", "p2", lambda i, half: pe.wait_ge(S("ffn3_conv"), i * 8 + (4 * half + 4)))
                down("ffn3")
            for b in range(TB):
                for half in range(2):
                    wait_x(pe, stages[-1], 4 * half + 3)
                    if b >= 2:
                        pe.wait_ge(S(f"out_turned{half}"), b - 1)
                    for k in range(4):
                        mm = pe.transpose(B[4 + (2 * b + half) % 4][:, k * P:(k + 1) * P], x[:, 4 * half + k, b * P:(b + 1) * P], ident[:])
                    mm.then_inc(S("out_t"), 1)


NAMES = (
    "x", "positions", "ffn1_norm", "ffn1_w_gate", "ffn1_w_up", "ffn1_w_down", "mix_norm", "w_in", "a_ln_gain", "a_ln_bias",
    "a_w_s", "a_b_s", "a_w_proj", "b_q_norm", "b_k_norm", "b_lambda_q1", "b_lambda_k1", "b_lambda_q2", "b_lambda_k2", "b_subln",
    "b_w_proj", "w_out", "ffn2_norm", "ffn2_w_gate", "ffn2_w_up", "ffn2_w_down", "c_2", "w_mod_2", "b_mod_2", "norm1_w_2",
    "w_in_2", "lam_re_2", "lam_im_2", "log_dt_2", "ssm_b_re_2", "ssm_b_im_2", "ssm_c_re_2", "ssm_c_im_2", "ssm_d_2", "w_glu_2",
    "b_glu_2", "q_norm_w_2", "k_norm_w_2", "rel_bias_2", "sinks_2", "out_norm_ssm_2", "out_norm_attn_2", "w_out_2", "norm2_w_2",
    "w_up_2", "conv_w_2", "conv_b_2", "w_down_2",
)


def distance_buckets():
    dist = 2 * P - 1 - np.arange(BAND)
    n = np.maximum(dist, 0)
    log_part = np.log(np.maximum(n, 1) / 16) / math.log(128 / 16)
    bucket = np.where(n < 16, n, np.minimum(16 + (log_part * 16).astype(np.int32), 31))
    seen = (dist >= 0) & (dist < WIN)
    table = np.zeros((33, BAND), np.float32)
    table[bucket[seen], np.flatnonzero(seen)] = 1.0
    table[32, ~seen] = NEG
    return table


def kernel(**inputs):
    from concourse import bacc
    from concourse.bass_utils import run_bass_kernel_spmd

    nc = bacc.Bacc("TRN2", target_bir_lowering=False, num_devices=1)
    arrays, aps = {}, {}
    for name in NAMES:
        a = np.ascontiguousarray(inputs[name])
        arrays[f"in_{name}"] = a
        aps[name] = nc.dram_tensor(f"in_{name}", a.shape, mybir.dt.from_np(a.dtype), kind="ExternalInput").ap()
    table = distance_buckets()
    arrays["rel_onehot"] = table
    onehot = nc.dram_tensor("rel_onehot", table.shape, F32, kind="ExternalInput").ap()
    out = nc.dram_tensor("out_x", (1, T, D), F32, kind="ExternalOutput").ap()
    build(nc, aps, onehot, out)
    r = run_bass_kernel_spmd(nc, [arrays], core_ids=[0])
    return r.results[0]["out_x"]
```

```python
import math
from contextlib import ExitStack

import numpy as np

import concourse.bass as bass
from concourse import mybir

F32 = mybir.dt.float32
F32R = mybir.dt.float32r
BF16 = mybir.dt.bfloat16
I32 = mybir.dt.int32
ALU = mybir.AluOpType
ACT = mybir.ActivationFunctionType
AX = mybir.AxisListType

P = 128
T = 512
TB = T // P
D = 1024
KD = D // P
FF = 2816
KF = FF // P
A_W = 512
A_G = 8
HEADS = 8
QK = 64
ROT = 8
LAM_INIT = 0.8 - 0.6 * math.exp(-0.3 * 0)
EPS = 1e-6
LN_EPS = 1e-5
NS = 16
SG = 16
WIN = 128
NQ = 8
NKV = 2
NEG = -1e30
BAND = 2 * P + P - 1
PANEL = 2048
PC = 256
DOWN_K = ((0, 6), (6, 6), (12, 5), (17, 5))
GU_STEPS = FF // PC
BESIDE = KF - 6
BESIDE_STEPS = BESIDE // 2
MOD_GROUPS = 6 * D // T
MOD_SLOTS = 4
MOD_STEPS = KD + 2
ROT_SLOTS = 3
MOD_END = MOD_GROUPS - BESIDE_STEPS
PHASES = {"ffn1": ((0, BESIDE_STEPS, True, 0), (BESIDE_STEPS, GU_STEPS, False, 0)),
          "ffn2": ((0, MOD_END, True, 1), (MOD_END, BESIDE_STEPS, False, (NS - MOD_END) // (BESIDE_STEPS - MOD_END)),
                   (BESIDE_STEPS, GU_STEPS, False, 0))}
MOD_AT = {"ffn1": 0, "ffn2": BESIDE_STEPS}
DOWN_PANELS = 16
FFN_PANELS = 2 * GU_STEPS + DOWN_PANELS
MIX_PANELS = 34
MIX2_PANELS = 10
BASE = {"ffn1": 0}
BASE["mixer"] = BASE["ffn1"] + FFN_PANELS
BASE["ffn2"] = BASE["mixer"] + MIX_PANELS
BASE["mix2"] = BASE["ffn2"] + FFN_PANELS
BASE["ffn3"] = BASE["mix2"] + MIX2_PANELS
END = BASE["ffn3"] + FFN_PANELS
ROUND = 12582912.0
TWO_PI = 2.0 * math.pi
PI_1 = 6.28125
PI_2 = float(np.float32(np.round((TWO_PI - PI_1) * 2.0**20) / 2.0**20))
PI_3 = TWO_PI - PI_1 - PI_2
PI_LOW = 3.1415925
EXP_RANGE = (-87.0, 88.7)
LN_2 = math.log(2.0)
LN_2_HI = 0.693359375
ROWS = {}
for _tile, _names in enumerate((
    (("ffn1_norm", 8), ("mix_norm", 8), ("ffn2_norm", 8), ("norm1_w_2", 8), ("norm2_w_2", 8), ("b_mod_2", 48),
     ("ssm_d_2", 4), ("b_glu_2", 4), ("out_norm_ssm_2", 4), ("out_norm_attn_2", 4), ("b_subln", 1), ("c_2", 8)),
    (("lam_re_2", 16), ("lam_im_2", 16), ("conv_b_2", 44), ("conv_w_2:2", 44)),
    (("conv_w_2:0", 44), ("conv_w_2:1", 44)),
)):
    _at = 0
    for _name, _n in _names:
        ROWS[_name] = (_tile, _at, _n)
        _at += _n
EARLY_ROWS = ("ffn1_norm", "mix_norm", "ffn2_norm", "norm1_w_2", "norm2_w_2", "c_2")
ROW_COUNTS = tuple(max(a + n for t, a, n in ROWS.values() if t == tile) for tile in range(3))


class Steps:

    def __init__(self, engine, semaphore):
        self.engine, self.semaphore, self.n = engine, semaphore, 0

    def __call__(self, instruction):
        instruction.then_inc(self.semaphore, 1)
        self.n += 1
        self.engine.wait_ge(self.semaphore, self.n)


def build(nc, inp, rel_onehot, out):

    def col_major(w):
        return w.rearrange("l (k p) n -> p (l k) n", p=P)

    rot_dram = nc.dram_tensor("rotations", (2, NS, P, T), F32).ap()
    band_dram = nc.dram_tensor("band", (NQ, BAND), F32)

    with ExitStack() as ctx:
        def sb(name, shape, dt=F32, scope=ctx):
            return scope.enter_context(nc.sbuf_tensor(name, shape, dt))

        sems = {}

        def S(name):
            if name not in sems:
                sems[name] = ctx.enter_context(nc.semaphore(name))
            return sems[name]

        B = [ctx.enter_context(nc.psum_tensor(f"bank{i}", [P, T], F32)) for i in range(8)]

        x = sb("x", [P, KD, T])
        w_raw = [sb(f"w_raw{i}", [P, PANEL]) for i in range(2)]
        w_hi = [sb(f"w_hi{i}", [P, PANEL], F32R) for i in range(2)]
        w_lo = [sb(f"w_lo{i}", [P, PANEL], F32R) for i in range(2)]
        tmp = sb("tmp", [P, 6, T])
        rstd = sb("rstd", [P, T])
        ident = sb("ident", [P, P])
        ones = sb("ones", [P, P])
        causal = sb("causal", [P, P])
        mask_parts = sb("mask_parts", [P, 2, P], BF16)
        vec = sb("vec", [P, 3, P])
        small = sb("small", [P, 96])
        stat = sb("stat", [P, 96])
        cos_t = sb("cos_t", [P, TB, ROT])
        sin_t = sb("sin_t", [P, TB, ROT])
        gains = sb("gains", [P, 4, QK])
        lam_in = sb("lam_in", [P, 4, QK])
        sink = sb("sink", [P, NQ])
        mod = sb("mod", [P, 48])
        gain2 = sb("gain2", [P, 2, KD])
        s5 = sb("s5", [P, 24, NS])
        pos_i = sb("pos_i", [P, TB], I32)
        ang = sb("ang", [P, 2, TB, ROT])
        log_dt = sb("log_dt", [P, 2 * NS])
        ones_r = sb("ones_r", [P, 2], F32R)

        def col(name, i):
            t, a, _ = ROWS[name]
            return vec[:, t, a + i:a + i + 1]

        def cols(name):
            t, a, n = ROWS[name]
            return vec[:, t, a:a + n]

        def col_at(name, i, off=0):
            t, a, _ = ROWS[name]
            return vec[:, t, bass.ds(i + (a + off), 1)]

        def overlay(size, *tiles):
            assert all(first < size for first, *_ in tiles)
            made = []
            for first, name, shape, dt in tiles:
                with ExitStack() as area:
                    if first:
                        sb(f"under_{name}", [P, first * T], F32, area)
                    made.append(sb(name, shape, dt, area))
            return made

        h_hi, h_lo, o_tok, yb_hi, rot, sc_a, sc_v, sc_p = overlay(
            2 * KD,
            (0, "h_hi", [P, KD, T], F32R), (KD, "h_lo", [P, KD, T], F32R),
            (KD, "o_tok", [P, TB, D], F32), (0, "yb_hi", [P, KD, T], F32R),
            (0, "rot", [P, ROT_SLOTS, 2, T], F32), (2 * ROT_SLOTS, "sc_a", [P, 4, T], F32),
            (2 * ROT_SLOTS + 4, "sc_v", [P, 4, T], F32), (2 * ROT_SLOTS + 8, "sc_p", [P, 2, T], F32),
        )
        sb("h_area", [P, 2 * KD * T])

        hid_hi, hid_lo, x_in, rows, oh, rel, band, rot_t, rot_ti, rot_n, rot_r, rot_abs, rot_cs, mod_acc, mod_raw, mod_lo, mod_hi = overlay(
            2 * KF,
            (0, "hid_hi", [P, KF, T], F32R), (KF, "hid_lo", [P, KF, T], F32R),
            (0, "x_in", [P, TB, D], F32), (8, "rows", [P, 3, P], F32), (9, "oh", [33, BAND], F32),
            (10, "rel", [33, NQ], F32), (11, "band_row", [NQ, BAND], F32),
            (BESIDE, "rot_t", [P, T], F32), (BESIDE + 1, "rot_ti", [P, T], I32), (BESIDE + 1, "rot_n", [P, T], F32),
            (BESIDE + 2, "rot_r", [P, T], F32), (BESIDE + 3, "rot_abs", [P, T], F32), (BESIDE + 4, "rot_cs", [P, 2, T], F32),
            (KF + BESIDE, "mod_acc", [P, T], F32), (KF + BESIDE + 1, "mod_raw", [P, MOD_SLOTS, T], F32),
            (KF + BESIDE, "mod_lo", [P, T], F32R), (KF + BESIDE + 1 + MOD_SLOTS, "mod_hi", [P, T], F32R),
        )
        vg, u_g, ya_hi, ya_lo, qT, kT, vtok, ga, gb, aT, m_hi, m_lo, yb_lo, ln_g, ln_b, wsT, ws_in, bs, qk_raw0, qk_raw1 = overlay(
            2 * KF,
            (0, "vg", [P, TB, A_W], F32), (4, "u_g", [P, 4, T], F32),
            (8, "ya_hi", [P, 4, T], F32R), (4, "ya_lo", [P, 4, T], F32R),
            (12, "qT", [P, HEADS, T], F32), (20, "kT", [P, HEADS, T], F32), (28, "vtok", [P, TB, D], F32),
            (36, "ga", [P, KD, T], F32),
            (0, "gb", [P, KD, T], F32), (8, "aT", [P, 2, T], F32),
            (12, "m_hi", [P, KD, T], F32R), (20, "m_lo", [P, KD, T], F32R), (28, "yb_lo", [P, KD, T], F32R),
            (12, "ln_g", [P, A_W], F32), (13, "ln_b", [P, A_W], F32),
            (28, "wsT", [P, A_G, P], F32), (30, "ws_in", [P, A_G, P], F32), (32, "bs", [P, 4, P], F32),
            (36, "qk_raw0", [P, TB, T], F32), (40, "qk_raw1", [P, TB, T], F32),
        )
        qk_raw = [qk_raw0, qk_raw1]
        (u2, q2T, k2T, v2, bbT, cT, yat, b_in, bb, c_in, bd, bias, hank, q_sq, k_sq, pT, prob,
         z_hi, z_lo, yat_sq, gate) = overlay(
            2 * KF,
            (0, "u2", [P, 4, T], F32), (4, "q2T", [P, 4, T], F32), (8, "k2T", [P, NKV, T], F32),
            (10, "v2", [P, TB, NKV, 2, QK], F32),
            (12, "bbT", [P, 2, NS, P], F32), (20, "cT", [P, 2, NS, P], F32), (28, "yat", [P, 4, T], F32),
            (32, "b_in", [P, 2, NS, SG], F32), (33, "bb", [P, 2, NS, SG], F32), (34, "c_in", [P, 2, 4, 2, QK], F32),
            (36, "bd", [P, NS, P], F32), (40, "bias", [P, NQ, 2 * P], F32), (28, "hank", [P, NQ, 2 * P], F32),
            (4, "q_sq", [P, TB, T], F32), (8, "k_sq", [P, TB, NKV * QK], F32),
            (32, "pT", [P, 2, 2, T], F32), (36, "prob", [P, 2, 4, 2 * P], F32),
            (12, "z_hi", [P, 4, T], F32R), (16, "z_lo", [P, 4, T], F32R), (4, "yat_sq", [P, 4, T], F32), (8, "gate", [P, 4, T], F32),
        )

        SW_UNITS = [(b, n) for b in range(TB) for n in range(NKV)]
        SW_BLOCKS = [(1,) if b == 0 else (0, 1) for b, _ in SW_UNITS]
        SW_BEFORE = [sum(len(k) for k in SW_BLOCKS[:u]) for u in range(len(SW_UNITS) + 1)]

        def scan_product(st, i):
            if st % 2 == 0:
                return tmp[:, i, :]
            return tmp[:, 4 + i, :] if i < 2 else sc_p[:, i - 2, :]

        def glu_bank(t):
            return B[(2, 3, 5, 6)[t]]

        def sw_cols(first, u):
            return stat[:, first + 4 * (u % 2):first + 4 * (u % 2) + 4]

        sb("shared_area", [P, 2 * KF * T])

        def used(n, quarters=4):
            return 4 * n + quarters

        def panel(buf, n, k, c):
            return buf[n % 2][:, :k * c].rearrange("p (k c) -> p k c", k=k)

        X_OF = {"start": ("x_turned", 1), "ffn1": ("ffn1_x", 5), "mixer": ("mixer_x", 1), "ffn2": ("ffn2_x", 5),
                "mix2": ("mix2_x", 1), "ffn3": ("ffn3_x", 5)}

        NORM_PARTS = {"n1": (KD, KD), "nm": (KD, 2), "n2": (KD, 2), "p1": (KD, 2), "pa": (4, 4), "ps": (4, 4), "p2": (KD, 2)}
        NORMS = list(NORM_PARTS)
        NORM, NORM_SQ, NORM_SUM = {}, {}, {}
        for name in NORMS:
            before = [NORM_PARTS[b] for b in NORMS[:len(NORM)]]
            NORM[name] = sum(tiles for tiles, _ in before)
            NORM_SQ[name] = sum(direct for _, direct in before)
            NORM_SUM[name] = NORM_SQ[name] + sum(direct < tiles for tiles, direct in before)
        ADDED = [name for name in NORMS if NORM_PARTS[name][1] < NORM_PARTS[name][0]]

        def sums_of(name):
            tiles, direct = NORM_PARTS[name]
            return NORM_SUM[name] + direct + (direct < tiles)

        HID = {"ffn1": 0, "ffn2": KF, "ffn3": 2 * KF}

        def wait_x(eng, stage, k):
            name, first = X_OF[stage]
            eng.wait_ge(S(name), first + k)

        def rotation(i, start, rots, r):
            return i * rots + (start - start * rots + r)

        def down_bank(name, t):
            return B[(4 if name == "ffn3" else 0) + t % 4]

        def bank_of(t):
            return B[t % 4]

        MIX = BASE["mixer"]
        MIX2 = BASE["mix2"]
        MIX_PARTS = (("v_gm", 0, 2, 4), ("u_gm", 2, 2, 4), ("qk0", 4, 2, 4), ("qk1", 6, 2, 4), ("qk2", 8, 2, 4),
                     ("v0", 10, 2, 4), ("qk3", 12, 2, 4), ("v1", 14, 2, 4), ("g_a", 16, 4, 8), ("a_proj", 20, 2, 8),
                     ("g_b", 22, 4, 8), ("b_proj", 26, 4, 8), ("w_out", 30, 4, 8))
        MIX2_PARTS = (("u2", 0, 2, 4), ("q2", 2, 2, 4), ("kv2", 4, 1, 4), ("glu", 5, 1, 4), ("w_out2", 6, 4, 8))
        PART = {name: (MIX + first, panels, outs) for name, first, panels, outs in MIX_PARTS}
        PART.update({name: (MIX2 + first, panels, outs) for name, first, panels, outs in MIX2_PARTS})
        BEFORE = {b[0]: a for parts in (MIX_PARTS, MIX2_PARTS) for a, b in zip(parts, parts[1:])}
        BEFORE = {name: (part[0], part[3]) for name, part in BEFORE.items()}
        W_IN_COL = {"v_gm": 2 * D + A_W, "qk0": 2 * D + 2 * A_W, "qk1": 2 * D + 2 * A_W + T, "qk2": 3 * D + 2 * A_W,
                    "qk3": 3 * D + 2 * A_W + T, "v0": 4 * D + 2 * A_W, "v1": 4 * D + 2 * A_W + T}
        UNITS = [(h, i) for h in range(HEADS) for i in range(TB)]

        eps_col, half_pi_col, ln_eps_col = (small[:, i:i + 1] for i in (20, 21, 22))
        eps_width_col = {T: EPS * T, D: EPS * D}
        q2_raw = tmp[:, 0:4, :]
        k2_raw = tmp[:, 4, :].rearrange("p (b n) -> p b n", b=TB)

        def load_row(eng, name):
            tile, at, n = ROWS[name]
            param, _, tap = name.partition(":")
            source = inp[param][0, int(tap)] if tap else (inp[param][0] if inp[param].shape[0] == 1 else inp[param])
            if len(source.shape) == 1:
                source = source.rearrange("(n p) -> n p", p=P)
            elif source.shape[1] != P:
                source = source.rearrange("(n two) p -> n (two p)", two=P // source.shape[1])
            eng.dma_start(rows[at:at + n, tile, :], source).then_inc(S("rows_landed"), 16)

        block = ctx.enter_context(nc.Block())

        @block.sync
        def _(sp):
            def load(n, source, k, c):
                if isinstance(n, int):
                    if n >= 2:
                        sp.wait_ge(S("w_split"), n - 1)
                else:
                    sp.wait_ge(S("w_split"), n[0] - 1)
                i = n if isinstance(n, int) else n[1]
                sp.dma_start(panel(w_raw, i, k, c), source).then_inc(S(f"w_landed{i % 2}"), 16)

            def load_parameters():
                for name in ROWS:
                    if name not in EARLY_ROWS:
                        load_row(sp, name)
                sp.dma_start(rel[0:32, :], inp["rel_bias_2"]).then_inc(S("rel_landed"), 16)
                sp.dma_start(oh[:], rel_onehot).then_inc(S("rel_landed"), 16)
                for tile, names in ((gains, ("b_q_norm", "b_k_norm", "q_norm_w_2", "k_norm_w_2")),
                                    (lam_in, ("b_lambda_q1", "b_lambda_k1", "b_lambda_q2", "b_lambda_k2"))):
                    for i, name in enumerate(names):
                        sp.dma_start(tile[:, i, :], inp[name][0].partition_broadcast(P)).then_inc(S("spread_landed"), 16)
                sp.dma_start(sink[:], inp["sinks_2"][0].partition_broadcast(P)).then_inc(S("spread_landed"), 16)
                sp.dma_start(log_dt[:], inp["log_dt_2"][0].partition_broadcast(P)).then_inc(S("spread_landed"), 16)
                sp.dma_start(pos_i[:], inp["positions"].rearrange("o (b p) -> p (o b)", p=P),
                             allow_slow_non_contiguous=True).then_inc(S("spread_landed"), 16)

            def load_ffn(name, gate, up, gate_col, up_col, down):
                base = BASE[name]
                gate_v, up_v, down_v = col_major(gate), col_major(up), col_major(down)
                first = 0
                if base == 0:
                    load(0, gate_v[:, :, gate_col:gate_col + PC], KD, PC)
                    load(1, up_v[:, :, up_col:up_col + PC], KD, PC)
                    first = 1
                    load_parameters()
                with sp.Fori(first, GU_STEPS) as i:
                    load((i * 2 + base, base), gate_v[:, :, bass.ds(i * PC + gate_col, PC)], KD, PC)
                    load((i * 2 + (base + 1), base + 1), up_v[:, :, bass.ds(i * PC + up_col, PC)], KD, PC)
                base += 2 * GU_STEPS
                with sp.Fori(0, 2) as j:
                    for c in range(8):
                        k0, kn = DOWN_K[c % 4]
                        load((j * 8 + (base + c), base + c),
                             down_v[:, k0:k0 + kn, bass.ds(j * 512 + c // 4 * PC, PC)], kn, PC)

            def load_tokens(name, w, at):
                base = PART[name][0]
                for half in range(2):
                    load(base + half, w[:, 4 * half:4 * half + 4, at:at + T], 4, T)

            def load_features(name, w, at, first=0, end=None):
                base, panels, _ = PART[name]
                for i in range(first, end or panels):
                    load(base + i, w[:, :, at + i * PC:at + (i + 1) * PC], KD, PC)

            x_v = inp["x"].rearrange("o (b p) d -> p (o b) d", p=P)
            for q in range(D // PC):
                sp.dma_start(x_in[:, :, q * PC:(q + 1) * PC], x_v[:, :, q * PC:(q + 1) * PC]).then_inc(S(f"x_landed{q}"), 16)
            load_ffn("ffn1", inp["ffn1_w_gate"], inp["ffn1_w_up"], 0, 0, inp["ffn1_w_down"])
            w_in = col_major(inp["w_in"])

            load_tokens("v_gm", w_in, W_IN_COL["v_gm"])
            load_features("u_gm", w_in, 2 * D)
            for name in ("qk0", "qk1", "qk2", "v0", "qk3", "v1"):
                load_tokens(name, w_in, W_IN_COL[name])
            load_features("g_a", w_in, 0)
            for i in range(2):
                load(PART["a_proj"][0] + i, col_major(inp["a_w_proj"])[:, :, i * T:(i + 1) * T], 4, T)
            load_features("g_b", w_in, D)
            load_features("b_proj", col_major(inp["b_w_proj"]), 0)
            load_features("w_out", col_major(inp["w_out"]), 0)
            load_ffn("ffn2", inp["ffn2_w_gate"], inp["ffn2_w_up"], 0, 0, inp["ffn2_w_down"])
            w_in = col_major(inp["w_in_2"])
            load_features("u2", w_in, 0)
            load_tokens("q2", w_in, T)
            load(PART["kv2"][0], w_in[:, :, 2 * T:2 * T + PC], KD, PC)
            load(PART["glu"][0], col_major(inp["w_glu_2"]), 4, T)
            load_features("w_out2", col_major(inp["w_out_2"]), 0, 0, 3)
            sp.wait_ge(S("rot_stored"), 16 * (NS + 1))
            sp.wait_ge(S("pe_done"), used(PART["kv2"][0]))
            for st in range(NS):
                if st >= ROT_SLOTS:
                    sp.wait_ge(S("scan_p"), 2 * (st - ROT_SLOTS) + 2)
                    sp.wait_ge(S("scan_q"), 2 * (st - ROT_SLOTS) + 2)
                sp.dma_start(rot[:, st % ROT_SLOTS], rot_dram[:, st].rearrange("w p t -> p w t")).then_inc(S(f"rot_landed{st % ROT_SLOTS}"), 16)
            load_features("w_out2", col_major(inp["w_out_2"]), 0, 3, 4)
            load_ffn("ffn3", inp["w_up_2"], inp["w_up_2"], 0, FF, inp["w_down_2"])
            out_v = out.rearrange("o (b p) d -> p (o b) d", p=P)
            for b in range(TB):
                for half in range(2):
                    sp.wait_ge(S(f"out_turned{half}"), b + 1)
                sp.dma_start(out_v[:, b, :], x_in[:, b, :]).then_inc(S("out_stored"), 16)
            sp.wait_ge(S("out_stored"), 16 * TB)

        @block.gpsimd
        def _(pool):
            done = Steps(pool, S("pool_done"))
            done(pool.memset(ones[:], 1.0))
            done(pool.memset(ident[:], 0.0))
            done(pool.memset(causal[:], 0.0))
            done(pool.affine_select(out=ident[:], in_=ident[:], compare_op=ALU.not_equal, fill=1.0, base=0,
                                    pattern=[[-1, P]], channel_multiplier=1))
            done(pool.affine_select(out=causal[:], in_=causal[:], compare_op=ALU.is_ge, fill=NEG, base=0,
                                    pattern=[[-1, P]], channel_multiplier=1))
            pool.memset(rel[32:33, :], 1.0).then_inc(S("consts_made"), 1)
            pool.wait_ge(S("consts_made"), 1)
            for i, source in enumerate((ident, causal)):
                pool.tensor_copy(mask_parts[:, i, :], source[:]).then_inc(S("mask_made"), 1)
            wm = col_major(inp["w_mod_2"])

            def beside(name):
                if any(rots for *_, rots in PHASES[name]):
                    done(pool.iota(rot_ti[:], pattern=[[1, T]], base=0, channel_multiplier=0))
                    pool.tensor_copy(rot_t[:], rot_ti[:]).then_inc(S("rot_t_made"), 1)
                first = MOD_AT[name]
                groups = sum(end - start for start, end, mods, _ in PHASES[name] if mods)
                with pool.Fori(0, groups) as i:
                    for k in range(KD):
                        pool.wait_ge(S("mod_step"), i * MOD_STEPS + (first * MOD_STEPS + k + 1))
                        pool.dma_start(mod_raw[:, k % MOD_SLOTS, :], wm[:, k, bass.ds(i * T + first * T, T)])\
                            .then_inc(S(f"mod_landed{k % MOD_SLOTS}"), 16)

            def split(n):
                pool.wait_ge(S("w_hi_done"), n + 1)
                s = n % 2
                pool.tensor_tensor(w_lo[s][:], w_raw[s][:], w_hi[s][:].bitcast(F32), ALU.subtract).then_inc(S("w_split"), 1)

            split(0)
            split(1)
            pool.wait_ge(S("band_made"), 1)
            pool.dma_start(band_dram.ap(), band[:]).then_inc(S("band_stored"), 16)
            beside("ffn1")

            def norm(name, before):
                tiles, direct = NORM_PARTS[name]
                for k in range(tiles - direct):
                    wait_x(pool, before, k)
                    done(pool.tensor_tensor(tmp[:, min(k, 1), :], x[:, k, :], x[:, k, :], ALU.mult))
                    if k:
                        ins = pool.tensor_tensor(tmp[:, 0, :], tmp[:, 0, :], tmp[:, 1, :], ALU.add)
                        if k < tiles - direct - 1:
                            done(ins)
                ins.then_inc(S("norm_added"), 1)

            norm("nm", "ffn1")
            wait_x(pool, "ffn1", KD - 1)
            pool.dma_start(ws_in[:], inp["a_w_s"][0].rearrange("g t s -> t g s")).then_inc(S("ws_landed"), 16)
            for name, tile in (("a_ln_gain", ln_g), ("a_ln_bias", ln_b)):
                pool.dma_start(tile[:], inp[name][0].partition_broadcast(P)).then_inc(S("gmlp_landed"), 16)
            for half in range(2):
                pool.dma_start(bs[64 * half:64 * half + 64], inp["a_b_s"][0].rearrange("(f two) t -> two f t", two=2)[half]
                              .partition_broadcast(64)).then_inc(S("gmlp_landed"), 16)
            split(BASE["mixer"] + 1)
            pool.wait_ge(S("ws_landed"), 16)
            pool.affine_select(out=ws_in[:], in_=ws_in[:], compare_op=ALU.is_ge, fill=0.0, base=0,
                               pattern=[[0, A_G], [-1, P]], channel_multiplier=1).then_inc(S("ws_masked"), 1)
            norm("n2", "mixer")
            split(BASE["ffn2"] + 1)
            wait_x(pool, "mixer", KD - 1)
            beside("ffn2")
            norm("p1", "ffn2")
            split(BASE["mix2"] + 1)
            s5_b = [inp[f"ssm_b_{part}_2"].rearrange("o (s two) n h -> (two n) (o s) h", two=2) for part in ("re", "im")]
            wait_x(pool, "ffn2", KD - 1)
            for i in range(2):
                pool.dma_start(b_in[:, i], s5_b[i]).then_inc(S("s5_landed"), 16)
                c_v = inp[f"ssm_c_{('re', 'im')[i]}_2"].rearrange("o (c g) h n -> (g h) (o c) n", c=4)
                for twice in range(2):
                    pool.dma_start(c_in[:, i, :, twice, :], c_v).then_inc(S("s5_landed"), 16)
            pool.wait_ge(S("band_stored"), 16)
            pool.dma_start(hank[:], bass.AP(band_dram, 0, [[1, P], [BAND, NQ], [1, 2 * P]])).then_inc(S("hank_landed"), 16)
            wait_x(pool, "ffn2", 0)
            done(pool.memset(causal[:], 0.0))
            pool.affine_select(out=causal[:], in_=causal[:], compare_op=ALU.not_equal, fill=1.0, base=1 - P,
                               pattern=[[1, P]], channel_multiplier=1).then_inc(S("flip_made"), 1)
            pool.memset(bd[:], 0.0).then_inc(S("zeroed"), 1)
            pool.memset(cT[:], 0.0).then_inc(S("zeroed"), 1)
            for st in range(NS + 1):
                if st < NS:
                    for i, op in enumerate((ALU.add, ALU.subtract)):
                        pool.wait_ge(S("scan_in"), 4 * st + 2 * i + 2)
                        if st:
                            pool.wait_ge(S("scanned"), 2 * (st - 1) + i + 1)
                        pool.tensor_tensor(sc_v[:, i, :], sc_a[:, 2 * i, :], sc_a[:, 2 * i + 1, :], op).then_inc(S("scan_v"), 1)
                if st:
                    r = rot[:, (st - 1) % ROT_SLOTS]
                    pool.wait_ge(S("scanned"), 2 * st - 1)
                    if st >= 3:
                        pool.wait_ge(S("y_added"), st - 2)
                    else:
                        pool.wait_ge(S("qk2_t"), 6)
                    for i in range(2):
                        pool.tensor_tensor(scan_product(st - 1, i), sc_v[:, 2, :], r[:, i, :], ALU.mult).then_inc(S("scan_p"), 1)
            for k in range(4):
                pool.wait_ge(S("sw_out"), 2 * len(SW_UNITS) - (2 if k < 2 else 0))
                pool.tensor_tensor(yat_sq[:, k, :], yat[:, k, :], yat[:, k, :], ALU.mult).then_inc(S("norm_sq"), 1)
            norm("p2", "mix2")
            split(BASE["ffn3"] + 1)

        @block.scalar
        def _(act):
            done = Steps(act, S("act_done"))

            def split(n, i=None):
                if i is None:
                    if n >= END:
                        return
                    i = n
                    act.wait_ge(S(f"w_landed{i % 2}"), 16 * (n // 2 + 1))
                    if n >= 2:
                        act.wait_ge(S("pe_done"), used(n - 2))
                else:
                    act.wait_ge(S(f"w_landed{i % 2}"), (n - (i % 2)) * 8 + 16)
                    act.wait_ge(S("pe_done"), (n - 2) * 4 + 4)
                act.copy(w_hi[i % 2][:], w_raw[i % 2][:]).then_inc(S("w_hi_done"), 1)

            def norm(name, tiles, ready, shift=None, hi=None, width=D, panel=None, between={}):
                hi = h_hi if hi is None else hi
                count, direct = NORM_PARTS[name]
                for d in range(direct if ready else 0):
                    if d in between:
                        split(between[d])
                    ready(act, count - direct + d)
                    if d >= 2:
                        act.wait_ge(S("norm_summed"), NORM_SUM[name] + d - 1)
                    act.activation(tmp[:, 2 + d % 2, :], tiles[:, count - direct + d, :], ACT.Square).then_inc(S("norm_sq"), 1)
                act.wait_ge(S("norm_summed"), sums_of(name))
                act.activation(rstd[:], B[7][:], ACT.Abs_reciprocal_sqrt, scale=1.0 / width, bias=eps_col).then_inc(S("norm_root"), 1)
                if panel is not None:
                    split(panel)
                for k in range(count):
                    act.wait_ge(S("norm_h"), NORM[name] + k + 1)
                    source = tmp[:, 2 + k % 4, :]
                    if shift is None:
                        act.copy(hi[:, k, :], source).then_inc(S("norm_hi"), 1)
                    else:
                        act.activation(hi[:, k, :], source, ACT.Identity, bias=shift(k)).then_inc(S("norm_hi"), 1)

            def rotations(st):
                act.wait_ge(S("rot_turns"), st + 1)
                act.wait_ge(S("rot_stored"), st * 16 + 16)
                act.activation(rot_cs[:, 1, :], rot_r[:], ACT.Sin, scale=-TWO_PI).then_inc(S("rot_made"), 1)
                act.activation(rot_abs[:], rot_r[:], ACT.Abs).then_inc(S("rot_read"), 1)
                act.wait_ge(S("rot_read"), st + 2)
                act.activation(rot_cs[:, 0, :], rot_abs[:], ACT.Sin, scale=-TWO_PI, bias=half_pi_col).then_inc(S("rot_made"), 1)
                act.wait_ge(S("rot_made"), st * 2 + 2)
                act.dma_start(rot_dram[:, bass.ds(st, 1)].rearrange("w s p t -> p (w s) t"), rot_cs[:]).then_inc(S("rot_stored"), 16)

            def swiglu(name):
                base = BASE[name]
                for start, stop, _, rots in PHASES[name]:
                    if start == BESIDE_STEPS and name == "ffn2":
                        act.wait_ge(S("rot_stored"), 16 * (NS + 1))
                    with act.Fori(start, stop) as i:
                        if rots:
                            rotations(rotation(i, start, rots, 0))
                        split(i * 2 + (base + 2), base)
                        for t in range(2):
                            act.wait_ge(S("pe_done"), i * 8 + (4 * base + 2 * t + 2))
                            act.wait_ge(S("hid"), i * 2 + (HID[name] + t + 1))
                            act.activation(tmp[:, t, :], B[t][:], ACT.Silu).then_inc(S("silu"), 1)
                        if rots > 1:
                            rotations(rotation(i, start, rots, 1))
                        split(i * 2 + (base + 3), base + 1)
                        for t in range(2):
                            act.wait_ge(S("hid"), i * 2 + (HID[name] + t + 3))
                            act.copy(hid_hi[:, bass.ds(i * 2 + t, 1), :], tmp[:, 2 + t:3 + t, :]).then_inc(S("hid_hi"), 1)
                        for r in range(2, rots):
                            rotations(rotation(i, start, rots, r))

            def down(name, beside={}):
                for c in range(DOWN_PANELS - 1):
                    split(BASE[name] + 2 * GU_STEPS + c + 2)
                    if c in beside:
                        beside[c]()

            act.sem_inc(S("silu"), 2)
            act.sem_inc(S("rot_read"), 1)
            act.sem_inc(S("rot_stored"), 16)
            for name in EARLY_ROWS:
                load_row(act, name)
            act.wait_ge(S("cols_made"), 1)

            norm("n1", x, lambda eng, k: wait_x(eng, "start", k), panel=1, between={4: 0})
            act.wait_ge(S("vec_made"), 3)
            act.activation(small[:, 0:KD], cols("c_2"), ACT.Silu).then_inc(S("silu_c"), 1)
            def sines():
                act.wait_ge(S("angles"), 1)
                for angle, sine, cosine in ((s5[:, 4, :], s5[:, 6, :], s5[:, 7, :]), (ang[:, 0], sin_t[:], cos_t[:])):
                    act.activation(sine, angle, ACT.Sin).then_inc(S("sines"), 1)
                    done(act.activation(cosine, angle, ACT.Abs))
                    act.activation(cosine, cosine, ACT.Sin, scale=-1.0, bias=half_pi_col).then_inc(S("sines"), 1)

            act.wait_ge(S("band_stored"), 16)
            swiglu("ffn1")
            down("ffn1", {10: sines})

            norm("nm", x, lambda eng, k: wait_x(eng, "ffn1", k), panel=BASE["mixer"] + 1)

            def tokens(name, evacuate):
                n = PART[name][0]
                split(n + 2)
                for b in range(TB):
                    if b == TB - 1:
                        split(n + 3)
                    act.wait_ge(S("pe_done"), used(n + 1, b + 1))
                    evacuate(b)

            def features(name, evacuate):
                n, panels, _ = PART[name]
                for i in range(panels):
                    for t in range(2):
                        if t == 1:
                            split(n + i + 2)
                        act.wait_ge(S("pe_done"), used(n + i, 2 * t + 2))
                        evacuate(2 * i + t)

            tokens("v_gm", lambda b: act.activation(vg[:, b, :], B[b][:], ACT.Gelu).then_inc(S("v_gm_out"), 1))
            features("u_gm", lambda t: act.activation(u_g[:, t, :], bank_of(t)[:], ACT.Gelu).then_inc(S("u_gm_out"), 1))
            act.wait_ge(S("ln_var"), 1)
            act.activation(stat[:, 40:44], stat[:, 36:40], ACT.Sqrt, bias=ln_eps_col).then_inc(S("ln_root"), 1)

            def turned(j):
                dst = (qT, kT)[j // 2]
                for f in range(4):
                    act.wait_ge(S("qk_t"), 4 * j + f + 1)
                    act.copy(dst[:, 4 * (j % 2) + f, :], B[4 + f][:]).then_inc(S("qk_t_out"), 1)

            def queries_keys(j):
                raw = qk_raw[j % 2]
                if j >= 2:
                    act.wait_ge(S("qk_t"), 4 * (j - 1))
                tokens(f"qk{j}", lambda b: act.copy(raw[:, b, :], B[b][:]).then_inc(S(f"qk{j}_out"), 1))
                if j == 2:
                    for f in range(4):
                        act.wait_ge(S("ya_h"), 2 * f + 2)
                        act.copy(ya_hi[:, f, :], tmp[:, 4 + f % 2, :]).then_inc(S("ya_hi_out"), 1)
                act.wait_ge(S(f"qk{j}_out"), TB)
                if j:
                    act.wait_ge(S("qk_done"), j)
                act.activation(tmp[:, 0:4, :], raw[:], ACT.Square).then_inc(S("qk_sq"), 1)
                act.wait_ge(S("qk_ssq"), j + 1)
                act.activation(stat[:, 0:32], stat[:, 0:32], ACT.Sqrt, scale=1.0 / QK, bias=eps_col).then_inc(S("qk_root"), 1)

            def values(g):
                tokens(f"v{g}", lambda b: act.copy(vtok[:, b, g * T:(g + 1) * T], B[b][:]).then_inc(S(f"v{g}_out"), 1))

            queries_keys(0)
            for f in range(2):
                act.wait_ge(S("ws_t"), f + 1)
                act.copy(wsT[:, 4 * f:4 * f + 4, :], B[6 + f][:].rearrange("p (g t) -> p g t", g=4)).then_inc(S("ws_t_out"), 1)
            queries_keys(1)
            turned(0)
            queries_keys(2)
            act.wait_ge(S("ya_h"), 8)
            values(0)
            turned(1)
            queries_keys(3)
            turned(2)
            values(1)
            turned(3)
            features("g_a", lambda t: act.activation(ga[:, t, :], bank_of(t)[:], ACT.Sigmoid).then_inc(S("g_a_out"), 1))
            for i in range(2):
                split(PART["a_proj"][0] + i + 2)
            features("g_b", lambda t: act.activation(gb[:, t, :], bank_of(t)[:], ACT.Sigmoid).then_inc(S("g_b_out"), 1))

            def soft(u):
                h, i = UNITS[u]
                keys = (i + 1) * P
                s = u % 2
                for m in range(2):
                    bank = 2 * (u % 3) + m
                    act.wait_ge(S("at_max"), 2 * u + m + 1)
                    if u >= 2:
                        act.wait_ge(S("at_a"), 2 * (u - 1))
                    act.activation(tmp[:, 2 * s + m, :keys], B[bank][:, :keys], ACT.Exp, bias=stat[:, bank:bank + 1],
                                   accum_out=stat[:, 6 + 2 * s + m:7 + 2 * s + m]).then_inc(S("at_exp"), 1)

            def a_turned(u):
                keys = (UNITS[u][1] + 1) * P
                act.wait_ge(S("at_t"), u + 1)
                if u >= 2:
                    act.wait_ge(S("at_pv"), u - 1)
                act.copy(aT[:, u % 2, :keys], B[6][:, :keys]).then_inc(S("at_t_out"), 1)

            def o_out(u):
                h, i = UNITS[u]
                act.wait_ge(S("at_pv"), u + 1)
                done(act.copy(o_tok[:, i, h * P:(h + 1) * P], B[7][:, 0:P]))
                act.activation(rstd[:, 0:P], o_tok[:, i, h * P:(h + 1) * P], ACT.Square,
                               accum_out=stat[:, 16 + i * HEADS + h:17 + i * HEADS + h]).then_inc(S("at_o"), 1)

            soft(0)
            for u in range(len(UNITS)):
                if u + 1 < len(UNITS):
                    soft(u + 1)
                a_turned(u)
                if u:
                    o_out(u - 1)
            o_out(len(UNITS) - 1)
            act.wait_ge(S("at_o"), len(UNITS))
            act.activation(stat[:, 16:48], stat[:, 16:48], ACT.Sqrt, scale=1.0 / P, bias=eps_col).then_inc(S("at_root"), 1)
            for h in range(HEADS):
                act.wait_ge(S("yb_h"), h + 1)
                act.copy(yb_hi[:, h, :], tmp[:, h % 4, :]).then_inc(S("yb_hi_out"), 1)

            def parts(name, evacuate=None):
                n, panels, outs = PART[name]
                for i in range(panels):
                    if n + i + 2 != BASE["ffn2"] + 1:
                        split(n + i + 2)
                    if evacuate:
                        for t in range(outs // panels):
                            evacuate(i * outs // panels + t)

            def m_hi_out(t):
                act.wait_ge(S("m_h"), t + 1)
                act.copy(m_hi[:, t, :], tmp[:, t % 4, :]).then_inc(S("m_hi_out"), 1)

            parts("b_proj", m_hi_out)
            parts("w_out")

            norm("n2", x, lambda eng, k: wait_x(eng, "mixer", k), panel=BASE["ffn2"] + 1)
            swiglu("ffn2")

            down("ffn2")

            act.wait_ge(S("mod_made"), 2)
            norm("p1", x, lambda eng, k: wait_x(eng, "ffn2", k), panel=BASE["mix2"] + 1, shift=lambda k: mod[:, k:k + 1])
            n = PART["u2"][0]
            for i in range(2):
                for t in range(2):
                    if t == 1:
                        split(n + i + 2)
                    act.wait_ge(S("pe_done"), used(n + i, 2 * t + 2))
                    act.copy(u2[:, 2 * i + t, :], bank_of(2 * i + t)[:]).then_inc(S("u2_out"), 1)
            def flipped():
                for g in range(4):
                    act.wait_ge(S("bias_flipped"), g + 1)
                    act.copy(bias[:, 2 * g:2 * g + 2, :], B[4 + g][:].rearrange("p (h k) -> p h k", h=2)).then_inc(S("bias_out"), 1)

            def s5_inputs(part):
                for g in range(4 * part, 4 * part + 4):
                    act.wait_ge(S("bb_t"), g + 1)
                    act.copy(bbT[:, part, 4 * (g % 4):4 * (g % 4) + 4, :],
                             B[4 + g % 4][:].rearrange("p (s c) -> p s c", s=4)).then_inc(S("bb_t_out"), 1)

            n = PART["q2"][0]
            split(n + 2)
            for b in range(TB):
                if b == TB - 1:
                    split(n + 3)
                act.wait_ge(S("pe_done"), used(n + 1, b + 1))
                act.copy(q2_raw[:, b, :], B[b][:]).then_inc(S("q2_out"), 1)
            act.wait_ge(S("q2_out"), TB)
            act.activation(q_sq[:], q2_raw[:], ACT.Square).then_inc(S("qk2_sq"), 1)
            s5_inputs(0)
            n = PART["kv2"][0]
            for b in range(TB):
                act.wait_ge(S("pe_done"), used(n, b + 1))
                act.copy(k2_raw[:, b, :], B[b][:, 0:NKV * QK]).then_inc(S("k2_out"), 1)
                for twice in range(2):
                    act.copy(v2[:, b, :, twice, :], B[b][:, NKV * QK:2 * NKV * QK].rearrange("p (n d) -> p n d", n=NKV)).then_inc(S("v2_out"), 1)
            act.wait_ge(S("k2_out"), TB)
            act.activation(k_sq[:], k2_raw[:], ACT.Square).then_inc(S("qk2_sq"), 1)
            split(n + 2)
            flipped()
            act.wait_ge(S("qk2_ssq"), 2)
            act.activation(stat[:, 0:40], stat[:, 0:40], ACT.Sqrt, scale=1.0 / QK, bias=eps_col).then_inc(S("qk2_root"), 1)
            s5_inputs(1)
            for f in range(6):
                act.wait_ge(S("qk2_t"), f + 1)
                dst = q2T[:, f, :] if f < 4 else k2T[:, f - 4, :]
                act.copy(dst, B[5 + f % 2][:]).then_inc(S("qk2_t_out"), 1)
            def sw_exp(u):
                b, n = SW_UNITS[u]
                lo = P if b == 0 else 0
                act.wait_ge(S("sw_max"), u + 1)
                for h in range(4):
                    p = prob[:, u % 2, h, lo:]
                    act.activation(p, p, ACT.Exp, bias=sw_cols(48, u)[:, h:h + 1], accum_out=sw_cols(56, u)[:, h:h + 1]).then_inc(S("sw_exp"), 1)
                act.activation(sw_cols(64, u), sw_cols(64, u), ACT.Exp).then_inc(S("sw_exp"), 1)

            def sw_scaled(u):
                lo = P if SW_UNITS[u][0] == 0 else 0
                act.wait_ge(S("sw_scale"), u + 1)
                for h in range(4):
                    p = prob[:, u % 2, h, lo:]
                    act.activation(p, p, ACT.Copy, scale=sw_cols(80, u)[:, h:h + 1]).then_inc(S("sw_p"), 1)

            def sw_turned(u):
                if u >= 2:
                    act.wait_ge(S("sw_pv"), u - 1)
                for i, kb in enumerate(SW_BLOCKS[u]):
                    act.wait_ge(S("sw_t"), SW_BEFORE[u] + i + 1)
                    act.copy(pT[:, u % 2, kb, :], B[5 + kb][:]).then_inc(S("sw_t_out"), 1)

            def sw_out(u):
                b, n = SW_UNITS[u]
                act.wait_ge(S("sw_pv"), u + 1)
                o = B[7][:].rearrange("p (j two q) -> p j two q", j=2, two=2)
                for half in range(2):
                    rows_of = slice(64 * half, 64 * half + 64)
                    act.copy(yat[rows_of, 2 * n:2 * n + 2, b * P:(b + 1) * P], o[rows_of, :, half, :]).then_inc(S("sw_out"), 1)

            def s5_gelu(tiles):
                for t in tiles:
                    act.wait_ge(S("s5_y"), t + 1)
                    act.activation(u2[:, t, :], u2[:, t, :], ACT.Gelu_apprx_tanh).then_inc(S("z_out"), 1)
                for t in tiles:
                    act.wait_ge(S("z_out"), t + 1)
                    act.copy(z_hi[:, t, :], u2[:, t, :]).then_inc(S("z_hi_out"), 1)

            for u in range(len(SW_UNITS)):
                sw_exp(u)
                sw_scaled(u)
                sw_turned(u)
                sw_out(u)
                if u == len(SW_UNITS) - 2:
                    act.wait_ge(S("bu"), 2 * NS)
                    s5_gelu(range(3))
            s5_gelu((3,))
            norm("pa", yat, None, hi=h_hi[:, 4:8], width=T)
            n = PART["glu"][0]
            split(n + 2)
            for t in range(4):
                act.wait_ge(S("pe_done"), used(n, t + 1))
                act.activation(gate[:, t, :], glu_bank(t)[:], ACT.Sigmoid, bias=col("b_glu_2", t)).then_inc(S("glu_gate"), 1)
            norm("ps", u2, lambda eng, k: eng.wait_ge(S("glu_out"), k + 1), hi=h_hi[:, 0:4], width=T)
            n = PART["w_out2"][0]
            for i in range(3):
                split(n + i + 2)

            norm("p2", x, lambda eng, k: wait_x(eng, "mix2", k), panel=BASE["ffn3"] + 1, shift=lambda k: mod[:, 24 + k:25 + k])
            base = BASE["ffn3"]
            with act.Fori(0, GU_STEPS) as i:
                for half in range(2):
                    split(i * 2 + (base + 2 + half), base + half)
                    for t in range(2):
                        act.wait_ge(S("pe_done"), i * 8 + (4 * base + 4 * half + 2 * t + 2))
                        act.wait_ge(S("hid"), i * 2 + (HID["ffn3"] + t + 1))
                        act.activation(tmp[:, 2 * half + t, :], B[2 * half + t][:], ACT.Identity,
                                       scale=col_at("conv_w_2:2", i * 2, KF * half + t),
                                       bias=col_at("conv_b_2", i * 2, KF * half + t)).then_inc(S("ffn3_own"), 1)
                for t in range(2):
                    act.wait_ge(S("ffn3_conv"), i * 8 + (2 * t + 14))
                    act.activation(tmp[:, 2 + t, :], tmp[:, 2 + t, :], ACT.Silu).then_inc(S("silu"), 1)
                for t in range(2):
                    act.wait_ge(S("hid"), i * 2 + (HID["ffn3"] + t + 3))
                    act.copy(hid_hi[:, bass.ds(i * 2 + t, 1), :], tmp[:, 4 + t:5 + t, :]).then_inc(S("hid_hi"), 1)
            down("ffn3")
            for b in range(TB):
                act.wait_ge(S("out_t"), 2 * b + 2)
                act.copy(x_in[:, b, T:D], B[(2 * b + 1) % 4][:]).then_inc(S("out_turned1"), 1)

        @block.vector
        def _(dve):
            done = Steps(dve, S("dve_done"))

            def split(n, i=None):
                if i is None:
                    if n >= END:
                        return
                    i = n
                dve.wait_ge(S("w_hi_done"), n + 1)
                if not isinstance(n, int) or n:
                    dve.wait_ge(S("w_split"), n)
                s = i % 2
                dve.tensor_tensor(w_lo[s][:], w_raw[s][:], w_hi[s][:].bitcast(F32), ALU.subtract).then_inc(S("w_split"), 1)

            def norm(name, tiles, gain, shift=None, hi=None, lo=None, width=D):
                hi, lo = (h_hi, h_lo) if hi is None else (hi, lo)
                count, at = NORM_PARTS[name][0], NORM[name]
                v, vr = tmp[:, 0, :], tmp[:, 1, :]
                eps = eps_width_col[width]
                dve.wait_ge(S("norm_root"), NORMS.index(name) + 1)
                done(dve.scalar_tensor_tensor(v, B[7][:], eps, rstd[:], ALU.add, ALU.mult))
                done(dve.scalar_tensor_tensor(vr, v, -0.5 / width, rstd[:], ALU.mult, ALU.mult))
                done(dve.scalar_tensor_tensor(rstd[:], vr, 1.5, rstd[:], ALU.add, ALU.mult))
                for k in range(count + 1):
                    if k < count:
                        if k >= 4:
                            dve.wait_ge(S("norm_split"), at + k - 3)
                        dve.scalar_tensor_tensor(tmp[:, 2 + k % 4, :], tiles[:, k, :], gain(k), rstd[:],
                                                 ALU.mult, ALU.mult).then_inc(S("norm_h"), 1)
                    if k:
                        dve.wait_ge(S("norm_hi"), at + k)
                        h, hi_k = tmp[:, 2 + (k - 1) % 4, :], hi[:, k - 1, :].bitcast(F32)
                        if shift is None:
                            ins = dve.tensor_tensor(lo[:, k - 1, :], h, hi_k, ALU.subtract)
                        else:
                            ins = dve.scalar_tensor_tensor(lo[:, k - 1, :], h, shift(k - 1), hi_k, ALU.add, ALU.subtract)
                        ins.then_inc(S("norm_split"), 1)

            def hid_lo_of(name, i, t, slot):
                dve.wait_ge(S("hid_hi"), i * 2 + (HID[name] + t + 1))
                dve.tensor_tensor(hid_lo[:, bass.ds(i * 2 + t, 1), :], tmp[:, slot:slot + 1, :],
                                  hid_hi[:, bass.ds(i * 2 + t, 1), :].bitcast(F32), ALU.subtract).then_inc(S("hid_split"), 1)

            def turns(st):
                fh_c, fl_c = (s5[:, row, bass.ds(st, 1)] for row in (13, 14))
                r = rot_r[:]
                dve.wait_ge(S("rot_read"), st + 1)
                dve.tensor_scalar(rot_n[:], rot_t[:], fh_c, ROUND, ALU.mult, ALU.add).then_inc(S("rot_step"), 1)
                dve.tensor_scalar(r, rot_t[:], fh_c, None, ALU.mult).then_inc(S("rot_step"), 1)
                dve.wait_ge(S("rot_step"), st * 5 + 2)
                dve.scalar_tensor_tensor(r, rot_n[:], ROUND, r, ALU.subtract, ALU.subtract).then_inc(S("rot_step"), 1)
                dve.wait_ge(S("rot_step"), st * 5 + 3)
                dve.scalar_tensor_tensor(r, rot_t[:], fl_c, r, ALU.mult, ALU.subtract).then_inc(S("rot_step"), 1)
                dve.wait_ge(S("rot_step"), st * 5 + 4)
                dve.tensor_scalar(rot_n[:], r, 1.0, ROUND, ALU.mult, ALU.add).then_inc(S("rot_step"), 1)
                dve.wait_ge(S("rot_step"), st * 5 + 5)
                dve.scalar_tensor_tensor(r, rot_n[:], ROUND, r, ALU.subtract, ALU.subtract).then_inc(S("rot_turns"), 1)

            def modulation(g):
                dve.wait_ge(S("mod_acc_free"), g + 1)
                for k in range(KD):
                    dve.wait_ge(S(f"mod_landed{k % MOD_SLOTS}"), g * 32 + (k // MOD_SLOTS + 1) * 16)
                    if k == 0:
                        ins = dve.tensor_scalar(mod_acc[:], mod_raw[:, k % MOD_SLOTS, :], small[:, k:k + 1], None, ALU.mult)
                    else:
                        dve.wait_ge(S("mod_step"), g * MOD_STEPS + (k + MOD_SLOTS))
                        ins = dve.scalar_tensor_tensor(mod_acc[:], mod_raw[:, k % MOD_SLOTS, :], small[:, k:k + 1], mod_acc[:], ALU.mult, ALU.add)
                    ins.then_inc(S("mod_step"), 1)
                dve.wait_ge(S("mod_step"), g * MOD_STEPS + (KD + MOD_SLOTS))
                dve.tensor_copy(mod_hi[:], mod_acc[:]).then_inc(S("mod_step"), 1)
                dve.wait_ge(S("mod_step"), g * MOD_STEPS + (KD + 1 + MOD_SLOTS))
                dve.tensor_tensor(mod_lo[:], mod_acc[:], mod_hi[:].bitcast(F32), ALU.subtract).then_inc(S("mod_step"), 1)

            def swiglu(name):
                base = BASE[name]
                if name == "ffn2":
                    dve.wait_ge(S("rot_t_made"), 1)
                for start, stop, mods, rots in PHASES[name]:
                    if start == BESIDE_STEPS:
                        groups = sum(b - a for f in list(PHASES)[:list(PHASES).index(name) + 1] for a, b, m, _ in PHASES[f] if m)
                        dve.wait_ge(S("mod_acc_free"), groups + 1)
                    with dve.Fori(start, stop) as i:
                        if rots:
                            turns(rotation(i, start, rots, 0))
                        if mods:
                            modulation(i + MOD_AT[name])
                        if rots > 1:
                            turns(rotation(i, start, rots, 1))
                        split(i * 2 + (base + 2), base)
                        for t in range(2):
                            dve.wait_ge(S("pe_done"), i * 8 + (4 * base + 4 + 2 * t + 2))
                            dve.wait_ge(S("silu"), i * 2 + (HID[name] + t + 3))
                            dve.wait_ge(S("hid_split"), i * 2 + (HID[name] + t + 1))
                            dve.tensor_tensor(tmp[:, 2 + t, :], tmp[:, t, :], B[2 + t][:], ALU.mult).then_inc(S("hid"), 1)
                        split(i * 2 + (base + 3), base + 1)
                        for t in range(2):
                            hid_lo_of(name, i, t, 2 + t)
                        for r in range(2, rots):
                            turns(rotation(i, start, rots, r))
                first = 4 * MOD_AT[name]
                last_col = 4 * groups
                dve.tensor_tensor(mod[:, first:last_col], B[6][:, 0:2 * (last_col - first):2], cols("b_mod_2")[:, first:last_col],
                                  ALU.add).then_inc(S("mod_made"), 1)

            def down(name, factor, beside=()):
                base = BASE[name] + 2 * GU_STEPS
                for c in range(DOWN_PANELS):
                    if c % 4 == 3:
                        for k in (c // 4 * 2, c // 4 * 2 + 1):
                            dve.wait_ge(S("pe_done"), used(base + c, 2 * (k % 2) + 2))
                            dve.scalar_tensor_tensor(x[:, k, :], down_bank(name, k)[:], factor(k), x[:, k, :], ALU.mult, ALU.add).then_inc(S(name + "_x"), 1)
                    if c < DOWN_PANELS - 1:
                        split(base + c + 2)
                    if c < len(beside):
                        beside[c]()

            dve.sem_inc(S("hid"), 2)
            dve.sem_inc(S("hid_split"), 2)
            for name in ("ffn1", "ffn2", "ffn3"):
                dve.sem_inc(S(name + "_x"), 4)
            dve.sem_inc(S("ffn3_conv"), 8)
            dve.sem_inc(S("mod_step"), MOD_SLOTS)
            for i, value in ((20, EPS), (21, math.pi / 2.0)):
                done(dve.memset(small[:, i:i + 1], value))
            dve.memset(small[:, 22:23], LN_EPS).then_inc(S("cols_made"), 1)
            dve.wait_ge(S("pool_done"), 1)
            done(dve.tensor_copy(ones_r[:], ones[:, 0:2]))
            for k in range(KD):
                dve.wait_ge(S("x_t"), k + 1)
                dve.tensor_copy(x[:, k, :], B[2 + k % 4][:]).then_inc(S("x_turned"), 1)
            dve.wait_ge(S("rows_t"), 3)
            for tile in range(3):
                dve.tensor_copy(vec[:, tile, :ROW_COUNTS[tile]], B[0][:, tile * P:tile * P + ROW_COUNTS[tile]]).then_inc(S("vec_made"), 1)
            dve.wait_ge(S("vec_made"), 3)
            dve.wait_ge(S("band_t"), 1)
            dve.tensor_copy(band[:], B[1][0:NQ, 0:BAND]).then_inc(S("band_made"), 1)
            norm("n1", x, lambda k: col("ffn1_norm", k))

            def exp(out, v, n):
                k, q, power = (s5[:, row, 0:n] for row in (17, 18, 19))
                done(dve.tensor_scalar(v, v, EXP_RANGE[0], EXP_RANGE[1], ALU.max, ALU.min))
                done(dve.tensor_scalar(k, v, 1.0 / LN_2, ROUND, ALU.mult, ALU.add))
                done(dve.tensor_scalar(k, k, ROUND, None, ALU.subtract))
                for part in (LN_2_HI, LN_2 - LN_2_HI):
                    done(dve.scalar_tensor_tensor(v, k, -part, v, ALU.mult, ALU.add))
                done(dve.tensor_scalar(q, v, 1.0 / math.factorial(7), None, ALU.mult))
                for i in range(6, 0, -1):
                    done(dve.scalar_tensor_tensor(q, q, 1.0 / math.factorial(i), v, ALU.add, ALU.mult))
                done(dve.tensor_scalar(k, k, 127.0, 2.0**23, ALU.add, ALU.mult))
                done(dve.tensor_copy(power.bitcast(I32), k))
                done(dve.scalar_tensor_tensor(out, q, 1.0, power, ALU.add, ALU.mult))

            def reduce_angle(a, n):
                done(dve.tensor_scalar(n, a, 1.0 / TWO_PI, ROUND, ALU.mult, ALU.add))
                done(dve.tensor_scalar(n, n, ROUND, None, ALU.subtract))
                for part in (PI_1, PI_2, PI_3):
                    done(dve.scalar_tensor_tensor(a, n, -part, a, ALU.mult, ALU.add))

            lr, dt, mag, th, n_, sn, cs, fh, fl, tv, t2, a_re, a_im, f_re, f_im = (
                s5[:, i, :] for i in (0, 2, 3, 4, 5, 6, 7, 13, 14, 15, 16, 8, 9, 11, 12))
            li = cols("lam_im_2")
            neg_lam = small[:, 12:13]

            def lambda_exponents():
                dve.wait_ge(S("spread_landed"), 16 * 11)
                for i in range(2):
                    done(dve.tensor_tensor(lam_in[:, 2 * i, :], lam_in[:, 2 * i, :], lam_in[:, 2 * i + 1, :], ALU.mult))
                    done(dve.tensor_reduce(small[:, 8 + i:9 + i], lam_in[:, 2 * i, :], AX.X, ALU.add))
                for i in (0, 2):
                    done(dve.tensor_scalar(gains[:, i, :], gains[:, i, :], QK**-0.5, None, ALU.mult))

            def lambda_value():
                exp(small[:, 10:12], small[:, 8:10], 2)
                done(dve.tensor_tensor(neg_lam, small[:, 11:12], small[:, 10:11], ALU.subtract))
                done(dve.tensor_scalar(neg_lam, neg_lam, -LAM_INIT, None, ALU.add))

            def s5_step():
                done(dve.tensor_scalar(lr, cols("lam_re_2"), -1e-4, None, ALU.min))
                for half in range(2):
                    own = slice(64 * half, 64 * half + 64)
                    done(dve.tensor_copy(s5[own, 15, :], log_dt[own, half::2]))
                exp(dt, tv, NS)

            def s5_decay():
                done(dve.tensor_tensor(th, dt, li, ALU.mult))
                done(dve.tensor_tensor(tv, dt, lr, ALU.mult))
                exp(mag, tv, NS)

            def s5_angle():
                reduce_angle(th, n_)
                done(dve.tensor_scalar(fh, th, 2.0**15 / TWO_PI, ROUND, ALU.mult, ALU.add))
                done(dve.tensor_scalar(fh, fh, ROUND, 2.0**-15, ALU.subtract, ALU.mult))
                done(dve.tensor_copy(fl, th))
                for part in (PI_1, PI_2, PI_3):
                    done(dve.scalar_tensor_tensor(fl, fh, -part, fl, ALU.mult, ALU.add))
                done(dve.tensor_scalar(fl, fl, 1.0 / TWO_PI, None, ALU.mult))
                done(dve.tensor_scalar(th, th, PI_LOW, -PI_LOW, ALU.min, ALU.max))

            def rotary_angles():
                posf = stat[:, 0:TB]
                done(dve.tensor_copy(posf, pos_i[:]))
                for r in range(ROT):
                    inv = float(np.float32(500000.0) ** np.float32(-np.float32(2 * r) / np.float32(2 * ROT)))
                    done(dve.tensor_scalar(ang[:, 0, :, r], posf, inv, None, ALU.mult))
                reduce_angle(ang[:, 0], ang[:, 1])
                dve.tensor_scalar(ang[:, 0], ang[:, 0], PI_LOW, -PI_LOW, ALU.min, ALU.max).then_inc(S("angles"), 1)

            def s5_eigenvalue():
                dve.wait_ge(S("sines"), 4)
                done(dve.tensor_tensor(a_re, mag, cs, ALU.mult))
                done(dve.tensor_tensor(a_im, mag, sn, ALU.mult))
                done(dve.tensor_scalar(a_re, a_re, -1.0, None, ALU.add))
                done(dve.tensor_tensor(tv, lr, lr, ALU.mult))
                done(dve.tensor_tensor(t2, li, li, ALU.mult))
                done(dve.tensor_tensor(tv, tv, t2, ALU.add))
                done(dve.reciprocal(tv, tv))

            def s5_factors():
                done(dve.tensor_tensor(f_re, a_re, lr, ALU.mult))
                done(dve.tensor_tensor(t2, a_im, li, ALU.mult))
                done(dve.tensor_tensor(f_re, f_re, t2, ALU.add))
                done(dve.tensor_tensor(f_re, f_re, tv, ALU.mult))
                done(dve.tensor_tensor(f_im, a_im, lr, ALU.mult))
                done(dve.tensor_tensor(t2, a_re, li, ALU.mult))
                done(dve.tensor_tensor(f_im, f_im, t2, ALU.subtract))
                done(dve.tensor_tensor(f_im, f_im, tv, ALU.mult))

            dve.wait_ge(S("silu_c"), 1)
            swiglu("ffn1")
            down("ffn1", lambda k: 0.5, (lambda_exponents, lambda_value, s5_step, s5_decay, s5_angle, rotary_angles, lambda: None,
                                         lambda: None, lambda: None, lambda: None, lambda: None, s5_eigenvalue, s5_factors))

            norm("nm", x, lambda k: col("mix_norm", k))

            def part_splits(name):
                n, panels, _ = PART[name]
                for i in range(panels):
                    split(n + i + 2)

            def spread(ap, shape):
                return ap.unsqueeze(2).to_broadcast(shape)

            part_splits("v_gm")
            dve.wait_ge(S("v_gm_out"), TB)
            for b in range(TB):
                done(dve.bn_stats(tmp[:, 4, 6 * b:6 * b + 6], vg[:, b, :]))
                done(dve.bn_aggr(tmp[:, 5, 2 * b:2 * b + 2], tmp[:, 4, 6 * b:6 * b + 6]))
            dve.tensor_copy(stat[:, 36:40], tmp[:, 5, 1:2 * TB:2]).then_inc(S("ln_var"), 1)
            part_splits("u_gm")
            dve.wait_ge(S("ln_root"), 1)
            done(dve.reciprocal(stat[:, 40:44], stat[:, 40:44]))
            dve.wait_ge(S("gmlp_landed"), 64)
            for b in range(TB):
                done(dve.tensor_scalar(vg[:, b, :], vg[:, b, :], tmp[:, 5, 2 * b:2 * b + 1], stat[:, 40 + b:41 + b],
                                       ALU.subtract, ALU.mult))
                done(dve.tensor_tensor(vg[:, b, :], vg[:, b, :], ln_g[:], ALU.mult))
                dve.tensor_tensor(vg[:, b, :], vg[:, b, :], ln_b[:], ALU.add).then_inc(S("ln_out"), 1)

            def heads(j, between=None):
                raw = qk_raw[j % 2][:].rearrange("p b (h d) -> p (b h) d", d=QK)
                n = TB * HEADS
                dve.wait_ge(S("qk_sq"), j + 1)
                dve.tensor_reduce(stat[:, 0:n], tmp[:, 0:4, :].rearrange("p b (h d) -> p (b h) d", d=QK), AX.X, ALU.add).then_inc(S("qk_ssq"), 1)
                dve.wait_ge(S("qk_root"), j + 1)
                done(dve.reciprocal(stat[:, 0:n], stat[:, 0:n]))
                done(dve.tensor_tensor(raw, raw, spread(stat[:, 0:n], [P, n, QK]), ALU.mult))
                done(dve.tensor_tensor(raw, raw, gains[:, j // 2:j // 2 + 1, :].to_broadcast([P, n, QK]), ALU.mult))
                if between is not None:
                    split(between)
                raw4 = qk_raw[j % 2][:].rearrange("p b (h d) -> p b h d", d=QK)
                r1, r2 = raw4[:, :, :, 0:ROT], raw4[:, :, :, ROT:2 * ROT]
                shape = [P, TB, HEADS, ROT]
                cos_b, sin_b = (a[:].unsqueeze(2).to_broadcast(shape) for a in (cos_t, sin_t))
                t = [tmp[:, 0, 256 * (i % 2):256 * (i % 2) + 256] if i < 2 else tmp[:, 1, 256 * (i % 2):256 * (i % 2) + 256] for i in range(4)]
                t = [a.rearrange("p (b h d) -> p b h d", b=TB, h=HEADS) for a in t]
                dve.wait_ge(S("qk_ssq"), j + 1)
                done(dve.tensor_tensor(t[0], r1, cos_b, ALU.mult))
                done(dve.tensor_tensor(t[1], r2, sin_b, ALU.mult))
                done(dve.tensor_tensor(t[2], r2, cos_b, ALU.mult))
                done(dve.tensor_tensor(t[3], r1, sin_b, ALU.mult))
                done(dve.tensor_tensor(r1, t[0], t[1], ALU.subtract))
                dve.tensor_tensor(r2, t[2], t[3], ALU.add).then_inc(S("qk_done"), 1)

            def gmlp():
                dve.wait_ge(S("gmlp_landed"), 64)
                dve.wait_ge(S("u_gm_out"), 4)
                for f in range(4):
                    y = tmp[:, 4 + f % 2, :]
                    dve.wait_ge(S("f_done"), f + 1)
                    dve.tensor_tensor(y.rearrange("p (c t) -> p c t", c=TB), B[4 + f][:].rearrange("p (c t) -> p c t", c=TB),
                                      bs[:, f:f + 1, :].to_broadcast([P, TB, P]), ALU.add).then_inc(S("ya_h"), 1)
                    dve.wait_ge(S("ya_h"), 2 * f + 1)
                    dve.tensor_tensor(y, y, u_g[:, f, :], ALU.mult).then_inc(S("ya_h"), 1)
                    dve.wait_ge(S("ya_hi_out"), f + 1)
                    dve.tensor_tensor(ya_lo[:, f, :], y, ya_hi[:, f, :].bitcast(F32), ALU.subtract).then_inc(S("ya_split"), 1)

            for j in range(3):
                part_splits(f"qk{j}")
                if j == 2:
                    gmlp()
                heads(j, PART["v0"][0] + 2 if j == 2 else None)
            split(PART["v0"][0] + 3)
            part_splits("qk3")
            heads(3)
            part_splits("v1")
            part_splits("g_a")
            n = PART["a_proj"][0]
            for i in range(2):
                for t in range(4):
                    dve.wait_ge(S("pe_done"), used(n + i, t + 1))
                    g = ga[:, 4 * i + t, :]
                    dve.wait_ge(S("g_a_out"), 4 * i + t + 1)
                    dve.tensor_tensor(g, g, bank_of(t)[:], ALU.mult).then_inc(S("a_proj_out"), 1)
                split(n + i + 2)
            part_splits("g_b")

            def row_max(u):
                keys = (UNITS[u][1] + 1) * P
                for m in range(2):
                    bank = 2 * (u % 3) + m
                    dve.wait_ge(S("at_s"), 2 * u + m + 1)
                    dve.tensor_reduce(stat[:, bank:bank + 1], B[bank][:, :keys], AX.X, ALU.max,
                                      negate=True).then_inc(S("at_max"), 1)

            def differ(u):
                keys = (UNITS[u][1] + 1) * P
                s = u % 2
                r = stat[:, 10 + 2 * s:12 + 2 * s]
                dve.wait_ge(S("at_exp"), 2 * u + 2)
                done(dve.reciprocal(r, stat[:, 6 + 2 * s:8 + 2 * s]))
                done(dve.tensor_tensor(r[:, 1:2], r[:, 1:2], neg_lam, ALU.mult))
                if u >= 2:
                    dve.wait_ge(S("at_t"), u - 1)
                a = tmp[:, 4 + s, :keys]
                dve.tensor_scalar(a, tmp[:, 2 * s, :keys], r[:, 0:1], None, ALU.mult).then_inc(S("at_a"), 1)
                dve.wait_ge(S("at_a"), 2 * u + 1)
                dve.scalar_tensor_tensor(a, tmp[:, 2 * s + 1, :keys], r[:, 1:2], a, ALU.mult, ALU.add).then_inc(S("at_a"), 1)

            row_max(0)
            row_max(1)
            for u in range(len(UNITS)):
                differ(u)
                if u + 2 < len(UNITS):
                    row_max(u + 2)
            dve.wait_ge(S("at_root"), 1)
            done(dve.reciprocal(stat[:, 16:48], stat[:, 16:48]))
            root = stat[:, 16:48].rearrange("p (i h) -> p i h", i=TB)

            def scale(h):
                o = o_tok[:, :, h * P:(h + 1) * P]
                dve.tensor_tensor(o, o, root[:, :, h:h + 1].to_broadcast([P, TB, P]), ALU.mult).then_inc(S("o_scaled"), 1)

            scale(0)
            scale(1)
            for h in range(HEADS + 1):
                if h < HEADS:
                    if h >= 4:
                        dve.wait_ge(S("yb_split"), h - 3)
                    dve.wait_ge(S("yb_t"), h + 1)
                    dve.tensor_scalar(tmp[:, h % 4, :], B[4 + h % 4][:], col("b_subln", 0), 1.0 - LAM_INIT, ALU.mult, ALU.mult).then_inc(S("yb_h"), 1)
                if h + 2 < HEADS:
                    scale(h + 2)
                if h:
                    dve.wait_ge(S("yb_hi_out"), h)
                    dve.tensor_tensor(yb_lo[:, h - 1, :], tmp[:, (h - 1) % 4, :], yb_hi[:, h - 1, :].bitcast(F32), ALU.subtract).then_inc(S("yb_split"), 1)
            n, panels, _ = PART["b_proj"]
            for i in range(panels):
                for t in range(2 * i, 2 * i + 2):
                    y = tmp[:, t % 4, :]
                    dve.wait_ge(S("pe_done"), used(n + i, 2 * (t % 2) + 2))
                    if t >= 4:
                        dve.wait_ge(S("m_split"), t - 3)
                    dve.tensor_tensor(y, gb[:, t, :], bank_of(t)[:], ALU.mult).then_inc(S("b_proj_out"), 1)
                    dve.wait_ge(S("b_proj_out"), t + 1)
                    dve.tensor_tensor(y, y, ga[:, t, :], ALU.add).then_inc(S("m_h"), 1)
                split(n + i + 2)
                for t in range(2 * i, 2 * i + 2):
                    dve.wait_ge(S("m_hi_out"), t + 1)
                    dve.tensor_tensor(m_lo[:, t, :], tmp[:, t % 4, :], m_hi[:, t, :].bitcast(F32), ALU.subtract).then_inc(S("m_split"), 1)
            n, panels, _ = PART["w_out"]
            for i in range(panels):
                for t in range(2 * i, 2 * i + 2):
                    dve.wait_ge(S("pe_done"), used(n + i, 2 * (t % 2) + 2))
                    dve.tensor_tensor(x[:, t, :], x[:, t, :], bank_of(t)[:], ALU.add).then_inc(S("mixer_x"), 1)
                if i < panels - 1:
                    split(n + i + 2)

            norm("n2", x, lambda k: col("ffn2_norm", k))
            swiglu("ffn2")

            down("ffn2", lambda k: 0.5)

            dve.wait_ge(S("mod_made"), 2)
            for i, name in enumerate(("norm1_w_2", "norm2_w_2")):
                at = 8 + 24 * i
                done(dve.scalar_tensor_tensor(gain2[:, i, :], mod[:, at:at + 8], 1.0, cols(name), ALU.add, ALU.mult))
            norm("p1", x, lambda k: gain2[:, 0, k:k + 1], lambda k: mod[:, k:k + 1])
            n, panels, _ = PART["u2"]
            for i in range(panels):
                split(n + i + 2)
            dve.wait_ge(S("s5_landed"), 96)
            shape = [P, NS, SG]
            f_re_b, f_im_b = (s5[:, row, :].unsqueeze(2).to_broadcast(shape) for row in (11, 12))
            t = [tmp[:, 4, 256 * i:256 * i + 256].rearrange("p (s h) -> p s h", s=NS) for i in range(2)]
            for part, (first, second, op) in enumerate(((0, 1, ALU.subtract), (1, 0, ALU.add))):
                done(dve.tensor_tensor(t[0], b_in[:, first], f_re_b, ALU.mult))
                done(dve.tensor_tensor(t[1], b_in[:, second], f_im_b, ALU.mult))
                done(dve.tensor_tensor(bb[:, part], t[0], t[1], op))
            def blocks(part):
                for s4 in range(4):
                    for half in range(2):
                        own = slice(64 * half, 64 * half + 64)
                        at = s4 * 2 * SG + half * SG
                        dve.tensor_copy(bd[own, s4::4, at:at + SG], bb[own, part, s4::4, :]).then_inc(S("bd_made"), 1)

            dve.wait_ge(S("zeroed"), 1)
            blocks(0)
            n = PART["q2"][0]
            split(n + 2)
            split(n + 3)
            dve.wait_ge(S("bb_t"), 4)
            blocks(1)
            dve.wait_ge(S("qk2_sq"), 1)
            dve.tensor_reduce(stat[:, 0:32], q_sq[:].rearrange("p b (h d) -> p (b h) d", d=QK), AX.X, ALU.add).then_inc(S("qk2_ssq"), 1)
            dve.wait_ge(S("qk2_sq"), 2)
            dve.tensor_reduce(stat[:, 32:40], k_sq[:].rearrange("p b (h d) -> p (b h) d", d=QK), AX.X, ALU.add).then_inc(S("qk2_ssq"), 1)
            split(PART["kv2"][0] + 2)
            dve.wait_ge(S("qk2_root"), 1)
            done(dve.reciprocal(stat[:, 0:40], stat[:, 0:40]))
            q_v = q2_raw[:].rearrange("p b (h d) -> p (b h) d", d=QK)
            k_v = k2_raw[:].rearrange("p b (h d) -> p (b h) d", d=QK)
            done(dve.tensor_tensor(q_v, q_v, spread(stat[:, 0:32], [P, 32, QK]), ALU.mult))
            dve.tensor_tensor(q_v, q_v, gains[:, 2:3, :].to_broadcast([P, 32, QK]), ALU.mult).then_inc(S("qk2_made"), 1)
            done(dve.tensor_tensor(k_v, k_v, spread(stat[:, 32:40], [P, 8, QK]), ALU.mult))
            dve.tensor_tensor(k_v, k_v, gains[:, 3:4, :].to_broadcast([P, 8, QK]), ALU.mult).then_inc(S("qk2_made"), 1)

            def s5_outputs():
                dve.wait_ge(S("zeroed"), 2)
                for part, sign in enumerate((1.0, -1.0)):
                    dve.wait_ge(S("c_t"), part + 1)
                    c_v = B[4 + 3 * part][:].rearrange("p (c n) -> p c n", c=4)
                    for s4 in range(4):
                        for half in range(2):
                            own = slice(64 * half, 64 * half + 64)
                            at = s4 * 2 * SG + half * SG
                            dve.tensor_scalar(cT[own, part, s4::4, at:at + SG], c_v[own, :, at:at + SG], sign, None, ALU.mult).then_inc(S("c_out"), 1)

            def sw_max(u):
                b, n = SW_UNITS[u]
                lo = P if b == 0 else 0
                p = prob[:, u % 2]
                if u == 0:
                    dve.wait_ge(S("bias_out"), 4)
                if u >= 2:
                    dve.wait_ge(S("sw_t"), SW_BEFORE[u - 1])
                for odd in range(2):
                    first = 4 * n + odd
                    dve.wait_ge(S("sw_s"), 2 * u + odd + 1)
                    dve.tensor_tensor(p[:, odd:odd + 3:2, lo:], B[5 + odd][:].rearrange("p (h k) -> p h k", h=2)[:, :, lo:],
                                      bias[:, first:first + 3:2, lo:], ALU.add).then_inc(S("sw_read"), 1)
                sinks = sink[:, 4 * n:4 * n + 4]
                dve.wait_ge(S("sw_read"), 2 * u + 2)
                done(dve.tensor_reduce(sw_cols(72, u), p[:, :, lo:], AX.X, ALU.max))
                done(dve.tensor_tensor(sw_cols(72, u), sw_cols(72, u), sinks, ALU.max))
                done(dve.tensor_tensor(sw_cols(64, u), sinks, sw_cols(72, u), ALU.subtract))
                dve.tensor_scalar(sw_cols(48, u), sw_cols(72, u), -1.0, None, ALU.mult).then_inc(S("sw_max"), 1)

            def sw_scale(u):
                dve.wait_ge(S("sw_exp"), 5 * (u + 1))
                done(dve.tensor_tensor(sw_cols(80, u), sw_cols(56, u), sw_cols(64, u), ALU.add))
                dve.reciprocal(sw_cols(80, u), sw_cols(80, u)).then_inc(S("sw_scale"), 1)

            def scan_in(st):
                re, im = B[2 * (st % 2)], B[2 * (st % 2) + 1]
                r = rot[:, st % ROT_SLOTS]
                dve.wait_ge(S("bu"), 2 * st + 2)
                dve.wait_ge(S(f"rot_landed{st % ROT_SLOTS}"), 16 * (st // ROT_SLOTS + 1))
                if st:
                    dve.wait_ge(S("scan_v"), 2 * st)
                for i, (a, w) in enumerate(((re, 0), (im, 1), (im, 0), (re, 1))):
                    dve.tensor_tensor(sc_a[:, i, :], a[:], r[:, w, :], ALU.mult).then_inc(S("scan_in"), 1)

            def scan(st):
                if st:
                    dve.wait_ge(S("scan_p"), 2 * st)
                    dve.wait_ge(S("scan_q"), 2 * st)
                for i in range(2):
                    dve.wait_ge(S("scan_v"), 2 * st + i + 1)
                    dve.tensor_tensor_scan(sc_v[:, 2 + i, :], s5[:, 3, st:st + 1].to_broadcast([P, T]), sc_v[:, i, :], 0.0,
                                           ALU.mult, ALU.add).then_inc(S("scanned"), 1)

            def scan_out(st):
                dve.wait_ge(S("scanned"), 2 * st + 2)
                if st >= 2:
                    dve.wait_ge(S("y_added"), st - 1)
                else:
                    dve.wait_ge(S("qk2_t"), 6)
                r = rot[:, st % ROT_SLOTS]
                dve.scalar_tensor_tensor(scan_product(st, 2), sc_v[:, 3, :], -1.0, r[:, 1, :], ALU.mult, ALU.mult).then_inc(S("scan_q"), 1)
                dve.tensor_tensor(scan_product(st, 3), sc_v[:, 3, :], r[:, 0, :], ALU.mult).then_inc(S("scan_q"), 1)

            def s5_y(c):
                dve.wait_ge(S("y_added"), 4 * c + 4)
                dve.scalar_tensor_tensor(u2[:, c, :], u2[:, c, :], col("ssm_d_2", c), B[4][:], ALU.mult, ALU.add).then_inc(S("s5_y"), 1)

            scan_in(0)
            s5_outputs()
            for st in range(NS):
                if st % 4 == 1 and st > 4:
                    s5_y(st // 4 - 1)
                if st + 1 < NS:
                    scan_in(st + 1)
                if st % 2:
                    sw_scale(st // 2)
                scan(st)
                scan_out(st)
                if st % 2 == 0:
                    sw_max(st // 2)
            def z_split(tiles):
                for t in tiles:
                    dve.wait_ge(S("z_hi_out"), t + 1)
                    dve.tensor_tensor(z_lo[:, t, :], u2[:, t, :], z_hi[:, t, :].bitcast(F32), ALU.subtract).then_inc(S("z_split"), 1)

            s5_y(3)
            z_split(range(4))
            norm("pa", yat, lambda k: col("out_norm_attn_2", k), hi=h_hi[:, 4:8], lo=h_lo[:, 4:8], width=T)
            split(PART["glu"][0] + 2)
            for t in range(4):
                dve.wait_ge(S("glu_gate"), t + 1)
                dve.tensor_tensor(u2[:, t, :], u2[:, t, :], gate[:, t, :], ALU.mult).then_inc(S("glu_out"), 1)
            norm("ps", u2, lambda k: col("out_norm_ssm_2", k), hi=h_hi[:, 0:4], lo=h_lo[:, 0:4], width=T)
            n, panels, _ = PART["w_out2"]
            for i in range(panels):
                for t in range(2 * i, 2 * i + 2):
                    dve.wait_ge(S("pe_done"), used(n + i, 2 * (t % 2) + 2))
                    dve.scalar_tensor_tensor(x[:, t, :], bank_of(t)[:], mod[:, 16 + t:17 + t], x[:, t, :],
                                             ALU.mult, ALU.add).then_inc(S("mix2_x"), 1)
                if i < panels - 1:
                    split(n + i + 2)

            norm("p2", x, lambda k: gain2[:, 1, k:k + 1], lambda k: mod[:, 24 + k:25 + k])
            base = BASE["ffn3"]
            with dve.Fori(0, GU_STEPS) as i:
                for half in range(2):
                    split(i * 2 + (base + 2 + half), base + half)
                    for t in range(2):
                        up, y = B[2 * half + t], tmp[:, 2 * half + t, :]
                        dve.wait_ge(S("ffn3_own"), i * 4 + (2 * half + t + 1))
                        for back in (1, 2):
                            dve.scalar_tensor_tensor(y[:, back:], up[:, :T - back], col_at(f"conv_w_2:{2 - back}", i * 2, KF * half + t),
                                                     y[:, back:], ALU.mult, ALU.add).then_inc(S("ffn3_conv"), 1)
                            if back == 1:
                                dve.wait_ge(S("ffn3_conv"), i * 8 + (4 * half + 2 * t + 9))
                for t in range(2):
                    dve.wait_ge(S("silu"), i * 2 + (HID["ffn3"] + t + 3))
                    dve.wait_ge(S("hid_split"), i * 2 + (HID["ffn3"] + t + 1))
                    dve.tensor_tensor(tmp[:, 4 + t, :], tmp[:, 2 + t, :], tmp[:, t, :], ALU.mult).then_inc(S("hid"), 1)
                for t in range(2):
                    hid_lo_of("ffn3", i, t, 4 + t)
            down("ffn3", lambda k: mod[:, 40 + k:41 + k])
            for b in range(TB):
                dve.wait_ge(S("out_t"), 2 * b + 1)
                dve.tensor_copy(x_in[:, b, 0:T], B[2 * b % 4][:]).then_inc(S("out_turned0"), 1)

        @block.tensor
        def _(pe):
            def products(out_ap, terms, first=True, last=True):
                for i, (stationary, moving) in enumerate(terms):
                    mm = pe.matmul(out_ap, stationary, moving, start=first and i == 0, stop=last and i == len(terms) - 1)
                return mm

            def feature_terms(n, k, c, at, hi, lo, wait=None, k0=0):
                wh, wl = panel(w_hi, n, k, c), panel(w_lo, n, k, c)
                for i in range(k):
                    if wait:
                        wait(i)
                    yield wh[:, i, at:at + P], hi[:, k0 + i, :]
                    yield wh[:, i, at:at + P], lo[:, k0 + i, :]
                    yield wl[:, i, at:at + P], hi[:, k0 + i, :]

            def token_terms(n, k, c, b, hi, lo, k0=0):
                wh, wl = panel(w_hi, n, k, c), panel(w_lo, n, k, c)
                own = slice(b * P, (b + 1) * P)
                for i in range(k):
                    yield hi[:, k0 + i, own], wh[:, i, :]
                    yield hi[:, k0 + i, own], wl[:, i, :]
                    yield lo[:, k0 + i, own], wh[:, i, :]

            def stream(out_ap, terms, total, first=True, last=True):
                for i, (stationary, moving) in enumerate(terms):
                    mm = pe.matmul(out_ap, stationary, moving, start=first and i == 0, stop=last and i == total - 1)
                return mm

            def norm(name, only=None):
                tiles, direct = NORM_PARTS[name]
                if direct < tiles:
                    pe.wait_ge(S("norm_added"), ADDED.index(name) + 1)
                    pe.matmul(B[7][:], ones[:], tmp[:, 0, :], start=True, stop=False).then_inc(S("norm_summed"), 1)
                for d in range(direct) if only is None else only:
                    pe.wait_ge(S("norm_sq"), NORM_SQ[name] + d + 1)
                    square = yat_sq[:, d, :] if name == "pa" else tmp[:, 2 + d % 2, :]
                    pe.matmul(B[7][:], ones[:], square, start=direct == tiles and d == 0,
                              stop=d == direct - 1).then_inc(S("norm_summed"), 1)

            def ready(name):
                return lambda k: pe.wait_ge(S("norm_split"), NORM[name] + k + 1)

            def ready_hi(name):
                return lambda k: pe.wait_ge(S("norm_hi"), NORM[name] + k + 1)

            def by_k(n, banks, hi, lo, wait=None, ks=range(KD), first=0, last=KD - 1, wait_hi=None):
                wh, wl = panel(w_hi, n, KD, PC), panel(w_lo, n, KD, PC)
                for k in ks:
                    if wait_hi:
                        wait_hi(k)
                    for part, terms in enumerate((((wh, hi), (wl, hi)), ((wh, lo),))):
                        if wait and part == (1 if wait_hi else 0):
                            wait(k)
                        for t, bank in enumerate(banks):
                            at = slice(t * P, (t + 1) * P)
                            for i, (w, h) in enumerate(terms):
                                mm = pe.matmul(bank[:], w[:, k, at], h[:, k, :], start=k == first and part == 0 and i == 0,
                                               stop=k == last and part == 1)
                            if k == last and part == 1:
                                mm.then_inc(S("pe_done"), 2)

            def gate_up(name, h_name, free):
                base = BASE[name]
                for start, stop, mods, _ in PHASES.get(name, ((0, GU_STEPS, False, False),)):
                    with pe.Fori(start, stop) as i:
                        for half in range(2):
                            pe.wait_ge(S("w_split"), i * 2 + (base + half + 1))
                            free(i, half)
                            by_k(base + half, [B[2 * half], B[2 * half + 1]], h_hi, h_lo, ready(h_name) if half == 0 else None,
                                 wait_hi=ready_hi(h_name) if half == 0 else None)
                        if mods:
                            pe.wait_ge(S("mod_step"), i * MOD_STEPS + ((MOD_AT[name] + 1) * MOD_STEPS + MOD_SLOTS))
                            for s4 in range(4):
                                for part in (mod_hi, mod_lo):
                                    mm = pe.matmul(B[6][:, bass.ds(i * 8 + 2 * s4, 2)], part[:, s4 * P:(s4 + 1) * P], ones_r[:],
                                                   start=part is mod_hi, stop=part is mod_lo)
                            mm.then_inc(S("mod_acc_free"), 1)

            def down(name):
                base = BASE[name] + 2 * GU_STEPS
                if name != "ffn3":
                    pe.wait_ge(S("silu"), HID[name] + KF + 2)
                with pe.Fori(0, 2) as j:
                    for c in range(8):
                        k0, kn = DOWN_K[c % 4]
                        pe.wait_ge(S("w_split"), j * 8 + (base + c + 1))
                        pe.wait_ge(S("hid_split"), HID[name] + k0 + kn + 2)
                        if c % 4 == 0:
                            pe.wait_ge(S(name + "_x"), j * 4 + (c // 4 * 2 + 2))
                        for t in range(2):
                            terms = feature_terms(base + c, kn, PC, t * P, hid_hi, hid_lo, None, k0)
                            mm = stream(down_bank(name, c // 4 * 2 + t)[:], terms, 3 * kn, c % 4 == 0, c % 4 == 3)
                            if c % 4 == 3:
                                mm.then_inc(S("pe_done"), 2)
                        if c % 4 < 3:
                            mm.then_inc(S("pe_done"), 4)

            pe.sem_inc(S("mod_acc_free"), 1)
            pe.wait_ge(S("pool_done"), 5)
            for k in range(KD + 3):
                if k < KD:
                    if k >= 4:
                        pe.wait_ge(S("x_turned"), k - 3)
                    pe.wait_ge(S(f"x_landed{k * P // PC}"), 16)
                    for b in range(TB):
                        mm = pe.transpose(B[2 + k % 4][:, b * P:(b + 1) * P], x_in[:, b, k * P:(k + 1) * P], ident[:])
                    mm.then_inc(S("x_t"), 1)
                if k >= 3:
                    norm("n1", (k - 3,))
            pe.wait_ge(S("rows_landed"), 16 * len(ROWS))
            for tile in range(3):
                n = ROW_COUNTS[tile]
                pe.transpose(B[0][:, tile * P:tile * P + n], rows[0:n, tile, :], ident[0:n, 0:n]).then_inc(S("rows_t"), 1)
            pe.wait_ge(S("rel_landed"), 32)
            pe.wait_ge(S("consts_made"), 1)
            pe.matmul(B[1][0:NQ, 0:BAND], rel[:], oh[:], start=True, stop=True).then_inc(S("band_t"), 1)
            pe.wait_ge(S("band_made"), 1)

            def silu_free(name):
                def free(i, half):
                    pe.wait_ge(S(("silu", "hid")[half]), i * 2 + (HID[name] + 2))
                return free

            gate_up("ffn1", "n1", silu_free("ffn1"))

            down("ffn1")

            norm("nm")

            def tokens(name, before, first=False):
                n = PART[name][0]
                for half in range(2):
                    pe.wait_ge(S("w_split"), n + half + 1)
                    wh, wl = panel(w_hi, n + half, 4, T), panel(w_lo, n + half, 4, T)
                    if first and half == 0:
                        for k in range(4):
                            for wait, terms in ((ready_hi, ((h_hi, wh), (h_hi, wl))), (ready, ((h_lo, wh),))):
                                wait("nm")(k)
                                for b in range(TB):
                                    own = slice(b * P, (b + 1) * P)
                                    for i, (h, w) in enumerate(terms):
                                        mm = pe.matmul(B[b][:], h[:, k, own], w[:, k, :], start=k == 0 and wait is ready_hi and i == 0,
                                                       stop=False)
                        mm.then_inc(S("pe_done"), 4)
                        continue
                    for b in range(TB):
                        if half == 0 and before:
                            pe.wait_ge(S(before[0]), before[1] - 3 + b)
                        if first and b == 0:
                            pe.wait_ge(S("norm_split"), NORM["nm"] + KD)
                        mm = stream(B[b][:], token_terms(n + half, 4, T, b, h_hi, h_lo, 4 * half), 12, half == 0, half == 1)
                        if half:
                            mm.then_inc(S("pe_done"), 1)
                    if half == 0:
                        mm.then_inc(S("pe_done"), 4)

            def features(name, evac, before, hi, lo, wait=None, start=0):
                n, panels, outs = PART[name]
                for t in range(start, outs):
                    i, per = divmod(t, outs // panels)
                    if per == 0:
                        pe.wait_ge(S("w_split"), n + i + 1)
                    if t >= 4:
                        pe.wait_ge(S(evac), t - 3)
                    elif before:
                        pe.wait_ge(S(before[0]), before[1] - 3 + t)
                    k, c = (4, T) if outs // panels == 4 else (KD, PC)
                    stream(bank_of(t)[:], feature_terms(n + i, k, c, per * P, hi, lo, wait if t == start else None), 3 * k)\
                        .then_inc(S("pe_done"), 4 // (outs // panels))

            def turn(j):
                pe.wait_ge(S("qk_done"), j + 1)
                for f in range(4):
                    if j:
                        pe.wait_ge(S("qk_t_out"), 4 * (j - 1) + f + 1)
                    elif f >= 2:
                        pe.wait_ge(S("ws_t_out"), f - 1)
                    if j == 1:
                        pe.wait_ge(S("ya_h"), 2 * f + 1)
                    for b in range(TB):
                        mm = pe.transpose(B[4 + f][:, b * P:(b + 1) * P], qk_raw[j % 2][:, b, f * P:(f + 1) * P], ident[:])
                    mm.then_inc(S("qk_t"), 1)

            tokens("v_gm", None, True)
            features("u_gm", "u_gm_out", ("v_gm_out", 4), h_hi, h_lo)
            tokens("qk0", ("u_gm_out", 4))
            pe.wait_ge(S("mod_made"), 1)
            pe.wait_ge(S("ws_masked"), 1)
            for f in range(2):
                for g in range(4):
                    mm = pe.transpose(B[6 + f][:, g * P:(g + 1) * P], ws_in[:, 4 * f + g, :], ident[:])
                mm.then_inc(S("ws_t"), 1)
            tokens("qk1", ("qk0_out", 4))
            turn(0)
            tokens("qk2", ("qk1_out", 4))
            pe.wait_ge(S("ws_t_out"), 2)
            pe.wait_ge(S("ln_out"), TB)
            pe.wait_ge(S("qk_t_out"), 4)
            for f in range(4):
                for half in range(2):
                    g = 2 * f + half
                    for c in range(TB):
                        mm = pe.matmul(B[4 + f][64 * half:64 * half + 64, c * P:(c + 1) * P],
                                       vg[:, c, g * 64:(g + 1) * 64], wsT[:, g, :], start=True, stop=True)
                mm.then_inc(S("f_done"), 1)
            tokens("v0", ("qk2_out", 4))
            turn(1)
            tokens("qk3", ("v0_out", 4))
            turn(2)
            tokens("v1", ("qk3_out", 4))
            turn(3)
            features("g_a", "g_a_out", ("v1_out", 4), h_hi, h_lo)
            features("a_proj", "a_proj_out", ("g_a_out", 8), ya_hi, ya_lo, lambda k: pe.wait_ge(S("ya_split"), k + 1))
            features("g_b", "g_b_out", ("a_proj_out", 8), h_hi, h_lo)

            def scores(u):
                h, i = UNITS[u]
                keys = (i + 1) * P
                if u == 0:
                    pe.wait_ge(S("mask_made"), 2)
                    pe.wait_ge(S("g_b_out"), 8)
                    pe.wait_ge(S("qk_t_out"), 16)
                if u >= 3:
                    pe.wait_ge(S("at_exp"), 2 * (u - 2))
                for m in range(2):
                    half = slice(64 * m, 64 * m + 64)
                    bank = B[2 * (u % 3) + m]
                    pe.matmul(bank[:, :keys], qT[half, h, i * P:(i + 1) * P], kT[half, h, :keys], start=True, stop=False)
                    pe.matmul(bank[:, i * P:keys], mask_parts[:, 0, :], mask_parts[:, 1, :], start=False, stop=True).then_inc(S("at_s"), 1)

            def weigh(u):
                h, i = UNITS[u]
                s = u % 2
                pe.wait_ge(S("at_a"), 2 * u + 2)
                if u:
                    pe.wait_ge(S("at_t_out"), u)
                for j in range(i + 1):
                    mm = pe.transpose(B[6][:, j * P:(j + 1) * P], tmp[:, 4 + s, j * P:(j + 1) * P], ident[:])
                mm.then_inc(S("at_t"), 1)

            def values(u):
                h, i = UNITS[u]
                s = u % 2
                pe.wait_ge(S("at_t_out"), u + 1)
                if u:
                    pe.wait_ge(S("at_o"), u)
                products(B[7][:, 0:P], [(aT[:, s, j * P:(j + 1) * P], vtok[:, j, h * P:(h + 1) * P])
                                            for j in range(i + 1)]).then_inc(S("at_pv"), 1)

            scores(0)
            scores(1)
            for u in range(len(UNITS)):
                if u + 2 < len(UNITS):
                    scores(u + 2)
                weigh(u)
                if u:
                    values(u - 1)
            values(len(UNITS) - 1)
            n = PART["b_proj"][0]
            lag = 3
            for h in range(HEADS + 2 + lag):
                if h < HEADS:
                    pe.wait_ge(S("o_scaled"), h + 1)
                    if h >= 4:
                        pe.wait_ge(S("yb_h"), h - 3)
                    for b in range(TB):
                        mm = pe.transpose(B[4 + h % 4][:, b * P:(b + 1) * P], o_tok[:, b, h * P:(h + 1) * P], ident[:])
                    mm.then_inc(S("yb_t"), 1)
                for i in range(2):
                    if 0 <= h - 2 - lag * i < HEADS:
                        pe.wait_ge(S("w_split"), n + i + 1)
                        by_k(n + i, [B[2 * i], B[2 * i + 1]], yb_hi, yb_lo, lambda k: pe.wait_ge(S("yb_split"), k + 1), (h - 2 - lag * i,))
            features("b_proj", "b_proj_out", None, yb_hi, yb_lo, start=4)
            features("w_out", "mixer_x", ("b_proj_out", 8), m_hi, m_lo, lambda k: pe.wait_ge(S("m_split"), k + 1))

            norm("n2")
            gate_up("ffn2", "n2", silu_free("ffn2"))
            down("ffn2")

            pe.wait_ge(S("mod_made"), 2)
            norm("p1")
            for i in range(2):
                pe.wait_ge(S("w_split"), PART["u2"][0] + i + 1)
                by_k(PART["u2"][0] + i, [B[2 * i], B[2 * i + 1]], h_hi, h_lo, ready("p1"), wait_hi=ready_hi("p1"))
            def s5_inputs(part):
                pe.wait_ge(S("bd_made"), 8 * (part + 1))
                for g in range(4 * part, 4 * part + 4):
                    for i in range(4):
                        mm = pe.transpose(B[4 + g % 4][:, i * P:(i + 1) * P], bd[:, 4 * (g % 4) + i, :], ident[:])
                    mm.then_inc(S("bb_t"), 1)

            tokens("q2", ("u2_out", 4))
            s5_inputs(0)
            n = PART["kv2"][0]
            pe.wait_ge(S("w_split"), n + 1)
            for b in range(TB):
                pe.wait_ge(S("q2_out"), b + 1)
                stream(B[b][:, 0:PC], token_terms(n, KD, PC, b, h_hi, h_lo), 3 * KD).then_inc(S("pe_done"), 1)
            pe.wait_ge(S("hank_landed"), 16)
            pe.wait_ge(S("flip_made"), 1)
            pe.wait_ge(S("bb_t_out"), 4)
            for g in range(4):
                pe.matmul(B[4 + g][:], causal[:], hank[:, 2 * g:2 * g + 2, :], start=True, stop=True).then_inc(S("bias_flipped"), 1)
            pe.wait_ge(S("bias_out"), 4)
            s5_inputs(1)
            def inputs(st):
                if st >= 2:
                    pe.wait_ge(S("scan_in"), 4 * (st - 1))
                for part in range(2):
                    pe.matmul(B[2 * (st % 2) + part][:], bbT[:, part, st, :], u2[:, st // 4, :], start=True, stop=True).then_inc(S("bu"), 1)

            pe.wait_ge(S("bb_t_out"), 8)
            pe.wait_ge(S("v2_out"), 8)
            pe.wait_ge(S("k2_out"), TB)
            inputs(0)
            inputs(1)
            pe.wait_ge(S("s5_landed"), 96)
            for part in range(2):
                for c in range(4):
                    mm = pe.transpose(B[4 + 3 * part][:, c * P:(c + 1) * P], c_in[:, part, c].rearrange("p w n -> p (w n)"), ident[:])
                mm.then_inc(S("c_t"), 1)
            for f in range(6):
                if f == 0:
                    pe.wait_ge(S("qk2_made"), 1)
                if f == 4:
                    pe.wait_ge(S("qk2_made"), 2)
                if f >= 2:
                    pe.wait_ge(S("qk2_t_out"), f - 1)
                for b in range(TB):
                    if f < 4:
                        mm = pe.transpose(B[5 + f % 2][:, b * P:(b + 1) * P], q2_raw[:, b, f * P:(f + 1) * P], ident[:])
                    else:
                        head = k2_raw[:, b, (f - 4) * QK:(f - 3) * QK]
                        for twice in range(2):
                            mm = pe.matmul(B[5 + f % 2][twice * QK:(twice + 1) * QK, b * P:(b + 1) * P], head, ident[:], start=True, stop=True)
                mm.then_inc(S("qk2_t"), 1)
            pe.wait_ge(S("qk2_t_out"), 6)

            def sw_scores(u):
                b, n = SW_UNITS[u]
                lo = P if b == 0 else 0
                if u:
                    pe.wait_ge(S("sw_t_out"), SW_BEFORE[u])
                for slot in range(2):
                    for odd in range(2):
                        half = slice(64 * odd, 64 * odd + 64)
                        mm = pe.matmul(B[5 + odd][:, slot * 2 * P + lo:(slot + 1) * 2 * P], q2T[half, 2 * n + slot, b * P:(b + 1) * P],
                                       k2T[half, n, (b - 1) * P + lo:(b + 1) * P], start=True, stop=True)
                        if slot:
                            mm.then_inc(S("sw_s"), 1)

            def sw_turn(u):
                pe.wait_ge(S("sw_p"), 4 * (u + 1))
                for kb in SW_BLOCKS[u]:
                    for h in range(4):
                        mm = pe.transpose(B[5 + kb][:, h * P:(h + 1) * P], prob[:, u % 2, h, kb * P:(kb + 1) * P], ident[:])
                    mm.then_inc(S("sw_t"), 1)

            def sw_values(u):
                b, n = SW_UNITS[u]
                pe.wait_ge(S("sw_t_out"), SW_BEFORE[u + 1])
                if u:
                    pe.wait_ge(S("sw_out"), 2 * u)
                products(B[7][:], [(v2[:, b - 1 + kb, n].rearrange("p w d -> p (w d)"), pT[:, u % 2, kb, :]) for kb in SW_BLOCKS[u]])\
                    .then_inc(S("sw_pv"), 1)

            SCAN_TERMS = (0, 2, 1, 3)

            def outputs(st):
                if st >= 4 and st % 4 == 0:
                    pe.wait_ge(S("s5_y"), st // 4)
                if st == 0:
                    pe.wait_ge(S("c_out"), 16)
                pe.wait_ge(S("scan_p"), 2 * st + 2)
                pe.wait_ge(S("scan_q"), 2 * st + 2)
                products(B[4][:], [(cT[:, i % 2, st, :], scan_product(st, i)) for i in SCAN_TERMS],
                         st % 4 == 0, st % 4 == 3).then_inc(S("y_added"), 1)

            for st in range(NS):
                u = st // 2
                if st + 2 < NS:
                    inputs(st + 2)
                if st % 2 == 0:
                    if u:
                        sw_values(u - 1)
                    sw_scores(u)
                if st:
                    outputs(st - 1)
                if st % 2:
                    sw_turn(u)
            sw_values(len(SW_UNITS) - 1)
            outputs(NS - 1)
            pe.wait_ge(S("sw_out"), 2 * len(SW_UNITS))
            norm("pa")
            n = PART["glu"][0]
            pe.wait_ge(S("w_split"), n + 1)
            wh, wl = panel(w_hi, n, 4, T), panel(w_lo, n, 4, T)
            for k in range(4):
                pe.wait_ge(S("z_split"), k + 1)
                for t in range(4):
                    own = slice(t * P, (t + 1) * P)
                    for i, (w, h) in enumerate(((wh, z_hi), (wh, z_lo), (wl, z_hi))):
                        mm = pe.matmul(glu_bank(t)[:], w[:, k, own], h[:, k, :], start=k == 0 and i == 0, stop=k == 3 and i == 2)
                    if k == 3:
                        mm.then_inc(S("pe_done"), 1)
            n = PART["w_out2"][0]
            halves = ((4, 5, 6, 7), (0, 1, 2, 3))
            for part, ks in enumerate(halves):
                for i in range(2):
                    pe.wait_ge(S("w_split"), n + i + 1)
                    if part == 0 and i == 1:
                        pe.wait_ge(S("glu_gate"), 2)
                    by_k(n + i, [B[2 * i], B[2 * i + 1]], h_hi, h_lo,
                         lambda k: pe.wait_ge(S("norm_split"), NORM["pa"] + k - 3 if k >= 4 else NORM["ps"] + k + 1), ks, 4, 3)
                    if part == 0 and i == 0:
                        norm("ps")
            features("w_out2", "mix2_x", None, h_hi, h_lo, start=4)

            norm("p2")
            gate_up("ffn3", "p2", lambda i, half: pe.wait_ge(S("ffn3_conv"), i * 8 + (4 * half + 4)))
            down("ffn3")
            for b in range(TB):
                for half in range(2):
                    wait_x(pe, "ffn3", 4 * half + 3)
                    if b >= 2:
                        pe.wait_ge(S(f"out_turned{half}"), b - 1)
                    for k in range(4):
                        mm = pe.transpose(B[(2 * b + half) % 4][:, k * P:(k + 1) * P], x[:, 4 * half + k, b * P:(b + 1) * P], ident[:])
                    mm.then_inc(S("out_t"), 1)


NAMES = (
    "x", "positions", "ffn1_norm", "ffn1_w_gate", "ffn1_w_up", "ffn1_w_down", "mix_norm", "w_in", "a_ln_gain", "a_ln_bias",
    "a_w_s", "a_b_s", "a_w_proj", "b_q_norm", "b_k_norm", "b_lambda_q1", "b_lambda_k1", "b_lambda_q2", "b_lambda_k2", "b_subln",
    "b_w_proj", "w_out", "ffn2_norm", "ffn2_w_gate", "ffn2_w_up", "ffn2_w_down", "c_2", "w_mod_2", "b_mod_2", "norm1_w_2",
    "w_in_2", "lam_re_2", "lam_im_2", "log_dt_2", "ssm_b_re_2", "ssm_b_im_2", "ssm_c_re_2", "ssm_c_im_2", "ssm_d_2", "w_glu_2",
    "b_glu_2", "q_norm_w_2", "k_norm_w_2", "rel_bias_2", "sinks_2", "out_norm_ssm_2", "out_norm_attn_2", "w_out_2", "norm2_w_2",
    "w_up_2", "conv_w_2", "conv_b_2", "w_down_2",
)


def distance_buckets():
    dist = 2 * P - 1 - np.arange(BAND)
    n = np.maximum(dist, 0)
    log_part = np.log(np.maximum(n, 1) / 16) / math.log(128 / 16)
    bucket = np.where(n < 16, n, np.minimum(16 + (log_part * 16).astype(np.int32), 31))
    seen = (dist >= 0) & (dist < WIN)
    table = np.zeros((33, BAND), np.float32)
    table[bucket[seen], np.flatnonzero(seen)] = 1.0
    table[32, ~seen] = NEG
    return table


def kernel(**inputs):
    from concourse import bacc
    from concourse.bass_utils import run_bass_kernel_spmd

    nc = bacc.Bacc("TRN2", target_bir_lowering=False, num_devices=1)
    arrays, aps = {}, {}
    for name in NAMES:
        a = np.ascontiguousarray(inputs[name])
        arrays[f"in_{name}"] = a
        aps[name] = nc.dram_tensor(f"in_{name}", a.shape, mybir.dt.from_np(a.dtype), kind="ExternalInput").ap()
    table = distance_buckets()
    arrays["rel_onehot"] = table
    onehot = nc.dram_tensor("rel_onehot", table.shape, F32, kind="ExternalInput").ap()
    out = nc.dram_tensor("out_x", (1, T, D), F32, kind="ExternalOutput").ap()
    build(nc, aps, onehot, out)
    r = run_bass_kernel_spmd(nc, [arrays], core_ids=[0])
    return r.results[0]["out_x"]
```
